# Optimizing a Trainium2 kernel written in Bass

```python
import math
import jax, jax.numpy as jnp
from jax import lax
import numpy as np
import jax
import jax.numpy as jnp

D_MODEL = 1024
BATCH = 1
SEQ = 512
DEPTH = 2

CHUNK = 64
LEFT_CHUNKS = 8
BAND = LEFT_CHUNKS + 1
ATTN_HEAD_DIM = 64
ATTN_HEADS = D_MODEL // ATTN_HEAD_DIM
MAX_REL = 256
DN_HEAD_DIM = 128
DN_HEADS = D_MODEL // DN_HEAD_DIM
DN_WIDTH = DN_HEADS * DN_HEAD_DIM
CONV_K = 4
D_FF = 4 * D_MODEL
EPS = 1e-6
N_MIXERS = 2
N_ATTN_LAYERS = (DEPTH + 1) // 2
N_DN_LAYERS = DEPTH // 2


def rmsnorm(x, w):
    xf = x.astype(jnp.float32)
    y = xf * lax.rsqrt(jnp.mean(xf * xf, axis=-1, keepdims=True) + EPS)
    return (y * w.astype(jnp.float32)).astype(x.dtype)

def l2norm(x):
    xf = x.astype(jnp.float32)
    return xf * lax.rsqrt(jnp.sum(xf * xf, axis=-1, keepdims=True) + EPS)

def chunked_rel_attention(h, w_qkv, rel_bias, w_o):
    B, S, _ = h.shape
    nc = S // CHUNK
    qkv = h @ w_qkv
    q, k, v = jnp.split(qkv, 3, axis=-1)
    q = q.reshape(B, S, ATTN_HEADS, ATTN_HEAD_DIM)
    k = k.reshape(B, S, ATTN_HEADS, ATTN_HEAD_DIM)
    v = v.reshape(B, S, ATTN_HEADS, ATTN_HEAD_DIM)
    pad = ((0, 0), (LEFT_CHUNKS * CHUNK, 0), (0, 0), (0, 0))
    kpad = jnp.pad(k, pad)
    vpad = jnp.pad(v, pad)
    q_off = jnp.arange(CHUNK)[:, None]
    k_off = jnp.arange(BAND * CHUNK)[None, :] - LEFT_CHUNKS * CHUNK
    dist = jnp.clip(q_off - k_off, -MAX_REL, MAX_REL) + MAX_REL
    bias = rel_bias[:, dist].astype(jnp.float32)
    scale = ATTN_HEAD_DIM ** -0.5

    def one_chunk(c):
        start = c * CHUNK
        q_c = lax.dynamic_slice_in_dim(q, start, CHUNK, axis=1)
        k_b = lax.dynamic_slice_in_dim(kpad, start, BAND * CHUNK, axis=1)
        v_b = lax.dynamic_slice_in_dim(vpad, start, BAND * CHUNK, axis=1)
        s = jnp.einsum('bqhd,bkhd->bhqk', q_c, k_b,
                       preferred_element_type=jnp.float32) * scale + bias[None]
        k_abs = start - LEFT_CHUNKS * CHUNK + jnp.arange(BAND * CHUNK)
        s = jnp.where((k_abs >= 0)[None, None, None, :], s, -jnp.inf)
        p = jax.nn.softmax(s, axis=-1).astype(v.dtype)
        return jnp.einsum('bhqk,bkhd->bqhd', p, v_b)

    o = lax.map(one_chunk, jnp.arange(nc))
    o = jnp.moveaxis(o, 0, 1).reshape(B, S, D_MODEL)
    return o @ w_o

def causal_conv(x, w):
    S = x.shape[1]
    xp = jnp.pad(x, ((0, 0), (CONV_K - 1, 0), (0, 0)))
    y = xp[:, 0:S] * w[0]
    for j in range(1, CONV_K):
        y = y + xp[:, j:j + S] * w[j]
    return y

def chunk_gated_delta_rule(q, k, v, g, beta):
    B, S, H, dk = q.shape
    dv = v.shape[-1]
    nc = S // CHUNK

    def to_chunks(t):
        t = t.astype(jnp.float32).reshape((B, nc, CHUNK, H) + t.shape[3:])
        return jnp.moveaxis(t, 3, 1)

    q, k, v, g, beta = map(to_chunks, (q, k, v, g, beta))
    gc = jnp.cumsum(g, axis=-1)
    idx = jnp.arange(CHUNK)
    incl = idx[:, None] >= idx[None, :]
    strict = idx[:, None] > idx[None, :]
    decay = jnp.exp(jnp.where(incl, gc[..., :, None] - gc[..., None, :], -jnp.inf))
    kb = k * beta[..., None]
    vb = v * beta[..., None]
    L = jnp.where(strict, jnp.einsum('bhnid,bhnjd->bhnij', kb, k) * decay, 0.0)
    M = L + jnp.eye(CHUNK, dtype=jnp.float32)
    rhs = jnp.concatenate([vb, kb * jnp.exp(gc)[..., None]], axis=-1)
    sol = lax.linalg.triangular_solve(M, rhs, left_side=True, lower=True,
                                      unit_diagonal=True)
    u, w = sol[..., :dv], sol[..., dv:]
    qk = jnp.einsum('bhnid,bhnjd->bhnij', q, k) * decay
    q_dec = q * jnp.exp(gc)[..., None]
    k_dec = k * jnp.exp(gc[..., -1:] - gc)[..., None]
    g_last = jnp.exp(gc[..., -1])
    xs = tuple(jnp.moveaxis(t, 2, 0) for t in (u, w, qk, q_dec, k_dec, g_last))

    def step(state, inp):
        u_c, w_c, qk_c, qd_c, kd_c, gl_c = inp
        v_new = u_c - jnp.einsum('bhck,bhkv->bhcv', w_c, state)
        o_c = jnp.einsum('bhck,bhkv->bhcv', qd_c, state) + jnp.einsum('bhij,bhjv->bhiv', qk_c, v_new)
        state = state * gl_c[..., None, None] + jnp.einsum('bhck,bhcv->bhkv', kd_c, v_new)
        return state, o_c

    s0 = jnp.zeros((B, H, dk, dv), jnp.float32)
    _, o = lax.scan(step, s0, xs)
    o = jnp.transpose(o, (1, 0, 3, 2, 4))
    return o.reshape(B, S, H, dv)

def gated_deltanet(h, w_in, conv_w, a_log, dt_bias, head_norm, w_o):
    B, S, _ = h.shape
    proj = h @ w_in
    qkv = proj[..., :3 * DN_WIDTH]
    z = proj[..., 3 * DN_WIDTH:4 * DN_WIDTH]
    a = proj[..., 4 * DN_WIDTH:4 * DN_WIDTH + DN_HEADS]
    b = proj[..., 4 * DN_WIDTH + DN_HEADS:]
    qkv = jax.nn.silu(causal_conv(qkv, conv_w))
    q, k, v = jnp.split(qkv, 3, axis=-1)
    q = l2norm(q.reshape(B, S, DN_HEADS, DN_HEAD_DIM)) * (DN_HEAD_DIM ** -0.5)
    k = l2norm(k.reshape(B, S, DN_HEADS, DN_HEAD_DIM))
    v = v.reshape(B, S, DN_HEADS, DN_HEAD_DIM)
    beta = jax.nn.sigmoid(b.astype(jnp.float32))
    g = -jnp.exp(a_log.astype(jnp.float32)) * jax.nn.softplus(
        a.astype(jnp.float32) + dt_bias.astype(jnp.float32))
    o = chunk_gated_delta_rule(q, k, v, g, beta)
    o = rmsnorm(o, head_norm) * jax.nn.silu(
        z.astype(jnp.float32).reshape(B, S, DN_HEADS, DN_HEAD_DIM))
    return o.reshape(B, S, DN_WIDTH).astype(h.dtype) @ w_o

def squared_relu_mlp(h, w_up, w_down):
    return jnp.square(jax.nn.relu(h @ w_up)) @ w_down

def first_inputs(seed: int = 0) -> dict:
    key = jax.random.key(seed)
    ks = jax.random.split(key, 18)
    f32 = jnp.float32

    def nrm(k, shape, fan_in, gain=1.0):
        return jax.random.normal(k, shape, f32) * (gain * fan_in ** -0.5)

    def gains(k, shape):
        return 1.0 + 0.02 * jax.random.normal(k, shape, f32)

    NA, NB = N_ATTN_LAYERS, N_DN_LAYERS
    x = jax.random.normal(ks[0], (BATCH, SEQ, D_MODEL), f32)
    attn_norm = gains(ks[1], (NA, D_MODEL))
    attn_w_qkv = nrm(ks[2], (NA, D_MODEL, 3 * D_MODEL), D_MODEL)
    attn_rel_bias = 0.1 * jax.random.normal(ks[3], (NA, ATTN_HEADS, 2 * MAX_REL + 1), f32)
    attn_w_o = nrm(ks[4], (NA, D_MODEL, D_MODEL), D_MODEL)
    dn_norm = gains(ks[5], (NB, D_MODEL))
    dn_w_in = nrm(ks[6], (NB, D_MODEL, 4 * DN_WIDTH + 2 * DN_HEADS), D_MODEL)
    dn_conv_w = nrm(ks[7], (NB, CONV_K, 3 * DN_WIDTH), CONV_K)
    dn_a_log = jnp.log(jax.random.uniform(ks[8], (NB, DN_HEADS), f32, 1.0, 16.0))
    dt = jnp.exp(jax.random.uniform(ks[9], (NB, DN_HEADS), f32,
                                    math.log(1e-3), math.log(1e-1)))
    dn_dt_bias = dt + jnp.log(-jnp.expm1(-dt))
    dn_head_norm = gains(ks[10], (NB, DN_HEAD_DIM))
    dn_w_o = nrm(ks[11], (NB, DN_WIDTH, D_MODEL), DN_WIDTH)
    mlp_norm = gains(ks[12], (DEPTH, D_MODEL))
    mlp_w_up = nrm(ks[13], (DEPTH, D_MODEL, D_FF), D_MODEL)
    mlp_w_down = nrm(ks[14], (DEPTH, D_FF, D_MODEL), D_FF, gain=0.5)
    final_norm = gains(ks[15], (D_MODEL,))
    return {"x": x, "attn_norm": attn_norm, "attn_w_qkv": attn_w_qkv,
            "attn_rel_bias": attn_rel_bias, "attn_w_o": attn_w_o,
            "dn_norm": dn_norm, "dn_w_in": dn_w_in, "dn_conv_w": dn_conv_w,
            "dn_a_log": dn_a_log, "dn_dt_bias": dn_dt_bias, "dn_head_norm": dn_head_norm,
            "dn_w_o": dn_w_o, "mlp_norm": mlp_norm, "mlp_w_up": mlp_w_up,
            "mlp_w_down": mlp_w_down, "final_norm": final_norm}

def first_block(x, attn_norm, attn_w_qkv, attn_rel_bias, attn_w_o,
              dn_norm, dn_w_in, dn_conv_w, dn_a_log, dn_dt_bias, dn_head_norm, dn_w_o,
              mlp_norm, mlp_w_up, mlp_w_down, final_norm):
    for i in range(DEPTH):
        j = i // N_MIXERS
        if i % N_MIXERS == 0:
            x = x + chunked_rel_attention(rmsnorm(x, attn_norm[j]), attn_w_qkv[j],
                                          attn_rel_bias[j], attn_w_o[j])
        else:
            x = x + gated_deltanet(rmsnorm(x, dn_norm[j]), dn_w_in[j], dn_conv_w[j],
                                   dn_a_log[j], dn_dt_bias[j], dn_head_norm[j], dn_w_o[j])
        x = x + squared_relu_mlp(rmsnorm(x, mlp_norm[i]), mlp_w_up[i], mlp_w_down[i])
    return rmsnorm(x, final_norm)


DEPTH_2 = 1

HEAD_DIM = 64
Q_BLOCK = 128
NORM_EPS = 1e-6

REL_BUCKETS = 32
REL_MAX_DIST = 2048

A_HEADS = 8
A_IDX_HEADS = 4
A_IDX_DIM = 64
A_TOPK_MAX = 256

B_HEADS = 8
B_KV_HEADS = 2
B_GROUP = B_HEADS // B_KV_HEADS
B_CMP_LEN = 32
B_CMP_STRIDE = 16
B_SEL_LEN = 64
B_SEL_TOPK_MAX = 16
B_WINDOW = 512
B_Q_BLOCK = 64

C_GROUPS = ((128, 1), (512, 4), (2048, 16))
C_HEADS_PER_GROUP = 4
C_HEADS = C_HEADS_PER_GROUP * len(C_GROUPS)
C_PAD = 2048

REL_HEADS = A_HEADS + B_HEADS + C_HEADS

D_FF_2 = ((8 * D_MODEL + 3 * 256 - 1) // (3 * 256)) * 256

IN_SIZES = (
    A_HEADS * HEAD_DIM,
    HEAD_DIM,
    HEAD_DIM,
    A_IDX_HEADS * A_IDX_DIM,
    A_IDX_DIM,
    A_IDX_HEADS,
    B_HEADS * HEAD_DIM,
    6 * B_KV_HEADS * HEAD_DIM,
    3 * B_HEADS,
    3 * C_HEADS * HEAD_DIM,
    3 * D_MODEL,
)
IN_TOTAL = sum(IN_SIZES)


def _rms(x, g):
    xf = x.astype(jnp.float32)
    y = xf * lax.rsqrt(jnp.mean(xf * xf, axis=-1, keepdims=True) + NORM_EPS)
    return (y * g.astype(jnp.float32)).astype(x.dtype)

def _split_last(y, sizes):
    out, off = [], 0
    for n in sizes:
        out.append(y[..., off:off + n])
        off += n
    return out

def _rel_bucket(dist):
    n = jnp.maximum(dist, 0)
    exact = REL_BUCKETS // 2
    nf = jnp.maximum(n, 1).astype(jnp.float32)
    large = exact + (jnp.log(nf / exact) / math.log(REL_MAX_DIST / exact)
                     * (REL_BUCKETS - exact)).astype(jnp.int32)
    return jnp.where(n < exact, n, jnp.minimum(large, REL_BUCKETS - 1))

def _masked_softmax(logits, mask):
    s = jnp.where(mask, logits, -jnp.inf)
    m = jnp.max(s, axis=-1, keepdims=True)
    m = jnp.where(jnp.isfinite(m), m, 0.0)
    e = jnp.exp(s - m)
    den = jnp.sum(e, axis=-1, keepdims=True)
    p = e / jnp.maximum(den, 1e-30)
    lse = (m + jnp.log(den))[..., 0]
    return p, lse

def _sweep(fn, seq, block):
    out = lax.map(fn, jnp.arange(seq // block))
    out = jnp.moveaxis(out, 0, 1)
    return out.reshape((out.shape[0], seq) + out.shape[3:])

_gather_rows = jax.vmap(lambda a, i: a[i])

def _dsa_attention(q, k, v, iq, ik, iw, rel_tab):
    seq = q.shape[1]
    topk = min(A_TOPK_MAX, seq // 4)
    scale = HEAD_DIM ** -0.5
    keys = jnp.arange(seq)

    def block(i):
        q0 = i * Q_BLOCK
        t = q0 + jnp.arange(Q_BLOCK)
        qb = lax.dynamic_slice_in_dim(q, q0, Q_BLOCK, axis=1)
        iqb = lax.dynamic_slice_in_dim(iq, q0, Q_BLOCK, axis=1)
        iwb = lax.dynamic_slice_in_dim(iw, q0, Q_BLOCK, axis=1).astype(jnp.float32)
        rel = jax.nn.relu(jnp.einsum("bqhd,bsd->bqhs", iqb, ik, preferred_element_type=jnp.float32))
        score = jnp.einsum("bqhs,bqh->bqs", rel, iwb)
        score = jnp.where(keys[None, None, :] <= t[None, :, None], score, -jnp.inf)
        _, idx = lax.top_k(score, topk)
        kg = _gather_rows(k, idx)
        vg = _gather_rows(v, idx)
        dist = t[None, :, None] - idx
        bias = jnp.moveaxis(rel_tab[_rel_bucket(dist)], -1, 1)
        logits = jnp.einsum("bqhd,bqkd->bhqk", qb, kg, preferred_element_type=jnp.float32) * scale + bias
        p, _ = _masked_softmax(logits, (dist >= 0)[:, None])
        return jnp.einsum("bhqk,bqkd->bqhd", p.astype(vg.dtype), vg).astype(q.dtype)

    o = _sweep(block, seq, Q_BLOCK)
    return o.reshape(o.shape[:2] + (A_HEADS * HEAD_DIM,))

def _nsa_attention(q, kc, vc, ks, vs, kw, vw, gates, cmp_pos, cmp_w, k_gain, rel_tab):
    bsz, seq = q.shape[:2]
    G, Hg, Dh = B_KV_HEADS, B_GROUP, HEAD_DIM
    scale = Dh ** -0.5
    n_cmp = (seq - B_CMP_LEN) // B_CMP_STRIDE + 1
    n_sel = seq // B_SEL_LEN
    n_top = min(B_SEL_TOPK_MAX, n_sel)

    cidx = jnp.arange(n_cmp)[:, None] * B_CMP_STRIDE + jnp.arange(B_CMP_LEN)[None, :]

    def compress(src, pos, w):
        blk = src[:, cidx] + pos[:, None, :]
        return jnp.einsum("bnlgd,lde->bnge", blk, w)

    kcmp = _rms(compress(kc, cmp_pos[0], cmp_w[0]), k_gain)
    vcmp = compress(vc, cmp_pos[1], cmp_w[1])
    cstart = cidx[:, 0]
    cend = cidx[:, -1]
    sstart = jnp.arange(n_sel) * B_SEL_LEN
    overlap = ((cstart[:, None] < sstart[None, :] + B_SEL_LEN)
               & (cstart[:, None] + B_CMP_LEN > sstart[None, :])).astype(jnp.float32)
    ksb = jnp.moveaxis(ks.reshape(bsz, n_sel, B_SEL_LEN, G, Dh), 3, 1)
    vsb = jnp.moveaxis(vs.reshape(bsz, n_sel, B_SEL_LEN, G, Dh), 3, 1)
    wpad = ((0, 0), (B_WINDOW, 0), (0, 0), (0, 0))
    kw_pad = jnp.pad(kw, wpad)
    vw_pad = jnp.pad(vw, wpad)
    tab = rel_tab.reshape(REL_BUCKETS, G, Hg)
    sel_blocks = jnp.arange(n_sel)
    gather_blocks = jax.vmap(jax.vmap(lambda a, i: a[i]))
    bias_per_group = jax.vmap(lambda tb, bk: tb[bk], in_axes=(1, 1), out_axes=1)

    def block(i):
        q0 = i * B_Q_BLOCK
        t = q0 + jnp.arange(B_Q_BLOCK)
        qb = lax.dynamic_slice_in_dim(q, q0, B_Q_BLOCK, axis=1).reshape(bsz, B_Q_BLOCK, G, Hg, Dh)
        gb = lax.dynamic_slice_in_dim(gates, q0, B_Q_BLOCK, axis=1).reshape(bsz, B_Q_BLOCK, G, Hg, 3)
        lc = jnp.einsum("bqghd,bngd->bghqn", qb, kcmp, preferred_element_type=jnp.float32) * scale
        pc, _ = _masked_softmax(lc, cend[None, :] <= t[:, None])
        oc = jnp.einsum("bghqn,bngd->bqghd", pc.astype(vcmp.dtype), vcmp)
        imp = jnp.einsum("bghqn,nm->bgqm", pc, overlap)
        jt = (t // B_SEL_LEN)[:, None]
        forced = (sel_blocks[None] == 0) | (sel_blocks[None] == jt) | (sel_blocks[None] == jt - 1)
        imp = jnp.where(forced, jnp.inf, jnp.where(sel_blocks[None] <= jt, imp, -jnp.inf))
        _, sel = lax.top_k(imp, n_top)
        kg = gather_blocks(ksb, sel).reshape(bsz, G, B_Q_BLOCK, n_top * B_SEL_LEN, Dh)
        vg = gather_blocks(vsb, sel).reshape(bsz, G, B_Q_BLOCK, n_top * B_SEL_LEN, Dh)
        pos = (sel[..., None] * B_SEL_LEN + jnp.arange(B_SEL_LEN)).reshape(bsz, G, B_Q_BLOCK, -1)
        dist = t[None, None, :, None] - pos
        bias_s = jnp.moveaxis(bias_per_group(tab, _rel_bucket(dist)), -1, 2)
        ls = jnp.einsum("bqghd,bgqkd->bghqk", qb, kg, preferred_element_type=jnp.float32) * scale + bias_s
        ps, _ = _masked_softmax(ls, (dist >= 0)[:, :, None])
        osel = jnp.einsum("bghqk,bgqkd->bqghd", ps.astype(vg.dtype), vg)
        kwb = lax.dynamic_slice_in_dim(kw_pad, q0, B_Q_BLOCK + B_WINDOW, axis=1)
        vwb = lax.dynamic_slice_in_dim(vw_pad, q0, B_Q_BLOCK + B_WINDOW, axis=1)
        kpos = q0 - B_WINDOW + jnp.arange(B_Q_BLOCK + B_WINDOW)
        dw = t[:, None] - kpos[None, :]
        mw = (dw >= 0) & (dw < B_WINDOW) & (kpos[None, :] >= 0)
        bias_w = jnp.transpose(tab[_rel_bucket(dw)], (2, 3, 0, 1))
        lw = jnp.einsum("bqghd,bkgd->bghqk", qb, kwb, preferred_element_type=jnp.float32) * scale + bias_w
        pw, _ = _masked_softmax(lw, mw)
        ow = jnp.einsum("bghqk,bkgd->bqghd", pw.astype(vwb.dtype), vwb)
        o = gb[..., 0:1] * oc + gb[..., 1:2] * osel + gb[..., 2:3] * ow
        return o.reshape(bsz, B_Q_BLOCK, G * Hg * Dh).astype(q.dtype)

    return _sweep(block, seq, B_Q_BLOCK)

def _dilated_attention(q, k, v, rel_tab):
    bsz, seq = q.shape[:2]
    scale = HEAD_DIM ** -0.5
    pad = ((0, 0), (C_PAD, 0), (0, 0), (0, 0))
    hsl = [slice(g * C_HEADS_PER_GROUP, (g + 1) * C_HEADS_PER_GROUP) for g in range(len(C_GROUPS))]
    kps = [jnp.pad(k[:, :, hs], pad) for hs in hsl]
    vps = [jnp.pad(v[:, :, hs], pad) for hs in hsl]

    def block(i):
        q0 = i * Q_BLOCK
        t = q0 + jnp.arange(Q_BLOCK)
        qb = lax.dynamic_slice_in_dim(q, q0, Q_BLOCK, axis=1)
        outs, lses = [], []
        for gi, (win, dil) in enumerate(C_GROUPS):
            steps = jnp.arange(win // dil + 1) * dil
            pos = t[:, None] - steps[None, :]
            kg = jnp.take(kps[gi], pos + C_PAD, axis=1)
            vg = jnp.take(vps[gi], pos + C_PAD, axis=1)
            bias = rel_tab[_rel_bucket(steps), hsl[gi]].T[None, :, None, :]
            logits = jnp.einsum("bqhd,bqkhd->bhqk", qb[:, :, hsl[gi]], kg,
                                preferred_element_type=jnp.float32) * scale + bias
            p, lse = _masked_softmax(logits, (pos >= 0)[None, None])
            outs.append(jnp.einsum("bhqk,bqkhd->bqhd", p.astype(vg.dtype), vg))
            lses.append(lse)
        w = jax.nn.softmax(jnp.stack(lses), axis=0)
        w = jnp.transpose(w, (0, 1, 3, 2))[..., None]
        o = w[0] * outs[0]
        for gi in range(1, len(C_GROUPS)):
            o = o + w[gi] * outs[gi]
        return o.reshape(bsz, Q_BLOCK, C_HEADS_PER_GROUP * HEAD_DIM).astype(q.dtype)

    return _sweep(block, seq, Q_BLOCK)

def second_inputs(seed: int = 0) -> dict:
    key = jax.random.key(seed)
    ks = jax.random.split(key, 14)

    def nrm(k, shape, scale):
        return jax.random.normal(k, shape, jnp.float32) * scale

    return {
        "x": nrm(ks[0], (BATCH, SEQ, D_MODEL), 1.0),
        "norm1_g": 1.0 + nrm(ks[1], (DEPTH_2, D_MODEL), 0.1),
        "norm2_g": 1.0 + nrm(ks[2], (DEPTH_2, D_MODEL), 0.1),
        "w_in": nrm(ks[3], (DEPTH_2, D_MODEL, IN_TOTAL), D_MODEL ** -0.5),
        "qk_norm_g": 1.0 + nrm(ks[4], (DEPTH_2, 6, HEAD_DIM), 0.1),
        "nsa_cmp_pos": nrm(ks[5], (DEPTH_2, 2, B_CMP_LEN, HEAD_DIM), 0.5),
        "nsa_cmp_w": nrm(ks[6], (DEPTH_2, 2, B_CMP_LEN, HEAD_DIM, HEAD_DIM), (B_CMP_LEN * HEAD_DIM) ** -0.5),
        "w_branch_a": nrm(ks[7], (DEPTH_2, A_HEADS * HEAD_DIM, D_MODEL), (A_HEADS * HEAD_DIM) ** -0.5),
        "w_branch_b": nrm(ks[8], (DEPTH_2, B_HEADS * HEAD_DIM, D_MODEL), (B_HEADS * HEAD_DIM) ** -0.5),
        "w_branch_c": nrm(ks[9], (DEPTH_2, C_HEADS_PER_GROUP * HEAD_DIM, D_MODEL), (C_HEADS_PER_GROUP * HEAD_DIM) ** -0.5),
        "w_out": nrm(ks[10], (DEPTH_2, D_MODEL, D_MODEL), D_MODEL ** -0.5),
        "w_ffn_in": nrm(ks[11], (DEPTH_2, D_MODEL, 2 * D_FF_2), D_MODEL ** -0.5),
        "w_ffn_out": nrm(ks[12], (DEPTH_2, D_FF_2, D_MODEL), D_FF_2 ** -0.5),
        "rel_bias": nrm(ks[13], (REL_BUCKETS, REL_HEADS), 0.5),
    }

def second_block(x, norm1_g, norm2_g, w_in, qk_norm_g, nsa_cmp_pos, nsa_cmp_w, w_branch_a, w_branch_b,
              w_branch_c, w_out, w_ffn_in, w_ffn_out, rel_bias):
    bsz, seq, _ = x.shape
    rel_a = rel_bias[:, :A_HEADS]
    rel_b = rel_bias[:, A_HEADS:A_HEADS + B_HEADS]
    rel_c = rel_bias[:, A_HEADS + B_HEADS:]
    for layer in range(DEPTH_2):
        h = _rms(x, norm1_g[layer])
        (a_q, a_k, a_v, i_q, i_k, i_w, b_q, b_kv, b_g, c_qkv, mix_g) = _split_last(h @ w_in[layer], IN_SIZES)
        qk = qk_norm_g[layer]
        a_q = _rms(a_q.reshape(bsz, seq, A_HEADS, HEAD_DIM), qk[0])
        a_k = _rms(a_k, qk[1])
        y_a = _dsa_attention(a_q, a_k, a_v, i_q.reshape(bsz, seq, A_IDX_HEADS, A_IDX_DIM), i_k, i_w,
                             rel_a) @ w_branch_a[layer]
        b_q = _rms(b_q.reshape(bsz, seq, B_HEADS, HEAD_DIM), qk[2])
        b_kv = b_kv.reshape(bsz, seq, 6, B_KV_HEADS, HEAD_DIM)
        b_gates = jax.nn.sigmoid(b_g).reshape(bsz, seq, B_HEADS, 3)
        y_b = _nsa_attention(b_q, b_kv[:, :, 0], b_kv[:, :, 1], _rms(b_kv[:, :, 2], qk[3]), b_kv[:, :, 3],
                             _rms(b_kv[:, :, 4], qk[3]), b_kv[:, :, 5], b_gates, nsa_cmp_pos[layer],
                             nsa_cmp_w[layer], qk[3], rel_b) @ w_branch_b[layer]
        c_qkv = c_qkv.reshape(bsz, seq, 3, C_HEADS, HEAD_DIM)
        y_c = _dilated_attention(_rms(c_qkv[:, :, 0], qk[4]), _rms(c_qkv[:, :, 1], qk[5]), c_qkv[:, :, 2],
                                 rel_c) @ w_branch_c[layer]
        g = jax.nn.sigmoid(mix_g).reshape(bsz, seq, 3, D_MODEL)
        x = x + (g[:, :, 0] * y_a + g[:, :, 1] * y_b + g[:, :, 2] * y_c) @ w_out[layer]
        h = _rms(x, norm2_g[layer])
        gate, up = jnp.split(h @ w_ffn_in[layer], 2, axis=-1)
        x = x + (jax.nn.silu(gate) * up) @ w_ffn_out[layer]
    return x


def setup_inputs(seed=0):
    out = dict(first_inputs(seed))
    for name, value in second_inputs(seed + 1).items():
        if name != "x":
            out[name + "_2"] = value
    return out


def reference(
    x, attn_norm, attn_w_qkv, attn_rel_bias, attn_w_o, dn_norm, dn_w_in, dn_conv_w, dn_a_log,
    dn_dt_bias, dn_head_norm, dn_w_o, mlp_norm, mlp_w_up, mlp_w_down, final_norm, norm1_g_2,
    norm2_g_2, w_in_2, qk_norm_g_2, nsa_cmp_pos_2, nsa_cmp_w_2, w_branch_a_2, w_branch_b_2,
    w_branch_c_2, w_out_2, w_ffn_in_2, w_ffn_out_2, rel_bias_2,
):
    x = first_block(
        x, attn_norm, attn_w_qkv, attn_rel_bias, attn_w_o, dn_norm, dn_w_in, dn_conv_w,
        dn_a_log, dn_dt_bias, dn_head_norm, dn_w_o, mlp_norm, mlp_w_up, mlp_w_down, final_norm,
    )
    return second_block(
        x, norm1_g_2, norm2_g_2, w_in_2, qk_norm_g_2, nsa_cmp_pos_2, nsa_cmp_w_2, w_branch_a_2,
        w_branch_b_2, w_branch_c_2, w_out_2, w_ffn_in_2, w_ffn_out_2, rel_bias_2,
    )


_drawn_inputs = setup_inputs


def setup_inputs(seed=0):
    import zlib

    import numpy as np

    out = dict(_drawn_inputs(seed))
    spreads = {}
    factors = {'attn_norm': 6.085,
     'attn_rel_bias': 3.071,
     'dn_norm': 18.388,
     'dn_head_norm': 29.528,
     'mlp_norm': 8.0,
     'qk_norm_g_2': 3.003}
    for name, (base, spread) in spreads.items():
        noise = np.random.default_rng([zlib.crc32(name.encode()), seed]).standard_normal(out[name].shape)
        drawn = base * np.exp(spread * noise) if base else spread * noise
        out[name] = jnp.asarray(drawn.astype(out[name].dtype))
    for name, factor in factors.items():
        out[name] = (out[name] * factor).astype(out[name].dtype)
    return out
```

```python
import math
from contextlib import ExitStack

import numpy as np
import concourse.bass as bass
from concourse import mybir

P = 128
F32 = mybir.dt.float32
F32R = mybir.dt.float32r
ALU = mybir.AluOpType
ACT = mybir.ActivationFunctionType
AX = mybir.AxisListType

SEQ, D = 512, 1024
KT = D // P
TT = SEQ // P
EPS = 1e-6
MASKED = -1e30
ATTN_HEADS, HEAD_DIM, MAX_REL = 16, 64, 256
CHUNK = 64
DN_HEADS, DN_HEAD_DIM = 8, 128
D_FF = 4 * D
FF_HALF = D_FF // P // 2
D_FF_2 = 2816
FF2 = D_FF_2 // P
CMP_LEN, CMP_STRIDE, CMP_PAD = 32, 16, 32
CMP_N = (SEQ - CMP_LEN) // CMP_STRIDE + 1
IDX_HEADS, TOPK = 4, 128
REL_BUCKETS, REL_MAX_DIST = 32, 2048
TOEPLITZ = SEQ + P - 1

RING = 4
AHEAD = 2
SLOT_TILES = 8


class Count:

    def __init__(self, sem, base):
        self.sem, self.base = sem, base

    def __call__(self, n):
        return self.sem, self.base + n


class Signal:

    def __init__(self, nc, name):
        self.sem, self.used = nc.alloc_semaphore(name), 0

    def reserve(self, total):
        self.used += total
        return Count(self.sem, self.used - total)


class Chain:

    def __init__(self, eng, sem):
        self.eng, self.sem = eng, sem
        self.start, self.turn, self.marks, self.local = 0, 0, 0, 0

    def mark(self, instruction):
        self.local += 1
        instruction.then_inc(self.sem, 1)

    def wait(self):
        self.eng.wait_ge(self.sem, self.turn * self.marks + self.start + self.local)

    def step(self, instruction):
        self.mark(instruction)
        self.wait()


def repeat(eng, n, unroll, chain=None, marks=0):
    whole = n // unroll

    def turn(i, u):
        if chain is not None:
            chain.start += chain.local
            chain.local = 0
            chain.turn, chain.marks = i * unroll + u, marks
        return i, u

    def ended():
        if chain is not None:
            assert chain.local == marks, (chain.local, marks)
            chain.local = 0

    if chain is not None:
        chain.start += chain.local
        chain.local = 0
    if whole > 1:
        with eng.Fori(0, whole) as i:
            for u in range(unroll):
                yield turn(i, u)
                ended()
    elif whole == 1:
        for u in range(unroll):
            yield turn(0, u)
            ended()
    for u in range(n - whole * unroll):
        yield turn(whole, u)
        ended()
    if chain is not None:
        chain.start += n * marks
        chain.turn, chain.marks = 0, 0


def at(buf, t):
    if isinstance(t, int):
        return buf[:, t]
    return buf[:, bass.ds(t, 1)].rearrange("p o n -> p (o n)")


class Core:

    def __init__(self, nc, ctx, io):
        self.nc, self.io = nc, io

        def sb(name, shape, dt=F32):
            return ctx.enter_context(nc.sbuf_tensor(name, shape, dt))

        self.w_raw = sb("w_raw", [P, RING, SLOT_TILES, P])
        self.w_hi = sb("w_hi", [P, RING, SLOT_TILES, P], F32R)
        self.w_lo = sb("w_lo", [P, RING, SLOT_TILES, P], F32R)
        self.x = sb("x", [P, KT, SEQ])
        start = -(-nc.sbuf_base // 64) * 64
        self.h_hi = sb("h_hi", [P, KT, SEQ], F32R)
        self.h_lo = sb("h_lo", [P, KT, SEQ], F32R)
        self.h_words = nc.alloc_sbuf_tensor_at("h_words", [P, 2 * KT, SEQ], F32, offset=start)
        self.ssq = sb("ssq", [P, SEQ])
        self.sq = sb("sq", [P, 2, SEQ])
        self.tmp = sb("tmp", [P, 2, SEQ])
        self.rstd = sb("rstd", [P, SEQ])
        self.norm_w = sb("norm_w", [P, 8, KT])
        self.ones = sb("ones", [P, P])
        self.ident = sb("ident", [P, P])
        self.halves = sb("halves", [P, 2])
        self.prefix = sb("prefix", [P, P])
        self.chunks = sb("chunks", [P, P])
        self.first = sb("first", [P, 2, P])
        self.levels = sb("levels", [P, 6, P])
        self.conv_w = sb("conv_w", [P, 3 * KT, 4])
        self.causal = sb("causal", [P, SEQ])
        self.gains = sb("gains", [P, 6])
        self.cmp_pos = sb("cmp_pos", [P, 2, CMP_LEN])
        self.cmp_mask = sb("cmp_mask", [P, TT, CMP_PAD])
        self.row_valid = sb("row_valid", [P, TT])
        self.dn_small = sb("dn_small", [P, 3, DN_HEADS])
        self.arena, self.used, self.named = -(-nc.sbuf_base // 64) * 64, 0, 0
        self.arena_words = (nc.sbuf_usable_end - self.arena) // 4
        self.psum = ctx.enter_context(nc.psum_tensor("psum", [P, 8, SEQ], F32))

        def sem(name):
            return nc.alloc_semaphore(name)

        self.raw_loaded = [sem(f"raw_loaded_{s}") for s in range(RING)]
        self.hi_ready, self.lo_ready, self.slot_used = sem("hi_ready"), sem("lo_ready"), sem("slot_used")
        self.loaded, self.all_done, self.stored = sem("loaded"), sem("all_done"), sem("stored")
        self.passed = [sem("vector_passed"), sem("pool_passed")]
        self.chains = [sem("scalar_steps"), sem("vector_steps"), sem("pool_steps")]
        self.signals = {}
        self.slots = 0

    def count(self, name, total):
        if name not in self.signals:
            self.signals[name] = Signal(self.nc, name)
        return self.signals[name].reserve(total)

    def take(self, *shape, dt=F32):
        words = -(-math.prod(shape) // 16) * 16
        assert self.used + words <= self.arena_words, (self.used, words, self.arena_words)
        self.named += 1
        buf = self.nc.alloc_sbuf_tensor_at(f"scratch_{self.named}", [P, *shape], dt, offset=self.arena + 4 * self.used)
        self.used += words
        return buf

    def take_parts(self, *shape):
        return self.take(*shape, dt=F32R), self.take(*shape, dt=F32R)

    def split_hi(self, act, i, per, k):
        s = k % RING
        act.wait_ge(self.raw_loaded[s], (i * (per // RING) + k // RING + 1) * 16)
        act.wait_ge(self.slot_used, i * per + k + 1)
        act.copy(self.w_hi[:, s], self.w_raw[:, s]).then_inc(self.hi_ready, 1)

    def split_lo(self, dve, i, per, k):
        s = k % RING
        dve.wait_ge(self.hi_ready, i * per + k + 1)
        self.nc.vector.tensor_tensor(self.w_lo[:, s], self.w_raw[:, s], self.w_hi[:, s],
                                     ALU.subtract).then_inc(self.lo_ready, 1)


class Stage:
    def tensor(self, pe): pass
    def vector(self, dve, chain): pass
    def scalar(self, act, chain): pass
    def gpsimd(self, pool, chain): pass


class Load(Stage):

    def __init__(self, c):
        self.c = c
        self.sq_done, self.sq_used = c.count("sq_done", KT), c.count("sq_used", KT + 2)

    def tensor(self, pe):
        pe.sem_inc(self.sq_used.sem, 2)
        pe.sem_inc(self.c.slot_used, RING)

    def scalar(self, act, chain):
        c = self.c
        act.wait_ge(c.loaded, 16 * c.n_loads)
        for k in range(KT):
            act.wait_ge(*self.sq_used(k + 1))
            act.activation(c.sq[:, k % 2], c.x[:, k], ACT.Square).then_inc(self.sq_done.sem, 1)
        for n in range(AHEAD):
            c.split_hi(act, 0, RING, n)

    def vector(self, dve, chain):
        c, nc = self.c, self.c.nc
        chain.step(nc.vector.memset(c.ssq[:], 0.0))
        for k in range(KT):
            dve.wait_ge(*self.sq_done(k + 1))
            ins = nc.vector.tensor_tensor(c.ssq[:], c.ssq[:], c.sq[:, k % 2], ALU.add)
            ins.then_inc(self.sq_used.sem, 1)
            dve.wait_ge(*self.sq_used(k + 3))
        for n in range(AHEAD):
            c.split_lo(dve, 0, RING, n)


class Norm(Stage):

    def __init__(self, c, index, keep=False):
        self.c, self.index, self.keep = c, index, keep
        self.sum_ready, self.var_ready = c.count("sum_ready", 1), c.count("var_ready", 1)
        self.rstd_ready = c.count("rstd_ready", 1)
        self.val_ready, self.hi_done, self.lo_done = (c.count(n, KT) for n in ("val_ready", "hi_done", "lo_done"))

    def tensor(self, pe):
        c = self.c
        pe.matmul(c.psum[:, 7], c.ones[:], c.ssq[:], start=True, stop=True).then_inc(self.sum_ready.sem, 1)

    def scalar(self, act, chain):
        c = self.c
        act.wait_ge(*self.var_ready(1))
        act.activation(c.rstd[:], c.tmp[:, 1], ACT.Sqrt).then_inc(self.rstd_ready.sem, 1)
        for k in range(KT):
            act.wait_ge(*self.val_ready(k + 1))
            if self.keep:
                act.activation(c.sq[:, k % 2], c.x[:, k], ACT.Square).then_inc(self.hi_done.sem, 1)
            else:
                act.copy(c.h_hi[:, k], c.tmp[:, k % 2]).then_inc(self.hi_done.sem, 1)

    def vector(self, dve, chain):
        c, nc = self.c, self.c.nc
        dve.wait_ge(*self.sum_ready(1))
        chain.step(nc.vector.tensor_scalar(c.tmp[:, 0], c.psum[:, 7], 1.0 / D, EPS, ALU.mult, ALU.add))
        nc.vector.reciprocal(c.tmp[:, 1], c.tmp[:, 0]).then_inc(self.var_ready.sem, 1)
        if self.keep:
            chain.step(nc.vector.memset(c.ssq[:], 0.0))
        dve.wait_ge(*self.rstd_ready(1))

        def finish(k):
            dve.wait_ge(*self.hi_done(k + 1))
            if self.keep:
                nc.vector.tensor_tensor(c.ssq[:], c.ssq[:], c.sq[:, k % 2], ALU.add).then_inc(self.lo_done.sem, 1)
            else:
                nc.vector.tensor_tensor(c.h_lo[:, k], c.tmp[:, k % 2], c.h_hi[:, k],
                                        ALU.subtract).then_inc(self.lo_done.sem, 1)

        for k in range(KT):
            if k >= 2:
                dve.wait_ge(*self.lo_done(k - 1))
            dst = c.x[:, k] if self.keep else c.tmp[:, k % 2]
            nc.vector.scalar_tensor_tensor(dst, c.x[:, k], c.norm_w[:, self.index, k:k + 1], c.rstd[:],
                                           ALU.mult, ALU.mult).then_inc(self.val_ready.sem, 1)
            if k >= 1:
                finish(k - 1)
                dve.wait_ge(*self.lo_done(k))
        finish(KT - 1)


class Linear(Stage):
    unroll = 4
    two_banks = True

    def __init__(self, c, tiles, source=None, slots=(SLOT_TILES,), token_major=False, cols=P, unroll=None):
        self.c, self.tiles, self.slots, self.token_major, self.cols = c, tiles, slots, token_major, cols
        self.source = source or (c.h_hi, c.h_lo)
        self.per = len(slots)
        self.unroll = unroll or 4
        assert self.unroll * self.per % RING == 0 and self.unroll % 2 == 0
        self.slot0 = c.slots
        c.slots += tiles * self.per
        if self.two_banks:
            self.bank_read = c.count("bank_read", tiles + 2)
        self.begin()

    def begin(self): pass

    def out(self, u):
        bank = self.c.psum[:, u % 2]
        if self.token_major:
            return bank[:, :TT * self.cols].rearrange("p (t n) -> p t n", t=TT)
        return bank

    def done(self, i, u):
        c = self.c
        return c.slot_used, (i * self.unroll + u + 1) * self.per + self.slot0 + RING

    def tensor(self, pe):
        c = self.c
        pe.sem_inc(self.bank_read.sem, 2)
        hi, lo = self.source
        for i, u in repeat(pe, self.tiles, self.unroll):
            pe.wait_ge(*self.bank_read(i * self.unroll + u + 1))
            self.kind = u
            for j, tiles in enumerate(self.slots):
                k0 = self.slot0 + u * self.per + j
                s = k0 % RING
                pe.wait_ge(c.lo_ready, i * (self.unroll * self.per) + k0 + 1)
                first, last = j == 0, j == self.per - 1
                if self.token_major:
                    out = self.out(u)
                    for t in range(TT):
                        for k in range(tiles):
                            rows = slice(t * P, (t + 1) * P)
                            pairs = ((hi, c.w_hi), (hi, c.w_lo), (lo, c.w_hi))
                            for n, (a, w) in enumerate(pairs):
                                mm = pe.matmul(out[:, t], a[:, k, rows], w[:, s, k, :self.cols],
                                               start=(k == 0 and n == 0), stop=(k == tiles - 1 and n == 2))
                else:
                    for k in range(tiles):
                        kk = j * SLOT_TILES + k
                        pairs = ((c.w_hi, hi), (c.w_hi, lo), (c.w_lo, hi))
                        for n, (w, b) in enumerate(pairs):
                            mm = pe.matmul(self.out(u), w[:, s, k], self.rhs(b, kk),
                                           start=(first and k == 0 and n == 0),
                                           stop=(last and k == tiles - 1 and n == 2))
                mm.then_inc(c.slot_used, 1)

    def rhs(self, part, k):
        return part[:, k]

    def scalar(self, act, chain):
        for i, u in repeat(act, self.tiles, self.unroll, chain, self.scalar_marks):
            for j in range(self.per):
                self.c.split_hi(act, i, self.unroll * self.per, self.slot0 + u * self.per + j + AHEAD)
            self.scalar_tile(act, chain, i, u)

    def vector(self, dve, chain):
        self.vector_begin(dve, chain)
        for i, u in repeat(dve, self.tiles, self.unroll, chain, self.vector_marks):
            for j in range(self.per):
                self.c.split_lo(dve, i, self.unroll * self.per, self.slot0 + u * self.per + j + AHEAD)
            self.vector_tile(dve, chain, i, u)

    scalar_marks = vector_marks = 0
    def scalar_tile(self, act, chain, i, u): pass
    def vector_begin(self, dve, chain): pass
    def vector_tile(self, dve, chain, i, u): pass


class Project(Linear):

    def __init__(self, c, tiles, dst, scale=1.0, func=ACT.Copy, **kw):
        self.dst, self.scale, self.func = dst, scale, func
        super().__init__(c, tiles, **kw)

    def scalar_tile(self, act, chain, i, u):
        t = i * self.unroll + u
        act.wait_ge(*self.done(i, u))
        if self.token_major:
            dst = self.dst[:, :, bass.ds(t * P, self.cols)]
        else:
            dst = at(self.dst, t)
        act.activation(dst, self.out(u), self.func, scale=self.scale).then_inc(self.bank_read.sem, 1)


class Residual(Linear):

    def __init__(self, c, tiles=KT, gather=True, **kw):
        self.gather = gather
        super().__init__(c, tiles, **kw)

    def begin(self):
        c = self.c
        self.sq_done, self.sq_used = c.count("sq_done", self.tiles), c.count("sq_used", self.tiles + 2)

    def tensor(self, pe):
        pe.sem_inc(self.sq_used.sem, 2)
        super().tensor(pe)

    def vector_begin(self, dve, chain):
        chain.step(self.c.nc.vector.memset(self.c.ssq[:], 0.0))

    def vector_tile(self, dve, chain, i, u):
        c, t = self.c, i * self.unroll + u
        dve.wait_ge(*self.done(i, u))
        c.nc.vector.tensor_tensor(at(c.x, t), at(c.x, t), self.out(u), ALU.add).then_inc(self.bank_read.sem, 1)
        dve.wait_ge(*self.sq_done(t + 1))
        dve.wait_ge(*self.sq_used(t + 2))
        c.nc.vector.tensor_tensor(c.ssq[:], c.ssq[:], c.sq[:, u % 2], ALU.add).then_inc(self.sq_used.sem, 1)

    def scalar_tile(self, act, chain, i, u):
        c, t = self.c, i * self.unroll + u
        act.wait_ge(*self.bank_read(t + 3))
        act.wait_ge(*self.sq_used(t + 1))
        act.activation(c.sq[:, u % 2], at(c.x, t), ACT.Square).then_inc(self.sq_done.sem, 1)


class ReluSquare(Linear):

    def __init__(self, c, tiles, dst, **kw):
        self.dst = dst
        super().__init__(c, tiles, **kw)

    def begin(self):
        c = self.c
        self.val_ready, self.hi_done = c.count("val_ready", self.tiles), c.count("hi_done", self.tiles)
        self.lo_done = c.count("lo_done", self.tiles + 2)

    def tensor(self, pe):
        pe.sem_inc(self.lo_done.sem, 2)
        super().tensor(pe)

    def scalar_tile(self, act, chain, i, u):
        c, t = self.c, i * self.unroll + u
        act.wait_ge(*self.done(i, u))
        act.wait_ge(*self.lo_done(t + 1))
        act.activation(c.tmp[:, u % 2], self.out(u), ACT.Relu).then_inc(self.bank_read.sem, 1)
        act.wait_ge(*self.bank_read(t + 3))
        act.activation(at(self.dst[0], t), c.tmp[:, u % 2], ACT.Square).then_inc(self.hi_done.sem, 1)

    def vector_tile(self, dve, chain, i, u):
        c, t = self.c, i * self.unroll + u
        dve.wait_ge(*self.bank_read(t + 3))
        c.nc.vector.tensor_tensor(c.sq[:, u % 2], c.tmp[:, u % 2], c.tmp[:, u % 2],
                                  ALU.mult).then_inc(self.val_ready.sem, 1)
        dve.wait_ge(*self.val_ready(t + 1))
        dve.wait_ge(*self.hi_done(t + 1))
        c.nc.vector.tensor_tensor(at(self.dst[1], t), c.sq[:, u % 2], at(self.dst[0], t),
                                  ALU.subtract).then_inc(self.lo_done.sem, 1)


class Steps:

    def __init__(self, c, name, steps, turns, before=0):
        assert len(set(steps)) == len(steps)
        self.steps, self.before = steps, before
        self.count, self.next = c.count(name, len(steps) * (turns + before)), 0

    def begin(self, eng):
        eng.sem_inc(self.count.sem, self.before * len(self.steps))

    def mark(self, instruction, step):
        assert self.steps[self.next % len(self.steps)] == step, (self.steps[self.next % len(self.steps)], step)
        self.next += 1
        instruction.then_inc(self.count.sem, 1)

    def __call__(self, turn, step):
        return self.count(turn * len(self.steps) + self.before * len(self.steps) + self.steps.index(step) + 1)


class ConvProject(Linear):
    TAPS = 4

    def __init__(self, c, tiles, dst):
        self.dst = dst
        self.raw, self.acc = c.take(2, SEQ + 16), c.take(2, SEQ)
        super().__init__(c, tiles)

    def begin(self):
        c = self.c
        self.conv_done = c.count("val_ready", self.tiles)
        self.silu_done = c.count("hi_done", self.tiles + 2)
        self.pads = self.TAPS - 1

    vector_marks = 3

    def tensor(self, pe):
        pe.sem_inc(self.silu_done.sem, 2)
        super().tensor(pe)

    def vector_begin(self, dve, chain):
        chain.step(self.c.nc.vector.memset(self.raw[:, :, :self.pads], 0.0))

    def scalar_tile(self, act, chain, i, u):
        t = i * self.unroll + u
        act.wait_ge(*self.done(i, u))
        act.wait_ge(*self.silu_done(t + 1))
        act.copy(self.raw[:, u % 2, self.pads:self.pads + SEQ], self.out(u)).then_inc(self.bank_read.sem, 1)
        act.wait_ge(*self.conv_done(t + 1))
        act.activation(at(self.dst, t), self.acc[:, u % 2], ACT.Silu).then_inc(self.silu_done.sem, 1)

    def vector_tile(self, dve, chain, i, u):
        c, t = self.c, i * self.unroll + u
        v, raw, acc = c.nc.vector, self.raw[:, u % 2], self.acc[:, u % 2]
        dve.wait_ge(*self.bank_read(t + 3))
        dve.wait_ge(*self.silu_done(t + 1))

        def tap(j):
            return c.conv_w[:, bass.ds(t, 1), j:j + 1].rearrange("p a b -> p (a b)")

        chain.step(v.tensor_scalar(acc, raw[:, :SEQ], tap(0), None, ALU.mult))
        for j in range(1, self.TAPS):
            ins = v.scalar_tensor_tensor(acc, raw[:, j:j + SEQ], tap(j), acc, ALU.mult, ALU.add)
            if j < self.TAPS - 1:
                chain.step(ins)
            else:
                ins.then_inc(self.conv_done.sem, 1)


class HeadNorm(Stage):

    def __init__(self, c, tiles, per=1, n=1.0, scale=1.0, gains=None):
        self.c, self.tiles, self.per, self.n, self.scale = c, tiles, per, n, scale
        self.gains = gains or [None] * len(tiles)
        self.cols = len(tiles) * per
        self.var = c.take(3, TT, self.cols)
        self.rows = c.take(SEQ)
        self.sq_done, self.sums_ready = c.count("sq_done", len(tiles)), c.count("sum_ready", len(tiles) + 2)
        self.inverse, self.root = c.count("var_ready", 1), c.count("rstd_ready", 1)
        self.turned, self.rows_ready = c.count("turned", 1), c.count("hi_done", 1)
        self.spread, self.scaled = c.count("aux_a", len(tiles)), c.count("aux_b", len(tiles))

    def tensor(self, pe):
        c = self.c
        sums = c.psum[:, 0, :TT * self.cols].rearrange("p (t n) -> p t n", t=TT)
        ones = c.ones[:, :1] if self.per == 1 else c.halves[:]
        pe.sem_inc(self.sums_ready.sem, 2)
        for j in range(len(self.tiles)):
            pe.wait_ge(*self.sq_done(j + 1))
            for t in range(TT):
                mm = pe.matmul(sums[:, t, j * self.per:(j + 1) * self.per], c.sq[:, j % 2, t * P:(t + 1) * P], ones,
                               start=True, stop=True)
            mm.then_inc(self.sums_ready.sem, 1)
        pe.wait_ge(*self.root(1))
        for t in range(TT):
            mm = pe.transpose(c.psum[:self.cols, 1, t * P:(t + 1) * P], self.var[:, 2, t], c.ident[:])
        mm.then_inc(self.turned.sem, 1)
        pe.wait_ge(*self.rows_ready(1))
        for j in range(len(self.tiles)):
            if j >= 2:
                pe.wait_ge(*self.scaled(j - 1))
            for k in range(self.per):
                to, wide = slice(k * P // self.per, (k + 1) * P // self.per), P // self.per
                row = j * self.per + k
                mm = pe.matmul(c.psum[to, 2 + j % 2], c.ident[:self.cols, row:row + 1].broadcast_to([self.cols, wide]),
                               self.rows[:self.cols], start=True, stop=True)
            mm.then_inc(self.spread.sem, 1)

    def scalar(self, act, chain):
        c = self.c
        for j, tile in enumerate(self.tiles):
            act.wait_ge(*self.sums_ready(j + 1))
            act.activation(c.sq[:, j % 2], tile, ACT.Square).then_inc(self.sq_done.sem, 1)
        act.wait_ge(*self.inverse(1))
        act.activation(self.var[:, 2], self.var[:, 1], ACT.Sqrt, scale=self.scale ** 2).then_inc(self.root.sem, 1)
        act.wait_ge(*self.turned(1))
        act.copy(self.rows[:self.cols], c.psum[:self.cols, 1]).then_inc(self.rows_ready.sem, 1)

    def vector(self, dve, chain):
        c, v = self.c, self.c.nc.vector
        dve.wait_ge(*self.sums_ready(len(self.tiles) + 2))
        sums = c.psum[:, 0, :TT * self.cols].rearrange("p (t n) -> p t n", t=TT)
        chain.step(v.tensor_scalar(self.var[:, 0], sums, 1.0 / self.n, EPS, ALU.mult, ALU.add))
        v.reciprocal(self.var[:, 1], self.var[:, 0]).then_inc(self.inverse.sem, 1)
        for j, tile in enumerate(self.tiles):
            dve.wait_ge(*self.spread(j + 1))
            gain = 1.0 if self.gains[j] is None else self.gains[j]
            v.scalar_tensor_tensor(tile, tile, gain, c.psum[:, 2 + j % 2], ALU.mult,
                                   ALU.mult).then_inc(self.scaled.sem, 1)


class DnGates(Stage):

    def __init__(self, c, ab):
        self.c, self.ab = c, ab
        n = TT * DN_HEADS
        self.w = c.take(12, TT, DN_HEADS)
        names = ("z", "abs", "soft", "softplus", "g", "beta", "gc", "rest", "beg", "dk", "eg", "minus")
        self.at = {name: self.w[:, k] for k, name in enumerate(names)}
        self.rate = c.take(DN_HEADS)
        self.last = c.take(2, TT, DN_HEADS)
        self.rows = c.take(2, SEQ)
        self.rows_dram = c.nc.dram_tensor("dn_rows", (2, DN_HEADS, SEQ), F32, kind="Internal").ap()
        self.did_dve = Steps(c, "aux_a", ("z", "minus", "abs", "sp", "g", "gc", "rest", "beg"), 1)
        self.did_act = Steps(c, "aux_b", ("exp", "ln", "rate", "beta", "eg", "dk", "last", "rows"), 1)
        self.did_pe = Steps(c, "aux_c", ("sums", "rows"), 1)
        self.stored = c.count("aux_d", 32)

    def vector(self, dve, chain):
        c, v, a, did = self.c, self.c.nc.vector, self.at, self.did_dve
        bias = c.dn_small[:, 1:2].broadcast_to([P, TT, DN_HEADS])
        did.mark(v.tensor_tensor(a["z"], self.ab[:, :, :DN_HEADS], bias, ALU.add), "z")
        dve.wait_ge(*did(0, "z"))
        did.mark(v.tensor_scalar(a["minus"], a["z"], -1.0, None, ALU.mult), "minus")
        dve.wait_ge(*did(0, "minus"))
        did.mark(v.tensor_tensor(a["abs"], a["z"], a["minus"], ALU.max), "abs")
        dve.wait_ge(*self.did_act(0, "ln"))
        did.mark(v.scalar_tensor_tensor(a["softplus"], a["z"], 0.0, a["soft"], ALU.max, ALU.add), "sp")
        dve.wait_ge(*did(0, "sp"))
        dve.wait_ge(*self.did_act(0, "rate"))
        rate = self.rate[:].unsqueeze(1).broadcast_to([P, TT, DN_HEADS])
        did.mark(v.scalar_tensor_tensor(a["g"], a["softplus"], -1.0, rate, ALU.mult, ALU.mult), "g")
        dve.wait_ge(*self.did_pe(0, "sums"))
        n = TT * DN_HEADS
        did.mark(v.tensor_copy(a["gc"], c.psum[:, 0, :n].rearrange("p (t h) -> p t h", t=TT)), "gc")
        dve.wait_ge(*did(0, "gc"))
        did.mark(v.tensor_tensor(a["rest"], c.psum[:, 0, n:2 * n].rearrange("p (t h) -> p t h", t=TT), a["gc"],
                                 ALU.subtract), "rest")
        dve.wait_ge(*self.did_act(0, "eg"))
        did.mark(v.tensor_tensor(a["beg"], a["beta"], a["eg"], ALU.mult), "beg")

    def scalar(self, act, chain):
        c, a, did = self.c, self.at, self.did_act
        act.wait_ge(*self.did_dve(0, "abs"))
        did.mark(act.activation(a["soft"], a["abs"], ACT.Exp, scale=-1.0), "exp")
        act.wait_ge(*did(0, "exp"))
        did.mark(act.activation(a["soft"], a["soft"], ACT.Ln, bias=1.0), "ln")
        did.mark(act.activation(self.rate[:], c.dn_small[:, 0], ACT.Exp), "rate")
        did.mark(act.activation(a["beta"], self.ab[:, :, DN_HEADS:], ACT.Sigmoid), "beta")
        act.wait_ge(*self.did_dve(0, "gc"))
        did.mark(act.activation(a["eg"], a["gc"], ACT.Exp), "eg")
        act.wait_ge(*self.did_dve(0, "rest"))
        did.mark(act.activation(a["dk"], a["rest"], ACT.Exp), "dk")
        n = TT * DN_HEADS
        did.mark(act.activation(self.last[:], c.psum[:, 0, 2 * n:4 * n].rearrange("p (b t h) -> p b t h", b=2, t=TT),
                                ACT.Exp), "last")
        act.wait_ge(*self.did_pe(0, "rows"))
        did.mark(act.copy(self.rows[:DN_HEADS], c.psum[:DN_HEADS, 1:3]), "rows")

    def tensor(self, pe):
        c, a = self.c, self.at
        n = TT * DN_HEADS
        pe.wait_ge(*self.did_dve(0, "g"))
        g = a["g"].rearrange("p t h -> p (t h)")
        for k, w in enumerate((c.prefix[:], c.chunks[:], c.first[:, 0], c.first[:, 1])):
            mm = pe.matmul(c.psum[:, 0, k * n:(k + 1) * n], w, g, start=True, stop=True)
        self.did_pe.mark(mm, "sums")
        pe.wait_ge(*self.did_dve(0, "gc"))
        pe.wait_ge(*self.did_act(0, "beta"))
        for k, name in enumerate(("gc", "beta")):
            for t in range(TT):
                mm = pe.transpose(c.psum[:DN_HEADS, 1 + k, t * P:(t + 1) * P], a[name][:, t], c.ident[:])
        self.did_pe.mark(mm, "rows")

    def gpsimd(self, pool, chain):
        pool.wait_ge(*self.did_act(0, "rows"))
        for k in range(2):
            pool.dma_start(self.rows_dram[k], self.rows[:DN_HEADS, k]).then_inc(self.stored.sem, 16)
        pool.wait_ge(*self.stored(32))


class DeltaRule(Stage):

    LEVELS = 6

    def __init__(self, c, qkv, gates, out):
        self.c, self.qkv, self.g, self.out = c, qkv, gates, out
        words = [c.h_words[:, k] for k in range(2 * KT)]
        names = ("decay", "grow", "qkd", "lt", "ct", "x", "xt", "y", "kbg", "vb", "kd", "u", "wt", "vn", "state")
        self.b = {name: words[k] for k, name in enumerate(names)}
        self.f = c.take(2, 5, SEQ)
        self.fetched = [c.count(f"fetched_{b}", 16 * 5 * DN_HEADS // 2) for b in range(2)]
        levels = range(1, self.LEVELS)
        scan = range(SEQ // CHUNK)
        pe = ["kk", "kq", "k_turned", "v_turned", "x0"] + [f"{s}{b}" for b in levels for s in ("y", "zt")]
        pe += ["u", "wt"] + [f"{s}{n}" for n in scan for s in ("ws", "o", "ds")]
        dve = [f"d{t}" for t in range(TT)] + ["decay", "qkd", "kkd", "lt", "ct0", "xt0", "qd"]
        dve += [f"{s}{b}" for b in levels for s in ("ct", "x", "xt") if (s, b) != ("x", self.LEVELS - 1)]
        dve += ["wt", "s0"] + [f"{s}{n}" for n in scan for s in ("vn", "s_")]
        act = ["decay", "grow"] + [f"{s}{t}" for t in range(TT) for s in ("kbg", "kd", "vb")]
        act += ["x0"] + [f"y{b}" for b in levels] + ["u", "o"]
        self.pe_did = Steps(c, "aux_a", pe, DN_HEADS)
        self.dve_did = Steps(c, "aux_b", dve, DN_HEADS)
        self.act_did = Steps(c, "aux_c", act, DN_HEADS, before=2)

    def gpsimd(self, pool, chain):
        for i, h in repeat(pool, DN_HEADS, 2):
            head = i * 2 + h
            pool.wait_ge(*self.act_did(head - 2, "o"))
            pool.sem_inc(self.c.passed[1], 1)
            rows = self.g.rows_dram
            moves = [(self.f[:, h, n], at(self.qkv, n * DN_HEADS + head)) for n in range(3)]
            moves += [(self.f[:, h, 3 + n], rows[n, bass.ds(head, 1)].broadcast_to([P, SEQ])) for n in range(2)]
            for to, of in moves:
                pool.dma_start(to, of).then_inc(self.fetched[h].sem, 16)

    def tensor(self, pe):
        c, b, did = self.c, self.b, self.pe_did
        dve, act = self.dve_did, self.act_did
        tiles = [slice(t * P, (t + 1) * P) for t in range(TT)]
        self.act_did.begin(pe)

        def product(bank, left, right):
            for t in tiles:
                mm = pe.matmul(c.psum[:, bank, t], left[:, t], right[:, t], start=True, stop=True)
            return mm

        def turn(bank, of):
            for t in tiles:
                mm = pe.transpose(c.psum[:, bank, t], of[:, t], c.ident[:])
            return mm

        for i, h in repeat(pe, DN_HEADS, 2):
            head = i * 2 + h
            q, k, v = (self.f[:, h, n] for n in range(3))
            pe.wait_ge(*self.fetched[h](i * 80 + 80))
            pe.wait_ge(*act(head - 1, "o"))
            did.mark(product(0, k, k), "kk")
            did.mark(product(1, k, q), "kq")
            did.mark(turn(2, k), "k_turned")
            did.mark(turn(3, v), "v_turned")
            pe.wait_ge(*dve(head, "xt0"))
            did.mark(turn(4, b["xt"]), "x0")
            for n in range(1, self.LEVELS):
                pe.wait_ge(*(act(head, "x0") if n == 1 else dve(head, f"xt{n - 1}")))
                pe.wait_ge(*dve(head, f"ct{n}"))
                did.mark(product(5, b["ct"], b["x"]), f"y{n}")
                pe.wait_ge(*act(head, f"y{n}"))
                if n < self.LEVELS - 1:
                    product(6, b["xt"], b["y"])
                did.mark(product(7, b["y"], b["xt"]), f"zt{n}")
            pe.wait_ge(*dve(head, f"xt{self.LEVELS - 1}"))
            pe.wait_ge(*act(head, f"vb{TT - 1}"))
            did.mark(product(4, b["xt"], b["vb"]), "u")
            did.mark(product(5, b["kbg"], b["xt"]), "wt")
            state = b["state"][:, :P]
            pe.wait_ge(*dve(head, "wt"))
            for n in range(SEQ // CHUNK):
                t, half = n // 2, n % 2
                rows, tokens = slice(half * CHUNK, (half + 1) * CHUNK), slice(n * CHUNK, (n + 1) * CHUNK)
                pe.wait_ge(*dve(head, "s0" if n == 0 else f"s_{n - 1}"))
                did.mark(pe.matmul(c.psum[:, 6, :P], b["wt"][:, tiles[t]], state, start=True, stop=True), f"ws{n}")
                pe.wait_ge(*dve(head, f"vn{n}"))
                out = c.psum[:, 7, tokens]
                pe.matmul(out, state, q[:, tokens], start=True, stop=False)
                did.mark(pe.matmul(out, b["vn"][rows, tiles[t]], b["qkd"][rows, tokens], start=False, stop=True), f"o{n}")
                did.mark(pe.matmul(c.psum[:, 5, :P], b["kd"][rows, tiles[t]], b["vn"][rows, tiles[t]],
                                   start=True, stop=True), f"ds{n}")

    def vector(self, dve, chain):
        c, v, b, did = self.c, self.c.nc.vector, self.b, self.dve_did
        pe, act, g = self.pe_did, self.act_did, self.g
        tiles = [slice(t * P, (t + 1) * P) for t in range(TT)]

        def tiled(buf):
            return buf.rearrange("p (t n) -> p t n", t=TT)

        def mask(m):
            return m.unsqueeze(1).broadcast_to([P, TT, P])

        for i, h in repeat(dve, DN_HEADS, 2):
            head = i * 2 + h
            q, grow, beta = self.f[:, h, 0], self.f[:, h, 3], self.f[:, h, 4]

            def column(buf, t):
                return buf[:, t, bass.ds(head, 1)]

            def step(ins, name):
                did.mark(ins, name)

            dve.wait_ge(*self.fetched[h](i * 80 + 80))
            dve.wait_ge(*act(head - 1, "o"))
            for t in range(TT):
                step(v.tensor_scalar(b["decay"][:, tiles[t]], grow[:, tiles[t]], column(g.at["gc"], t), 0.0,
                                     ALU.subtract, ALU.min), f"d{t}")
            dve.wait_ge(*act(head, "decay"))
            step(v.tensor_tensor(tiled(b["decay"]), tiled(b["decay"]), mask(c.prefix[:]), ALU.mult), "decay")
            dve.wait_ge(*did(head, "decay"))
            dve.wait_ge(*pe(head, "kq"))
            step(v.tensor_tensor(b["qkd"], c.psum[:, 1], b["decay"], ALU.mult), "qkd")
            step(v.tensor_tensor(b["lt"], c.psum[:, 0], b["decay"], ALU.mult), "kkd")
            dve.wait_ge(*did(head, "kkd"))
            step(v.tensor_tensor(b["lt"], b["lt"], beta, ALU.mult), "lt")
            dve.wait_ge(*did(head, "lt"))
            step(v.tensor_tensor(tiled(b["ct"]), tiled(b["lt"]), mask(c.levels[:, 0]), ALU.mult), "ct0")
            dve.wait_ge(*did(head, "ct0"))
            step(v.scalar_tensor_tensor(tiled(b["xt"]), tiled(b["ct"]), -1.0, mask(c.ident[:]), ALU.mult, ALU.add), "xt0")
            dve.wait_ge(*act(head, "grow"))
            step(v.tensor_tensor(q, q, b["grow"], ALU.mult), "qd")
            for n in range(1, self.LEVELS):
                dve.wait_ge(*(did(head, "xt0") if n == 1 else pe(head, f"y{n - 1}")))
                step(v.tensor_tensor(tiled(b["ct"]), tiled(b["lt"]), mask(c.levels[:, n]), ALU.mult), f"ct{n}")
                dve.wait_ge(*pe(head, f"zt{n}"))
                if n < self.LEVELS - 1:
                    step(v.tensor_tensor(b["x"], b["x"], c.psum[:, 6], ALU.subtract), f"x{n}")
                step(v.tensor_tensor(b["xt"], b["xt"], c.psum[:, 7], ALU.subtract), f"xt{n}")
            dve.wait_ge(*pe(head, "wt"))
            step(v.tensor_copy(b["wt"], c.psum[:, 5]), "wt")
            state = b["state"][:, :P]
            step(v.memset(state, 0.0), "s0")
            dve.wait_ge(*act(head, "u"))
            for n in range(SEQ // CHUNK):
                t, half = n // 2, n % 2
                rows = slice(half * CHUNK, (half + 1) * CHUNK)
                dve.wait_ge(*pe(head, f"ws{n}"))
                step(v.tensor_tensor(b["vn"][rows, tiles[t]], b["u"][rows, tiles[t]], c.psum[rows, 6, :P],
                                     ALU.subtract), f"vn{n}")
                dve.wait_ge(*pe(head, f"ds{n}"))
                last = g.last[:, half, t, bass.ds(head, 1)]
                step(v.scalar_tensor_tensor(state, state, last, c.psum[:, 5, :P], ALU.mult, ALU.add), f"s_{n}")

    def scalar(self, act, chain):
        c, b, did = self.c, self.b, self.act_did
        pe, dve, g = self.pe_did, self.dve_did, self.g
        tiles = [slice(t * P, (t + 1) * P) for t in range(TT)]
        for i, h in repeat(act, DN_HEADS, 2):
            head = i * 2 + h
            act.wait_ge(*self.fetched[h](i * 80 + 80))
            act.wait_ge(*dve(head, f"d{TT - 1}"))
            did.mark(act.activation(b["decay"], b["decay"], ACT.Exp), "decay")
            did.mark(act.activation(b["grow"], self.f[:, h, 3], ACT.Exp), "grow")
            act.wait_ge(*pe(head, "v_turned"))
            for t in range(TT):
                for name, bank, by in (("kbg", 2, "beg"), ("kd", 2, "dk"), ("vb", 3, "beta")):
                    did.mark(act.activation(b[name][:, tiles[t]], c.psum[:, bank, tiles[t]], ACT.Copy,
                                            scale=g.at[by][:, t, bass.ds(head, 1)]), f"{name}{t}")
            act.wait_ge(*pe(head, "x0"))
            did.mark(act.copy(b["x"], c.psum[:, 4]), "x0")
            for n in range(1, self.LEVELS):
                act.wait_ge(*pe(head, f"y{n}"))
                did.mark(act.copy(b["y"], c.psum[:, 5]), f"y{n}")
            act.wait_ge(*pe(head, "u"))
            did.mark(act.copy(b["u"], c.psum[:, 4]), "u")
            act.wait_ge(*pe(head, f"ds{SEQ // CHUNK - 1}"))
            did.mark(act.copy(at(self.out, head), c.psum[:, 7]), "o")


class Gate(Stage):

    def __init__(self, c, out, gate):
        self.c, self.out, self.gate = c, out, gate
        self.val_ready, self.hi_done, self.lo_done = (c.count(n, KT) for n in ("val_ready", "hi_done", "lo_done"))

    def scalar(self, act, chain):
        for k in range(KT):
            act.wait_ge(*self.val_ready(k + 1))
            act.copy(self.c.h_hi[:, k], self.out[:, k]).then_inc(self.hi_done.sem, 1)

    def vector(self, dve, chain):
        c, v = self.c, self.c.nc.vector
        for k in range(KT + 1):
            if k < KT:
                v.tensor_tensor(self.out[:, k], self.out[:, k], self.gate[:, k], ALU.mult).then_inc(self.val_ready.sem, 1)
            if k > 0:
                dve.wait_ge(*self.hi_done(k))
                v.tensor_tensor(c.h_lo[:, k - 1], self.out[:, k - 1], c.h_hi[:, k - 1],
                                ALU.subtract).then_inc(self.lo_done.sem, 1)


class Attention(Stage):
    BODY_HEADS = 4
    LAG = 5

    def __init__(self, c, heads, fetch, dmas, dst, groups=1, small=(None,), masks=None, select=None, gates=None,
                 block_mask=False, direct=None):
        self.direct = direct
        self.c, self.heads, self.fetch, self.dst, self.groups = c, heads, fetch, dst, groups
        self.small = small
        self.passes = len(small)
        self.masks, self.select, self.gates, self.block_mask = masks, select, gates, block_mask
        self.dmas = dmas
        self.body = self.BODY_HEADS * self.passes
        self.bodies = heads // self.BODY_HEADS
        self.rows = self.body * TT
        self.banks = 2 if groups == 1 else 3
        self.bias = c.take(2 * groups, SEQ)
        if direct is None:
            self.q, self.k = c.take(2 * groups, SEQ), c.take(2 * groups, SEQ)
            self.v = c.take(2 * groups, TT * HEAD_DIM)
            self.s = c.take(2 * groups, SEQ)
            self.pt = c.take(2 * groups, SEQ)
            self.pair = c.take(2, TT, P)
        else:
            self.s, self.pt = c.h_words[:, :2 * groups], c.h_words[:, 2 * groups:4 * groups]
            self.pair = c.h_words[:, 4 * groups:4 * groups + 2].rearrange("p a (t n) -> p a t n", t=TT)
        self.peak, self.shift = c.take(2, 4), c.take(2, 4)
        self.sums, self.scale = c.take(TT, 4), c.take(3, 4)
        self.both = c.take(2, SEQ) if select is not None else None
        n, r = self.bodies * self.rows, c.count
        self.fetched = [r(f"fetched_{b}", 16 * self.transfers(b, self.bodies * self.body)) for b in range(2)]
        self.scores_ready, self.scores_read = r("scores_ready", n * groups), r("scores_read", n * groups + self.banks)
        self.max_ready, self.probs_ready = r("max_ready", n), r("probs_ready", n * groups)
        self.turned, self.turned_read = r("turned", (n + 2) * groups), r("turned_read", n * groups + 2)
        self.attended, self.row_done = r("attended", n + 2), r("row_done", n + 2 * TT)
        self.pair_turned, self.pair_hi = r("pair_turned", heads // 2 + 2), r("pair_hi", heads // 2)
        self.pair_lo = r("pair_lo", heads // 2 + 1)

    def transfers(self, parity, rounds):
        return sum(self.dmas[r % self.passes] * self.groups for r in range(rounds) if r % 2 == parity)

    def fetched_value(self, i, r):
        return self.fetched[r % 2](i * (16 * self.transfers(r % 2, self.body)) + 16 * self.transfers(r % 2, r + 1))

    def width(self, row):
        return self.small[row // TT % self.passes] or P * (row % TT + 1)

    def blocks(self, row):
        w = self.width(row)
        return [(a, min(P, w - a)) for a in range(0, w, P)]

    def ends_pair(self, row):
        return 0 <= row < self.rows and (row + 1) % (2 * self.passes * TT) == 0

    def buffer(self, row, g):
        return row // TT % 2 * self.groups + g

    def operands(self, row, g):
        if self.direct is not None:
            return self.direct(row // TT, g)
        b = self.buffer(row, g)
        return (self.q[:HEAD_DIM, b], self.k[:HEAD_DIM, b],
                lambda j: self.v[:, b, j * HEAD_DIM:(j + 1) * HEAD_DIM])

    def gpsimd(self, pool, chain):
        c = self.c
        for i, _ in repeat(pool, self.bodies, 1):
            for r in range(self.body):
                pool.wait_ge(*self.row_done(i * self.rows + (r + 1) * TT))
                pool.sem_inc(c.passed[1], 1)
                for g in range(self.groups):
                    moves = self.fetch(self, r % 2 * self.groups + g, i, r // self.passes, r % self.passes, g)
                    assert len(moves) == self.dmas[r % self.passes]
                    for to, of in moves:
                        pool.dma_start(to, of).then_inc(self.fetched[r % 2].sem, 16)

    def tensor(self, pe):
        c, G = self.c, self.groups
        for count, n in ((self.scores_read, self.banks), (self.turned, 2 * G), (self.turned_read, 2),
                         (self.attended, 2), (self.row_done, 2 * TT), (self.pair_turned, 2), (self.pair_lo, 1)):
            pe.sem_inc(count.sem, n)
        for i, _ in repeat(pe, self.bodies, 1):
            for s in range(self.rows + self.LAG):
                if s < self.rows:
                    row, w = s, self.width(s)
                    if row % TT == 0:
                        pe.wait_ge(*self.fetched_value(i, row // TT))
                    for g in range(G):
                        cell = i * (self.rows * G) + row * G + g
                        q, k, _ = self.operands(row, g)
                        pe.wait_ge(*self.scores_read(cell + 1))
                        queries = slice(row % TT * P, (row % TT + 1) * P)
                        pe.matmul(c.psum[:, (row * G + g) % self.banks, :w], q[:, queries], k[:, :w],
                                  start=True, stop=True).then_inc(self.scores_ready.sem, 1)
                if 0 <= s - 1 < self.rows:
                    row = s - 1
                    for g in range(G):
                        cell = i * (self.rows * G) + row * G + g
                        pe.wait_ge(*self.probs_ready(cell + 1))
                        pe.wait_ge(*self.turned_read(cell + 1))
                        for a, n in self.blocks(row):
                            mm = pe.transpose(c.psum[:n, self.banks + (row * G + g) % 2, a:a + P],
                                              self.s[:, row % 2 * G + g, a:a + n], c.ident[:])
                        mm.then_inc(self.turned.sem, 1)
                if 0 <= s - 2 < self.rows:
                    row = s - 2
                    out = c.psum[:, self.banks + 2 + row % 2, :HEAD_DIM]
                    pe.wait_ge(*self.row_done(i * self.rows + row + 2 * TT - 1))
                    for g in range(G):
                        cell = i * (self.rows * G) + row * G + g
                        _, _, v = self.operands(row, g)
                        pe.wait_ge(*self.turned_read(cell + 3))
                        for j, (a, n) in enumerate(self.blocks(row)):
                            mm = pe.matmul(out, self.pt[:n, row % 2 * G + g, a:a + P],
                                           v(j)[:n],
                                           start=(g == 0 and j == 0), stop=(g == G - 1 and a + n == self.width(row)))
                    mm.then_inc(self.attended.sem, 1)
                if self.ends_pair(s - 4):
                    row = s - 4
                    pair = row // (2 * self.passes * TT)
                    pe.wait_ge(*self.row_done(i * self.rows + row + 1 + 2 * TT))
                    pe.wait_ge(*self.pair_lo(i * (self.BODY_HEADS // 2) + pair + 1))
                    for t in range(TT):
                        mm = pe.transpose(c.psum[:, 7, t * P:(t + 1) * P], self.pair[:, pair % 2, t], c.ident[:])
                    mm.then_inc(self.pair_turned.sem, 1)

    def vector(self, dve, chain):
        c, v, G = self.c, self.c.nc.vector, self.groups
        extra = (G > 1) + (self.select is not None) * (TT - 1) / TT + (G > 1) + 1 + (self.gates is not None)
        extra = int(self.rows * extra) + self.block_mask * self.body
        for i, _ in repeat(dve, self.bodies, 1, chain, extra):
            for s in range(self.rows + self.LAG):
                if s < self.rows:
                    row, w, t = s, self.width(s), s % TT
                    ps = row // TT % self.passes
                    if t == 0:
                        dve.wait_ge(*self.fetched_value(i, row // TT))
                        if self.block_mask:
                            chain.step(v.memset(self.bias[:CHUNK, self.buffer(row, 0), SEQ - CHUNK:], MASKED))
                    for g in range(G):
                        cell, b = i * (self.rows * G) + row * G + g, self.buffer(row, g)
                        bias = self.masks[:, t, :w] if self.small[ps] else self.bias[:, b, SEQ - w:]
                        if self.select is not None and t > 0:
                            if g == 0:
                                dve.wait_ge(*self.turned(i * (self.rows * G) + (row + 1) * G))
                            chain.step(v.tensor_tensor(self.both[:, row % 2, :w], bias, self.select[t - 1], ALU.add))
                            bias = self.both[:, row % 2, :w]
                        dve.wait_ge(*self.scores_ready(cell + 1))
                        if g == 0:
                            dve.wait_ge(*self.turned(i * (self.rows * G) + (row + 1) * G))
                        dve.sem_inc(c.passed[0], 1)
                        v.tensor_tensor_reduce(
                            out=self.s[:, row % 2 * G + g, :w], in0=c.psum[:, (row * G + g) % self.banks, :w], in1=bias,
                            scale=1.0, scalar=-3e38, op0=ALU.add, op1=ALU.max,
                            accum_out=self.peak[:, row % 2, g:g + 1]).then_inc(self.scores_read.sem, 1)
                    dve.wait_ge(*self.scores_read(i * (self.rows * G) + (row + 1) * G + self.banks))
                    peak = self.peak[:, row % 2, 0:1]
                    if G > 1:
                        chain.step(v.tensor_reduce(self.peak[:, row % 2, 3:4], self.peak[:, row % 2, :G], AX.X, ALU.max))
                        peak = self.peak[:, row % 2, 3:4]
                    v.tensor_scalar(self.shift[:, row % 2, 0:1], peak, -1.0, None,
                                    ALU.mult).then_inc(self.max_ready.sem, 1)
                if 0 <= s - 2 < self.rows:
                    row, t = s - 2, (s - 2) % TT
                    head, ps = row // TT // self.passes, row // TT % self.passes
                    dve.wait_ge(*self.attended(i * self.rows + row + 3))
                    sums = self.sums[:, t, 0:1]
                    if G > 1:
                        chain.step(v.tensor_reduce(self.sums[:, t, 3:4], self.sums[:, t, :G], AX.X, ALU.add))
                        sums = self.sums[:, t, 3:4]
                    chain.step(v.reciprocal(self.scale[:, 0, row % 2:row % 2 + 1], sums))
                    scale = self.scale[:, 0, row % 2:row % 2 + 1]
                    if self.gates is not None:
                        gate = self.gates[:, t, bass.ds(i * self.body + head * self.passes + ps, 1)]
                        chain.step(v.tensor_tensor(self.scale[:, 1, row % 2:row % 2 + 1], scale, gate, ALU.mult))
                        scale = self.scale[:, 1, row % 2:row % 2 + 1]
                    if head % 2 == 0 and ps == 0 and t == 0:
                        dve.wait_ge(*self.pair_turned(i * (self.BODY_HEADS // 2) + head // 2 + 1))
                    to = self.pair[:, head // 2 % 2, t, head % 2 * HEAD_DIM:(head % 2 + 1) * HEAD_DIM]
                    out = c.psum[:, self.banks + 2 + row % 2, :HEAD_DIM]
                    if ps == 0:
                        ins = v.tensor_scalar(to, out, scale, None, ALU.mult)
                    else:
                        dve.wait_ge(*self.row_done(i * self.rows + row - TT + 1 + 2 * TT))
                        ins = v.scalar_tensor_tensor(to, out, scale, to, ALU.mult, ALU.add)
                    ins.then_inc(self.row_done.sem, 1)
                if self.ends_pair(s - 4):
                    pair = i * (self.BODY_HEADS // 2) + (s - 4) // (2 * self.passes * TT)
                    dve.wait_ge(*self.pair_hi(pair + 1))
                    v.tensor_tensor(at(self.dst[1], pair), c.psum[:, 7], at(self.dst[0], pair),
                                    ALU.subtract).then_inc(self.pair_lo.sem, 1)

    def scalar(self, act, chain):
        c, G = self.c, self.groups
        for i, _ in repeat(act, self.bodies, 1):
            for s in range(self.rows + self.LAG):
                if s < self.rows:
                    row, w, t = s, self.width(s), s % TT
                    act.wait_ge(*self.max_ready(i * self.rows + row + 1))
                    for g in range(G):
                        p = self.s[:, row % 2 * G + g, :w]
                        act.activation(p, p, ACT.Exp, bias=self.shift[:, row % 2, 0:1],
                                       accum_out=self.sums[:, t, g:g + 1]).then_inc(self.probs_ready.sem, 1)
                if 0 <= s - 1 < self.rows:
                    row = s - 1
                    last = self.blocks(row)[-1]
                    act.wait_ge(*self.attended(i * self.rows + row + 1))
                    for g in range(G):
                        cell = i * (self.rows * G) + row * G + g
                        act.wait_ge(*self.turned(cell + 1 + 2 * G))
                        act.copy(self.pt[:last[1], row % 2 * G + g, :last[0] + P],
                                 c.psum[:last[1], self.banks + (row * G + g) % 2, :last[0] + P]
                                 ).then_inc(self.turned_read.sem, 1)
                if self.ends_pair(s - 4):
                    pair = i * (self.BODY_HEADS // 2) + (s - 4) // (2 * self.passes * TT)
                    act.wait_ge(*self.pair_turned(pair + 3))
                    act.copy(at(self.dst[0], pair), c.psum[:, 7]).then_inc(self.pair_hi.sem, 1)


class SplitWindows(Stage):

    def __init__(self, c, tiles, hi, lo):
        self.c, self.tiles, self.hi, self.lo = c, tiles, hi, lo
        self.full = c.take(2, CMP_LEN, CMP_PAD + 2)
        self.cleared, self.copied, self.hi_done = c.count("aux_a", 1), c.count("aux_b", 6), c.count("hi_done", 1)

    def vector(self, dve, chain):
        v, c = self.c.nc.vector, self.c
        v.memset(self.full[:], 0.0).then_inc(self.cleared.sem, 1)
        dve.wait_ge(*self.cleared(1))
        for kind, tile in enumerate(self.tiles):
            by = tile.rearrange("p (n l) -> p l n", l=CMP_STRIDE)
            for j in range(2):
                v.tensor_copy(self.full[:, kind, j * CMP_STRIDE:(j + 1) * CMP_STRIDE, :CMP_N],
                              by[:, :, j:j + CMP_N]).then_inc(self.copied.sem, 1)
            pos = c.cmp_pos[:, kind].unsqueeze(2).broadcast_to([P, CMP_LEN, 2])
            v.tensor_copy(self.full[:, kind, :, CMP_PAD:], pos).then_inc(self.copied.sem, 1)
        dve.wait_ge(*self.hi_done(1))
        v.tensor_tensor(self.lo[:], self.full[:], self.hi[:], ALU.subtract)

    def scalar(self, act, chain):
        act.wait_ge(*self.copied(6))
        act.copy(self.hi[:], self.full[:]).then_inc(self.hi_done.sem, 1)


class Compress(Linear):

    def __init__(self, c, source, keys, values):
        self.keys, self.values = keys, values
        self.sum = c.take(2, CMP_PAD + 2)
        super().__init__(c, 2, source=source, slots=(SLOT_TILES,) * (CMP_LEN // SLOT_TILES), unroll=2)

    def begin(self):
        self.added, self.turned = self.c.count("aux_a", 4), self.c.count("aux_b", 1)

    def out(self, u):
        return self.c.psum[:, u % 2, :CMP_PAD + 2]

    def rhs(self, part, k):
        return part[:, self.kind, k]

    def tensor(self, pe):
        super().tensor(pe)
        pe.wait_ge(*self.added(4))
        pe.transpose(self.c.psum[:CMP_PAD, 2, :P], self.sum[:, 1, :CMP_PAD], self.c.ident[:]).then_inc(self.turned.sem, 1)

    def scalar_tile(self, act, chain, i, u):
        act.wait_ge(*self.done(i, u))
        act.copy(self.sum[:, u], self.out(u)).then_inc(self.bank_read.sem, 1)

    def scalar(self, act, chain):
        super().scalar(act, chain)
        act.wait_ge(*self.turned(1))
        act.copy(self.values[:CMP_PAD], self.c.psum[:CMP_PAD, 2, :P])

    def vector_begin(self, dve, chain):
        self.c.nc.vector.memset(self.keys, 0.0).then_inc(self.added.sem, 1)
        dve.wait_ge(*self.added(1))

    def vector_tile(self, dve, chain, i, u):
        v = self.c.nc.vector
        dve.wait_ge(*self.bank_read(u + 3))
        to = self.keys[:, :CMP_PAD] if u == 0 else self.sum[:, 1, :CMP_PAD]
        v.tensor_scalar(to, self.sum[:, u, :CMP_PAD], self.sum[:, u, CMP_PAD:CMP_PAD + 1], None,
                        ALU.add).then_inc(self.added.sem, 1)
        dve.wait_ge(*self.added(u + 2))
        if u == 1:
            v.memset(self.sum[:, 0], 0.0).then_inc(self.added.sem, 1)


class TopKeys(Stage):

    def __init__(self, c, iq, ik, iw, out):
        self.c, self.iq, self.ik, self.iw, self.out = c, iq, ik, iw, out
        self.rel, self.best = c.take(2, SEQ), c.take(3, 8)
        self.score = c.take(3, SEQ)
        n = (TT - 1) * IDX_HEADS
        self.scored, self.relu_done = c.count("aux_a", n), c.count("aux_b", n + 2)
        self.added = c.count("aux_c", n + 2)

    def tensor(self, pe):
        c = self.c
        pe.sem_inc(self.relu_done.sem, 2)
        pe.sem_inc(self.added.sem, 2)
        for t in range(1, TT):
            for h in range(IDX_HEADS):
                n = (t - 1) * IDX_HEADS + h
                half = slice(h % 2 * HEAD_DIM, (h % 2 + 1) * HEAD_DIM)
                pe.wait_ge(*self.relu_done(n + 1))
                pe.matmul(c.psum[:, n % 2, :(t + 1) * P], self.iq[half, h // 2, t * P:(t + 1) * P],
                          self.ik[half, :(t + 1) * P], start=True, stop=True).then_inc(self.scored.sem, 1)

    def scalar(self, act, chain):
        c = self.c
        for n in range((TT - 1) * IDX_HEADS):
            w = (n // IDX_HEADS + 2) * P
            act.wait_ge(*self.scored(n + 1))
            act.wait_ge(*self.added(n + 1))
            act.activation(self.rel[:, n % 2, :w], c.psum[:, n % 2, :w], ACT.Relu).then_inc(self.relu_done.sem, 1)

    def vector(self, dve, chain):
        c, v = self.c, self.c.nc.vector
        for n in range((TT - 1) * IDX_HEADS):
            t, h = n // IDX_HEADS + 1, n % IDX_HEADS
            w = (t + 1) * P
            dve.wait_ge(*self.relu_done(n + 3))
            score = self.score[:, t - 1, :w]
            before = c.causal[:, SEQ - w:] if h == 0 else score
            v.scalar_tensor_tensor(score, self.rel[:, n % 2, :w], self.iw[:, t, h:h + 1], before, ALU.mult,
                                   ALU.add).then_inc(self.added.sem, 1)
            dve.wait_ge(*self.added(n + 3))
        taken = -3e38
        for _ in range(TOPK // 8):
            for t in range(1, TT):
                chain.mark(v.max(self.best[:, t - 1], self.score[:, t - 1, :(t + 1) * P]))
            chain.wait()
            for t in range(1, TT):
                score = self.score[:, t - 1, :(t + 1) * P]
                chain.mark(v.match_replace(score, self.best[:, t - 1], score, taken))
            chain.wait()
        for t in range(1, TT):
            w = (t + 1) * P
            v.tensor_scalar(self.out[:, t - 1, :w], self.score[:, t - 1, :w], taken, MASKED, ALU.not_equal, ALU.mult)


class SigmoidGates(Stage):

    def __init__(self, c, source, out):
        self.c, self.source, self.out = c, source, out
        self.done = c.count("aux_a", 1)

    def scalar(self, act, chain):
        act.activation(self.out[:], self.source, ACT.Sigmoid).then_inc(self.done.sem, 1)

    def vector(self, dve, chain):
        v = self.c.nc.vector
        dve.wait_ge(*self.done(1))
        gates = self.out[:].rearrange("p t (h k) -> p t h k", k=3)[:, :, :, 0]
        valid = self.c.row_valid[:].unsqueeze(2).broadcast_to([P, TT, 8])
        v.tensor_tensor(gates, gates, valid, ALU.mult)


class Mix(Linear):
    two_banks = False

    def __init__(self, c, branches, dst):
        self.branches, self.dst = branches, dst
        self.gate, self.part = c.take(3, SEQ), c.take(3, SEQ)
        self.tiles_of = [((0, c.h_hi, c.h_lo, 0, KT),), ((1, c.h_hi, c.h_lo, 0, KT),), ((2, c.h_hi, c.h_lo, 0, KT),),
                         ((3, *branches[0], 0, 4), (4, *branches[1], 4, 4)), ((5, *branches[2], 0, 2),)]
        super().__init__(c, KT, slots=(8, 8, 8, 8, 2))

    def begin(self):
        c = self.c
        self.did_act = Steps(c, "aux_a", ("g0", "g1", "g2", "hi"), KT, before=1)
        self.did_dve = Steps(c, "aux_b", ("a", "b", "ab", "c", "abc", "lo"), KT, before=1)

    def tensor(self, pe):
        c = self.c
        self.did_act.begin(pe)
        self.did_dve.begin(pe)
        for i, u in repeat(pe, self.tiles, self.unroll):
            t = i * self.unroll + u
            for j, parts in enumerate(self.tiles_of):
                k0 = self.slot0 + u * self.per + j
                s = k0 % RING
                pe.wait_ge(*(self.did_act(t - 1, f"g{j}") if j < 3 else self.did_dve(t - 1, "b" if j == 3 else "c")))
                pe.wait_ge(c.lo_ready, i * (self.unroll * self.per) + k0 + 1)
                for bank, hi, lo, first, n in parts:
                    for k in range(n):
                        pairs = ((c.w_hi, hi), (c.w_hi, lo), (c.w_lo, hi))
                        for m, (w, x) in enumerate(pairs):
                            mm = pe.matmul(c.psum[:, bank], w[:, s, first + k], x[:, k],
                                           start=(k == 0 and m == 0), stop=(k == n - 1 and m == 2))
                mm.then_inc(c.slot_used, 1)

    def slot_done(self, i, u, j):
        return self.c.slot_used, (i * self.unroll + u) * self.per + j + 1 + self.slot0 + RING

    def scalar(self, act, chain):
        c, did = self.c, self.did_act
        for i, u in repeat(act, self.tiles, self.unroll):
            t = i * self.unroll + u
            for j in range(self.per):
                c.split_hi(act, i, self.unroll * self.per, self.slot0 + u * self.per + j + AHEAD)
                if j < 3:
                    act.wait_ge(*self.slot_done(i, u, j))
                    act.wait_ge(*self.did_dve(t - 1, ("a", "b", "c")[j]))
                    did.mark(act.activation(self.gate[:, j], c.psum[:, j], ACT.Sigmoid), f"g{j}")
            act.wait_ge(*self.did_dve(t, "abc"))
            did.mark(act.copy(at(self.dst[0], t), self.part[:, 0]), "hi")

    def vector(self, dve, chain):
        c, v, did = self.c, self.c.nc.vector, self.did_dve
        for i, u in repeat(dve, self.tiles, self.unroll):
            t = i * self.unroll + u
            gate, part = self.gate, self.part
            for j in range(self.per):
                c.split_lo(dve, i, self.unroll * self.per, self.slot0 + u * self.per + j + AHEAD)
                if j == 3:
                    dve.wait_ge(*self.slot_done(i, u, 3))
                    dve.wait_ge(*self.did_act(t, "g1"))
                    did_lo = did(t - 1, "lo")
                    dve.wait_ge(*did_lo)
                    did.mark(v.tensor_tensor(part[:, 0], gate[:, 0], c.psum[:, 3], ALU.mult), "a")
                    did.mark(v.tensor_tensor(part[:, 1], gate[:, 1], c.psum[:, 4], ALU.mult), "b")
                    dve.wait_ge(*did(t, "b"))
                    did.mark(v.tensor_tensor(part[:, 0], part[:, 0], part[:, 1], ALU.add), "ab")
            dve.wait_ge(*self.slot_done(i, u, 4))
            dve.wait_ge(*self.did_act(t, "g2"))
            did.mark(v.tensor_tensor(part[:, 2], gate[:, 2], c.psum[:, 5], ALU.mult), "c")
            dve.wait_ge(*did(t, "c"))
            did.mark(v.tensor_tensor(part[:, 0], part[:, 0], part[:, 2], ALU.add), "abc")
            dve.wait_ge(*self.did_act(t, "hi"))
            did.mark(v.tensor_tensor(at(self.dst[1], t), part[:, 0], at(self.dst[0], t), ALU.subtract), "lo")


class SwiGlu(Linear):
    two_banks = False

    def __init__(self, c, tiles, dst):
        self.dst = dst
        super().__init__(c, tiles, slots=(SLOT_TILES, SLOT_TILES), unroll=2)

    def begin(self):
        c = self.c
        self.did_act = Steps(c, "aux_a", ("silu", "hi"), self.tiles, before=2)
        self.did_dve = Steps(c, "aux_b", ("value", "lo"), self.tiles, before=2)

    def tensor(self, pe):
        c = self.c
        self.did_act.begin(pe)
        self.did_dve.begin(pe)
        for i, u in repeat(pe, self.tiles, self.unroll):
            t = i * self.unroll + u
            for j in range(2):
                k0 = self.slot0 + u * self.per + j
                s = k0 % RING
                pe.wait_ge(*(self.did_act(t - 2, "silu") if j == 0 else self.did_dve(t - 2, "value")))
                pe.wait_ge(c.lo_ready, i * (self.unroll * self.per) + k0 + 1)
                for k in range(KT):
                    pairs = ((c.w_hi, c.h_hi), (c.w_hi, c.h_lo), (c.w_lo, c.h_hi))
                    for n, (w, x) in enumerate(pairs):
                        mm = pe.matmul(c.psum[:, u % 2 * 2 + j], w[:, s, k], x[:, k], start=(k == 0 and n == 0),
                                       stop=(k == KT - 1 and n == 2))
                mm.then_inc(c.slot_used, 1)

    def scalar_tile(self, act, chain, i, u):
        c, t = self.c, i * self.unroll + u
        act.wait_ge(c.slot_used, t * self.per + 1 + self.slot0 + RING)
        act.wait_ge(*self.did_dve(t - 2, "value"))
        self.did_act.mark(act.activation(c.tmp[:, u % 2], c.psum[:, u % 2 * 2], ACT.Silu), "silu")
        act.wait_ge(*self.did_dve(t, "value"))
        self.did_act.mark(act.copy(at(self.dst[0], t), c.sq[:, u % 2]), "hi")

    def vector_tile(self, dve, chain, i, u):
        c, t, v = self.c, i * self.unroll + u, self.c.nc.vector
        dve.wait_ge(*self.done(i, u))
        dve.wait_ge(*self.did_act(t, "silu"))
        dve.wait_ge(*self.did_dve(t - 2, "lo"))
        self.did_dve.mark(v.tensor_tensor(c.sq[:, u % 2], c.tmp[:, u % 2], c.psum[:, u % 2 * 2 + 1], ALU.mult), "value")
        dve.wait_ge(*self.did_act(t, "hi"))
        self.did_dve.mark(v.tensor_tensor(at(self.dst[1], t), c.sq[:, u % 2], at(self.dst[0], t), ALU.subtract), "lo")


def build_stages(c, upto=None):
    io = c.io

    def fresh():
        c.used = 0

    def mlp(index):
        c.used = 0
        hidden = c.take_parts(FF_HALF, SEQ)
        st = [Norm(c, index)]
        for _ in range(2):
            st.append(ReluSquare(c, FF_HALF, hidden))
            st.append(Residual(c, source=hidden, slots=(SLOT_TILES,) * (FF_HALF // SLOT_TILES)))
        return st

    st = [Load(c), Norm(c, 0)]
    q, k, v = c.take(KT, SEQ), c.take(KT, SEQ), c.take(TT, D)
    st += [Project(c, KT, q, scale=HEAD_DIM ** -0.5), Project(c, KT, k), Project(c, KT, v, token_major=True)]

    def fetch(a, b, i, head, ps, g):
        half, pair = head % 2 * HEAD_DIM, head // 2
        tile = bass.ds(i * 2 + pair, 1)
        return [(a.q[:HEAD_DIM, b], q[half:half + HEAD_DIM, tile].rearrange("p o n -> p (o n)")),
                (a.k[:HEAD_DIM, b], k[half:half + HEAD_DIM, tile].rearrange("p o n -> p (o n)")),
                (a.v[:, b].rearrange("p (t n) -> p t n", t=TT),
                 v[:, :, bass.ds(i * (4 * HEAD_DIM) + head * HEAD_DIM, HEAD_DIM)]),
                (a.bias[:, b], io["rel"][bass.ds(i * 4 + head, 1)].rearrange("o p n -> p (o n)"))]

    st += [Attention(c, ATTN_HEADS, fetch, (4,), (c.h_hi, c.h_lo), block_mask=True)]
    st += [Residual(c)] + mlp(1)
    c.used = 0
    qkv, z, ab = c.take(3 * KT, SEQ), c.take(KT, SEQ), c.take(TT, 2 * DN_HEADS)
    mark = c.used
    st += [Norm(c, 2), ConvProject(c, 3 * KT, qkv), Project(c, KT, z, func=ACT.Silu),
           Project(c, 1, ab, token_major=True, cols=2 * DN_HEADS)]
    c.used = mark
    for part, scale in ((0, DN_HEAD_DIM ** -0.5), (1, 1.0)):
        st += [HeadNorm(c, [qkv[:, part * KT + k] for k in range(KT)], scale=scale)]
        c.used = mark
    gates = DnGates(c, ab)
    st += [gates, DeltaRule(c, qkv, gates, qkv)]
    c.used = mark
    st += [HeadNorm(c, [qkv[:, k] for k in range(KT)], n=DN_HEAD_DIM, gains=[c.dn_small[:, 2, :1]] * KT),
           Gate(c, qkv, z), Residual(c)] + mlp(3)
    st += [Norm(c, 4, keep=True)]

    c.used = 0
    out_a, out_b = c.take_parts(4, SEQ), c.take_parts(4, SEQ)
    mark = c.used
    scale = HEAD_DIM ** -0.5
    gain = [c.gains[:, k:k + 1] for k in range(6)]

    a_tiles, a_tokens, select = c.take(8, SEQ), c.take(TT, P), c.take(3, SEQ)
    inner = c.used
    st += [Norm(c, 5), Project(c, 8, a_tiles), Project(c, 1, a_tokens, token_major=True)]
    st += [HeadNorm(c, [a_tiles[:, k] for k in range(4)], per=2, n=HEAD_DIM, scale=scale, gains=[gain[0]] * 4)]
    c.used = inner
    st += [HeadNorm(c, [a_tiles[:, 4]], per=2, n=HEAD_DIM, gains=[gain[1]])]
    c.used = inner
    st += [TopKeys(c, a_tiles[:, 5:7], a_tiles[:, 7], a_tokens[:, :, HEAD_DIM:HEAD_DIM + IDX_HEADS], select)]
    c.used = inner

    def fetch_a(a, b, i, head, ps, g):
        half = head % 2 * HEAD_DIM
        q = a_tiles[half:half + HEAD_DIM, bass.ds(i * 2 + head // 2, 1)].rearrange("p o n -> p (o n)")
        return [(a.q[:HEAD_DIM, b], q), (a.k[:HEAD_DIM, b], a_tiles[:HEAD_DIM, 4]),
                (a.v[:, b].rearrange("p (t n) -> p t n", t=TT), a_tokens[:, :, :HEAD_DIM]),
                (a.bias[:, b], io["rel_2"][bass.ds(i * 4 + head, 1)].rearrange("o p n -> p (o n)"))]

    widths = [select[:, t - 1, :(t + 1) * P] for t in range(1, TT)]
    st += [Attention(c, 8, fetch_a, (4,), out_a, select=widths)]

    c.used = mark
    b_tiles, b_tokens, keys_cmp = c.take(8, SEQ), c.take(TT, 3 * P), c.take(SEQ)
    values_cmp, gates_b = c.take(P), c.take(TT, 24)
    inner = c.used
    cmp_hi, cmp_lo = c.take_parts(2, CMP_LEN, CMP_PAD + 2)
    st += [Project(c, 8, b_tiles), Project(c, 3, b_tokens, token_major=True),
           SplitWindows(c, [b_tiles[:, 4], b_tiles[:, 5]], cmp_hi, cmp_lo),
           Compress(c, (cmp_hi, cmp_lo), keys_cmp[:], values_cmp)]
    c.used = inner
    st += [HeadNorm(c, [b_tiles[:, k] for k in range(4)], per=2, n=HEAD_DIM, scale=scale, gains=[gain[2]] * 4)]
    c.used = inner
    st += [HeadNorm(c, [b_tiles[:, 6], b_tiles[:, 7], keys_cmp[:]], per=2, n=HEAD_DIM, gains=[gain[3]] * 3)]
    c.used = inner
    st += [SigmoidGates(c, b_tokens[:, :, :24], gates_b)]

    def fetch_b(a, b, i, head, ps, g):
        group, pair = head % 2, i * 2 + head // 2
        half = slice(group * HEAD_DIM, (group + 1) * HEAD_DIM)
        q = (a.q[:HEAD_DIM, b], b_tiles[half, bass.ds(pair, 1)].rearrange("p o n -> p (o n)"))
        if ps == 0:
            return [q, (a.k[:HEAD_DIM, b, :CMP_PAD], keys_cmp[half, :CMP_PAD]),
                    (a.v[:CMP_PAD, b, :HEAD_DIM], values_cmp[:CMP_PAD, half])]
        cols = slice(ps * P + group * HEAD_DIM, ps * P + (group + 1) * HEAD_DIM)
        rel = io["rel_2"][bass.ds(pair + (8 + 4 * group), 1)].rearrange("o p n -> p (o n)")
        return [q, (a.k[:HEAD_DIM, b], b_tiles[half, 5 + ps]),
                (a.v[:, b].rearrange("p (t n) -> p t n", t=TT), b_tokens[:, :, cols]), (a.bias[:, b], rel)]

    st += [Attention(c, 8, fetch_b, (3, 4, 4), out_b, small=(CMP_PAD, None, None), masks=c.cmp_mask, gates=gates_b)]

    c.used = mark
    out_c = c.take_parts(2, SEQ)
    inner = c.used
    c_q, c_k, c_v = c.take(6, SEQ), c.take(6, SEQ), c.take(TT, 6 * P)
    rest = c.used
    st += [Project(c, 6, c_q), Project(c, 6, c_k), Project(c, 6, c_v, token_major=True)]
    st += [HeadNorm(c, [c_q[:, k] for k in range(6)], per=2, n=HEAD_DIM, scale=scale, gains=[gain[4]] * 6)]
    c.used = rest
    st += [HeadNorm(c, [c_k[:, k] for k in range(6)], per=2, n=HEAD_DIM, gains=[gain[5]] * 6)]
    c.used = rest

    def direct_c(head, g):
        half, tile = slice(head % 2 * HEAD_DIM, (head % 2 + 1) * HEAD_DIM), g * 2 + head // 2
        col = (g * 4 + head) * HEAD_DIM
        return c_q[half, tile], c_k[half, tile], lambda j: c_v[:, j, col:col + HEAD_DIM]

    def fetch_c(a, b, i, head, ps, g):
        return [(a.bias[:, b], io["rel_2"][16 + g * 4 + head])]

    st += [Attention(c, 4, fetch_c, (1,), out_c, groups=3, direct=direct_c)]

    c.used = inner
    mixed = c.take_parts(KT, SEQ)
    st += [Norm(c, 5), Mix(c, (out_a, out_b, out_c), mixed), Residual(c, source=mixed), Norm(c, 6)]
    c.used = 0
    hidden = c.take_parts(FF2, SEQ)
    st += [SwiGlu(c, FF2, hidden), Residual(c, source=hidden, slots=(SLOT_TILES, SLOT_TILES, FF2 - 2 * SLOT_TILES))]
    return st[:upto]


def program(nc, io, upto=None, dump=()):
    ctx = ExitStack()
    with ctx:
        c = Core(nc, ctx, io)
        stages = build_stages(c, upto)
        slots = sum(s.tiles * s.per for s in stages if isinstance(s, Linear)) + AHEAD
        consts = io["consts"]
        loads = [(c.x[:], io["x"]), (c.norm_w[:], io["norms"]), (c.conv_w[:], io["conv"]),
                 (c.dn_small[:], io["dn_small"]), (c.ones[:], consts[:, 0]), (c.ident[:], consts[:, 1]),
                 (c.prefix[:], consts[:, 2]), (c.chunks[:], consts[:, 3]), (c.first[:], consts[:, 4:6]),
                 (c.levels[:], consts[:, 6:12]), (c.halves[:], io["halves"])]
        loads += [(c.causal[:], io["causal"]), (c.gains[:], io["gains"]), (c.cmp_pos[:], io["cmp_pos"]),
                  (c.cmp_mask[:], io["cmp_mask"]), (c.row_valid[:], io["row_valid"])]
        c.n_loads = len(loads)
        block = ctx.enter_context(nc.Block())

        def stage_end(eng, n):
            eng.drain().then_inc(c.all_done, 1)
            eng.wait_ge(c.all_done, 4 * (n + 1))

        @block.sync
        def _(sp):
            for dst, src in loads:
                sp.dma_start(dst, src).then_inc(c.loaded, 16)
            def load(n, s):
                src = io["stream"][n if isinstance(n, int) else bass.ds(n, 1)]
                src = src.rearrange("p (k n) -> p k n", n=P) if isinstance(n, int) else \
                    src.rearrange("o p (k n) -> p (o k) n", n=P)
                sp.dma_start(c.w_raw[:, s], src).then_inc(c.raw_loaded[s], 16)
            for n in range(RING):
                load(n, n)
            with sp.Fori(1, slots // RING) as i:
                for s in range(RING):
                    sp.wait_ge(c.lo_ready, i * RING + s - RING + 1)
                    load(i * RING + s, s)
            for n in range(slots // RING * RING, slots):
                sp.wait_ge(c.lo_ready, n - RING + 1)
                load(n, n % RING)
            sp.wait_ge(c.all_done, 4 * len(stages))
            if upto is None:
                sp.dma_start(io["out"], c.x[:]).then_inc(c.stored, 16)
                sp.wait_ge(c.stored, 16)
            for n, what in enumerate(dump):
                sp.dma_start(io[f"dump{n}"], what(c, stages)).then_inc(c.stored, 16)
                sp.wait_ge(c.stored, 16 * (n + 1))

        @block.tensor
        def _(pe):
            pe.wait_ge(c.loaded, 16 * c.n_loads)
            for n, stage in enumerate(stages):
                stage.tensor(pe)
                stage_end(pe, n)

        @block.vector
        def _(dve):
            chain = Chain(dve, c.chains[1])
            dve.wait_ge(c.loaded, 16 * c.n_loads)
            for n, stage in enumerate(stages):
                stage.vector(dve, chain)
                stage_end(dve, n)

        @block.scalar
        def _(act):
            chain = Chain(act, c.chains[0])
            for n, stage in enumerate(stages):
                stage.scalar(act, chain)
                stage_end(act, n)

        @block.gpsimd
        def _(pool):
            chain = Chain(pool, c.chains[2])
            for n, stage in enumerate(stages):
                stage.gpsimd(pool, chain)
                stage_end(pool, n)


def tiles(w, per=None):
    rows, cols = w.shape
    k, n = rows // P, -(-cols // P)
    w = np.pad(w, ((0, 0), (0, n * P - cols)))
    per = per or -(-k // SLOT_TILES)
    w = w.reshape(k, P, n, P).transpose(2, 1, 0, 3)
    w = np.pad(w, ((0, 0), (0, 0), (0, per * SLOT_TILES - k), (0, 0)))
    return w.reshape(n, P, per, SLOT_TILES * P).transpose(0, 2, 1, 3).reshape(n * per, P, SLOT_TILES * P)


def channels(v):
    return np.moveaxis(v.reshape(*v.shape[:-1], -1, P), -1, 0)


def toeplitz(rows):
    return rows[:, np.arange(SEQ)[None] + (P - 1 - np.arange(P))[:, None]]


def bucket(dist):
    n, exact = np.maximum(dist, 0), REL_BUCKETS // 2
    large = exact + (np.log(np.maximum(n, 1).astype(np.float32) / np.float32(exact))
                     / np.float32(math.log(REL_MAX_DIST / exact)) * np.float32(REL_BUCKETS - exact)).astype(np.int32)
    return np.where(n < exact, n, np.minimum(large, REL_BUCKETS - 1))


def second_stream(a):
    w = a["w_in_2"][0]
    sizes = (512, 64, 64, 256, 64, 4, 512, 768, 24, 2304, 3072)
    a_q, a_k, a_v, i_q, i_k, i_w, b_q, b_kv, b_g, c_qkv, mix = np.split(w, np.cumsum(sizes)[:-1], axis=1)
    order = [p + 4 * g for p in range(4) for g in range(2)]
    heads = lambda m, n: m.reshape(D, 8, n)[:, order].reshape(D, 8 * n)
    kc, vc, ks, vs, kw, vw = np.split(b_kv, 6, axis=1)
    pad = lambda m: np.pad(m, ((0, 0), (0, P - m.shape[1])))
    c_q, c_k, c_v = np.split(c_qkv, 3, axis=1)
    stream = []
    stream.append(tiles(np.concatenate([a_q, a_k, a_k, i_q, i_k, i_k], axis=1)))
    stream.append(tiles(pad(np.concatenate([a_v, i_w], axis=1))))
    stream.append(tiles(np.concatenate([heads(b_q, HEAD_DIM), kc, vc, ks, kw, pad(heads(b_g, 3)), vs, vw], axis=1)))
    cmp = a["nsa_cmp_w_2"][0]
    both = np.zeros((2, CMP_LEN, 2, HEAD_DIM, 2, HEAD_DIM), np.float32)
    both[:, :, 0, :, 0], both[:, :, 1, :, 1] = cmp, cmp
    for kind in both.reshape(2, CMP_LEN * P, P):
        stream.append(tiles(kind))
    stream.append(tiles(np.concatenate([c_q, c_k, c_v], axis=1)))
    rows = np.concatenate([np.r_[h * HEAD_DIM:(h + 1) * HEAD_DIM] for h in order])
    branch_ab = tiles(np.concatenate([a["w_branch_a_2"][0], a["w_branch_b_2"][0][rows]], axis=0))
    branch_c = tiles(a["w_branch_c_2"][0])
    gate = tiles(mix).reshape(3, KT, P, SLOT_TILES * P)
    mixed = np.stack([*gate, branch_ab, branch_c], axis=1)
    gate, up = (tiles(m) for m in np.split(a["w_ffn_in_2"][0], 2, axis=1))
    stream += [mixed.reshape(-1, P, SLOT_TILES * P), tiles(a["w_out_2"][0])]
    stream += [np.stack([gate, up], axis=1).reshape(-1, P, SLOT_TILES * P), tiles(a["w_ffn_out_2"][0])]
    return stream


def lay_out(a):
    rel = a["attn_rel_bias"][0][:, ::-1]
    rel = np.concatenate([np.repeat(rel[:, :1], SEQ - 1 - MAX_REL, axis=1), rel[:, :MAX_REL + P]], axis=1)
    half = D_FF // 2

    def mlp(i):
        up, down = a["mlp_w_up"][i], a["mlp_w_down"][i]
        return [tiles(up[:, :half]), tiles(down[:half]), tiles(up[:, half:]), tiles(down[half:])]

    stream = [tiles(a["attn_w_qkv"][0]), tiles(a["attn_w_o"][0]), *mlp(0),
              tiles(a["dn_w_in"][0]), tiles(a["dn_w_o"][0]), *mlp(1)]
    stream += second_stream(a)
    stream.append(np.zeros((AHEAD, P, SLOT_TILES * P), np.float32))
    norms = np.stack([a["attn_norm"][0], a["mlp_norm"][0], a["dn_norm"][0], a["mlp_norm"][1], a["final_norm"],
                      a["norm1_g_2"][0], a["norm2_g_2"][0], a["norm2_g_2"][0]])
    m, i = np.arange(P)[:, None], np.arange(P)[None]
    level = [(m >> n + 1 == i >> n + 1) & (m >> n & 1 == 0) & (i >> n & 1 == 1) for n in range(6)]
    consts = [m >= 0 * i, m == i, (m <= i) & (m // CHUNK == i // CHUNK), m // CHUNK == i // CHUNK,
              m + 0 * i < CHUNK, m + 0 * i >= CHUNK, *level]
    conv = a["dn_conv_w"][0]
    spread = lambda row: np.broadcast_to(row, (P, DN_HEADS))
    head_norm = np.broadcast_to(a["dn_head_norm"][0][:, None], (P, DN_HEADS))
    dist = np.arange(SEQ - 1, -P, -1)
    table = a["rel_bias_2"][bucket(dist)].T
    win = ((P, 1), (4 * P, 4), (16 * P, 16))
    seen = np.stack([dist >= 0] * 16 + [(dist >= 0) & (dist <= w) & (dist % d == 0) for w, d in win for _ in range(4)])
    rel_2 = np.where(seen, table, np.float32(MASKED))
    token = np.arange(TT)[None, :, None] * P + np.arange(P)[:, None, None]
    window = np.arange(CMP_PAD)[None, None]
    cmp_seen = (window * CMP_STRIDE + CMP_LEN - 1 <= token) & (window < CMP_N)
    twice = lambda v: np.concatenate([v, v], axis=-1)
    return {
        "rel_2": toeplitz(rel_2), "causal": toeplitz(np.where(dist >= 0, 0, MASKED).astype(np.float32)[None])[0],
        "gains": twice(a["qk_norm_g_2"][0]).T, "cmp_pos": twice(a["nsa_cmp_pos_2"][0]).transpose(2, 0, 1),
        "cmp_mask": np.where(cmp_seen, 0, MASKED).astype(np.float32),
        "row_valid": cmp_seen.any(axis=2).astype(np.float32),
        "rel": toeplitz(rel), "x": channels(a["x"][0]).transpose(0, 2, 1), "norms": channels(norms), 
        "consts": np.stack(consts, axis=1).astype(np.float32), "conv": channels(conv).transpose(0, 2, 1),
        "halves": (m // CHUNK == np.arange(2)[None]).astype(np.float32),
        "dn_small": np.stack([spread(a["dn_a_log"][0]), spread(a["dn_dt_bias"][0]), head_norm], axis=1),
        "stream": np.concatenate(stream),
    }


def kernel(**inputs):
    import concourse.bacc as bacc
    from concourse.bass_utils import run_bass_kernel_spmd

    nc = bacc.Bacc("TRN2", target_bir_lowering=False, num_devices=1)
    arrays = {f"in_{k}": np.ascontiguousarray(v) for k, v in lay_out({k: np.asarray(v) for k, v in inputs.items()}).items()}
    io = {k[3:]: nc.dram_tensor(k, v.shape, F32, kind="ExternalInput").ap() for k, v in arrays.items()}
    io["out"] = nc.dram_tensor("out", (P, KT, SEQ), F32, kind="ExternalOutput").ap()
    program(nc, io)
    out = run_bass_kernel_spmd(nc, [arrays], core_ids=[0]).results[0]["out"]
    return out.transpose(2, 1, 0).reshape(1, SEQ, D)
```

```python
import math
from contextlib import ExitStack

import numpy as np
import concourse.bass as bass
from concourse import mybir

P = 128
F32 = mybir.dt.float32
F32R = mybir.dt.float32r
ALU = mybir.AluOpType
ACT = mybir.ActivationFunctionType
AX = mybir.AxisListType

SEQ, D = 512, 1024
KT = D // P
TT = SEQ // P
EPS = 1e-6
MASKED = -1e30
ATTN_HEADS, HEAD_DIM, MAX_REL = 16, 64, 256
CHUNK = 64
DN_HEADS, DN_HEAD_DIM = 8, 128
D_FF = 4 * D
FF_HALF = D_FF // P // 2
D_FF_2 = 2816
FF2 = D_FF_2 // P
CMP_LEN, CMP_STRIDE, CMP_PAD = 32, 16, 32
CMP_N = (SEQ - CMP_LEN) // CMP_STRIDE + 1
IDX_HEADS, TOPK = 4, 128
REL_BUCKETS, REL_MAX_DIST = 32, 2048
TOEPLITZ = SEQ + P - 1

RING = 4
AHEAD = 2
SLOT_TILES = 8


class Count:

    def __init__(self, sem, base):
        self.sem, self.base = sem, base

    def __call__(self, n):
        return self.sem, self.base + n


class Signal:

    def __init__(self, nc, name):
        self.sem, self.used = nc.alloc_semaphore(name), 0

    def reserve(self, total):
        self.used += total
        return Count(self.sem, self.used - total)


class Chain:

    def __init__(self, eng, sem):
        self.eng, self.sem = eng, sem
        self.start, self.turn, self.marks, self.local = 0, 0, 0, 0

    def mark(self, instruction):
        self.local += 1
        instruction.then_inc(self.sem, 1)

    def wait(self):
        self.eng.wait_ge(self.sem, self.turn * self.marks + self.start + self.local)

    def step(self, instruction):
        self.mark(instruction)
        self.wait()


def repeat(eng, n, unroll, chain=None, marks=0):
    whole = n // unroll

    def turn(i, u):
        if chain is not None:
            chain.start += chain.local
            chain.local = 0
            chain.turn, chain.marks = i * unroll + u, marks
        return i, u

    def ended():
        if chain is not None:
            assert chain.local == marks, (chain.local, marks)
            chain.local = 0

    if chain is not None:
        chain.start += chain.local
        chain.local = 0
    if whole > 1:
        with eng.Fori(0, whole) as i:
            for u in range(unroll):
                yield turn(i, u)
                ended()
    elif whole == 1:
        for u in range(unroll):
            yield turn(0, u)
            ended()
    for u in range(n - whole * unroll):
        yield turn(whole, u)
        ended()
    if chain is not None:
        chain.start += n * marks
        chain.turn, chain.marks = 0, 0


def at(buf, t):
    if isinstance(t, int):
        return buf[:, t]
    return buf[:, bass.ds(t, 1)].rearrange("p o n -> p (o n)")


class Core:

    def __init__(self, nc, ctx, io):
        self.nc, self.io = nc, io

        def sb(name, shape, dt=F32):
            return ctx.enter_context(nc.sbuf_tensor(name, shape, dt))

        self.w_raw = sb("w_raw", [P, RING, SLOT_TILES, P])
        self.w_hi = sb("w_hi", [P, RING, SLOT_TILES, P], F32R)
        self.w_lo = sb("w_lo", [P, RING, SLOT_TILES, P], F32R)
        self.x = sb("x", [P, KT, SEQ])
        start = -(-nc.sbuf_base // 64) * 64
        self.h_hi = sb("h_hi", [P, KT, SEQ], F32R)
        self.h_lo = sb("h_lo", [P, KT, SEQ], F32R)
        self.h_words = nc.alloc_sbuf_tensor_at("h_words", [P, 2 * KT, SEQ], F32, offset=start)
        self.ssq = sb("ssq", [P, SEQ])
        self.sq = sb("sq", [P, 2, SEQ])
        self.tmp = sb("tmp", [P, 2, SEQ])
        self.rstd = sb("rstd", [P, SEQ])
        self.norm_w = sb("norm_w", [P, 8, KT])
        self.ones = sb("ones", [P, P])
        self.ident = sb("ident", [P, P])
        self.halves = sb("halves", [P, 2])
        self.prefix = sb("prefix", [P, P])
        self.chunks = sb("chunks", [P, P])
        self.first = sb("first", [P, 2, P])
        self.levels = sb("levels", [P, 6, P])
        self.conv_w = sb("conv_w", [P, 3 * KT, 4])
        self.causal = sb("causal", [P, SEQ])
        self.gains = sb("gains", [P, 6])
        self.cmp_pos = sb("cmp_pos", [P, 2, CMP_LEN])
        self.cmp_mask = sb("cmp_mask", [P, TT, CMP_PAD])
        self.row_valid = sb("row_valid", [P, TT])
        self.dn_small = sb("dn_small", [P, 3, DN_HEADS])
        self.arena, self.used, self.named = -(-nc.sbuf_base // 64) * 64, 0, 0
        self.arena_words = (nc.sbuf_usable_end - self.arena) // 4
        self.psum = ctx.enter_context(nc.psum_tensor("psum", [P, 8, SEQ], F32))

        def sem(name):
            return nc.alloc_semaphore(name)

        self.raw_loaded = [sem(f"raw_loaded_{s}") for s in range(RING)]
        self.hi_ready, self.lo_ready, self.slot_used = sem("hi_ready"), sem("lo_ready"), sem("slot_used")
        self.loaded, self.all_done, self.stored = sem("loaded"), sem("all_done"), sem("stored")
        self.passed = sem("vector_passed")
        self.chains = [sem("scalar_steps"), sem("vector_steps")]
        self.signals = {}
        self.slots = 0

    def count(self, name, total):
        if name not in self.signals:
            self.signals[name] = Signal(self.nc, name)
        return self.signals[name].reserve(total)

    def take(self, *shape, dt=F32):
        words = -(-math.prod(shape) // 16) * 16
        assert self.used + words <= self.arena_words, (self.used, words, self.arena_words)
        self.named += 1
        buf = self.nc.alloc_sbuf_tensor_at(f"scratch_{self.named}", [P, *shape], dt, offset=self.arena + 4 * self.used)
        self.used += words
        return buf

    def take_parts(self, *shape):
        return self.take(*shape, dt=F32R), self.take(*shape, dt=F32R)

    def split_hi(self, act, i, per, k):
        s = k % RING
        act.wait_ge(self.raw_loaded[s], (i * (per // RING) + k // RING + 1) * 16)
        act.wait_ge(self.slot_used, i * per + k + 1)
        act.copy(self.w_hi[:, s], self.w_raw[:, s]).then_inc(self.hi_ready, 1)
        if isinstance(i, int) and i == 0 and k == 0:
            return
        act.wait_ge(self.lo_ready, i * per + k)
        n, s = i * per + k + RING - 1, (k - 1) % RING
        src = self.io["stream"][bass.ds(n, 1)].rearrange("o p (k n) -> p (o k) n", n=P)
        act.dma_start(self.w_raw[:, s], src).then_inc(self.raw_loaded[s], 16)

    def split_lo(self, dve, i, per, k):
        s = k % RING
        dve.wait_ge(self.hi_ready, i * per + k + 1)
        self.nc.vector.tensor_tensor(self.w_lo[:, s], self.w_raw[:, s], self.w_hi[:, s],
                                     ALU.subtract).then_inc(self.lo_ready, 1)


class Stage:
    def tensor(self, pe): pass
    def vector(self, dve, chain): pass
    def scalar(self, act, chain): pass
    def sync(self, sp): pass


class Load(Stage):

    def __init__(self, c):
        self.c = c
        self.sq_done, self.sq_used = c.count("sq_done", KT), c.count("sq_used", KT + 2)

    def tensor(self, pe):
        pe.sem_inc(self.sq_used.sem, 2)
        pe.sem_inc(self.c.slot_used, RING)

    def scalar(self, act, chain):
        c = self.c
        act.wait_ge(c.loaded, 16 * c.n_loads)
        for k in range(KT):
            act.wait_ge(*self.sq_used(k + 1))
            act.activation(c.sq[:, k % 2], c.x[:, k], ACT.Square).then_inc(self.sq_done.sem, 1)
        for n in range(AHEAD):
            c.split_hi(act, 0, RING, n)

    def vector(self, dve, chain):
        c, nc = self.c, self.c.nc
        chain.step(nc.vector.memset(c.ssq[:], 0.0))
        for k in range(KT):
            dve.wait_ge(*self.sq_done(k + 1))
            ins = nc.vector.tensor_tensor(c.ssq[:], c.ssq[:], c.sq[:, k % 2], ALU.add)
            ins.then_inc(self.sq_used.sem, 1)
            dve.wait_ge(*self.sq_used(k + 3))
        for n in range(AHEAD):
            c.split_lo(dve, 0, RING, n)


class Norm(Stage):

    def __init__(self, c, index, keep=False):
        self.c, self.index, self.keep = c, index, keep
        self.sum_ready, self.var_ready = c.count("sum_ready", 1), c.count("var_ready", 1)
        self.rstd_ready = c.count("rstd_ready", 1)
        self.val_ready, self.hi_done, self.lo_done = (c.count(n, KT) for n in ("val_ready", "hi_done", "lo_done"))

    def tensor(self, pe):
        c = self.c
        pe.matmul(c.psum[:, 7], c.ones[:], c.ssq[:], start=True, stop=True).then_inc(self.sum_ready.sem, 1)

    def scalar(self, act, chain):
        c = self.c
        act.wait_ge(*self.var_ready(1))
        act.activation(c.rstd[:], c.tmp[:, 1], ACT.Sqrt).then_inc(self.rstd_ready.sem, 1)
        for k in range(KT):
            act.wait_ge(*self.val_ready(k + 1))
            if self.keep:
                act.activation(c.sq[:, k % 2], c.x[:, k], ACT.Square).then_inc(self.hi_done.sem, 1)
            else:
                act.copy(c.h_hi[:, k], c.tmp[:, k % 2]).then_inc(self.hi_done.sem, 1)

    def vector(self, dve, chain):
        c, nc = self.c, self.c.nc
        dve.wait_ge(*self.sum_ready(1))
        chain.step(nc.vector.tensor_scalar(c.tmp[:, 0], c.psum[:, 7], 1.0 / D, EPS, ALU.mult, ALU.add))
        nc.vector.reciprocal(c.tmp[:, 1], c.tmp[:, 0]).then_inc(self.var_ready.sem, 1)
        if self.keep:
            chain.step(nc.vector.memset(c.ssq[:], 0.0))
        dve.wait_ge(*self.rstd_ready(1))

        def finish(k):
            dve.wait_ge(*self.hi_done(k + 1))
            if self.keep:
                nc.vector.tensor_tensor(c.ssq[:], c.ssq[:], c.sq[:, k % 2], ALU.add).then_inc(self.lo_done.sem, 1)
            else:
                nc.vector.tensor_tensor(c.h_lo[:, k], c.tmp[:, k % 2], c.h_hi[:, k],
                                        ALU.subtract).then_inc(self.lo_done.sem, 1)

        for k in range(KT):
            if k >= 2:
                dve.wait_ge(*self.lo_done(k - 1))
            dst = c.x[:, k] if self.keep else c.tmp[:, k % 2]
            nc.vector.scalar_tensor_tensor(dst, c.x[:, k], c.norm_w[:, self.index, k:k + 1], c.rstd[:],
                                           ALU.mult, ALU.mult).then_inc(self.val_ready.sem, 1)
            if k >= 1:
                finish(k - 1)
                dve.wait_ge(*self.lo_done(k))
        finish(KT - 1)


class Linear(Stage):
    unroll = 4
    two_banks = True

    def __init__(self, c, tiles, source=None, slots=(SLOT_TILES,), unroll=None):
        self.c, self.tiles, self.slots = c, tiles, slots
        self.source = source or (c.h_hi, c.h_lo)
        self.per = len(slots)
        self.unroll = unroll or 4
        assert self.unroll * self.per % RING == 0 and self.unroll % 2 == 0
        self.slot0 = c.slots
        c.slots += tiles * self.per
        if self.two_banks:
            self.bank_read = c.count("bank_read", tiles + 2)
        self.begin()

    def begin(self): pass

    def out(self, u):
        return self.c.psum[:, u % 2]

    def done(self, i, u):
        c = self.c
        return c.slot_used, (i * self.unroll + u + 1) * self.per + self.slot0 + RING

    def tensor(self, pe):
        c = self.c
        pe.sem_inc(self.bank_read.sem, 2)
        for i, u in repeat(pe, self.tiles, self.unroll):
            self.products(pe, i, u)

    def products(self, pe, i, u):
        c, (hi, lo) = self.c, self.source
        pe.wait_ge(*self.bank_read(i * self.unroll + u + 1))
        self.kind = u
        for j, tiles in enumerate(self.slots):
            k0 = self.slot0 + u * self.per + j
            s = k0 % RING
            pe.wait_ge(c.lo_ready, i * (self.unroll * self.per) + k0 + 1)
            first, last = j == 0, j == self.per - 1
            for k in range(tiles):
                kk = j * SLOT_TILES + k
                pairs = ((c.w_hi, hi), (c.w_hi, lo), (c.w_lo, hi))
                for n, (w, b) in enumerate(pairs):
                    mm = pe.matmul(self.out(u), w[:, s, k], self.rhs(b, kk),
                                   start=(first and k == 0 and n == 0),
                                   stop=(last and k == tiles - 1 and n == 2))
            mm.then_inc(c.slot_used, 1)

    def rhs(self, part, k):
        return part[:, k]

    def scalar(self, act, chain):
        for i, u in repeat(act, self.tiles, self.unroll, chain, self.scalar_marks):
            for j in range(self.per):
                self.c.split_hi(act, i, self.unroll * self.per, self.slot0 + u * self.per + j + AHEAD)
            self.scalar_tile(act, chain, i, u)

    def vector(self, dve, chain):
        self.vector_begin(dve, chain)
        for i, u in repeat(dve, self.tiles, self.unroll, chain, self.vector_marks):
            for j in range(self.per):
                self.c.split_lo(dve, i, self.unroll * self.per, self.slot0 + u * self.per + j + AHEAD)
            self.vector_tile(dve, chain, i, u)

    scalar_marks = vector_marks = 0
    def scalar_tile(self, act, chain, i, u): pass
    def vector_begin(self, dve, chain): pass
    def vector_tile(self, dve, chain, i, u): pass


class Project(Linear):

    def __init__(self, c, tiles, dst, scale=1.0, func=ACT.Copy, **kw):
        self.dst, self.scale, self.func = dst, scale, func
        super().__init__(c, tiles, **kw)

    def scalar_tile(self, act, chain, i, u):
        t = i * self.unroll + u
        act.wait_ge(*self.done(i, u))
        act.activation(at(self.dst, t), self.out(u), self.func, scale=self.scale).then_inc(self.bank_read.sem, 1)


class ProjectTokens(Linear):

    def __init__(self, c, tiles, dst, cols=P):
        self.dst, self.cols = dst, cols
        super().__init__(c, tiles)

    def begin(self):
        self.turned = self.c.count("turned", self.tiles + 2)
        self.turned_read = self.c.count("turned_read", self.tiles + 2)

    def turn(self, pe, i, u):
        c, t = self.c, i * self.unroll + u
        pe.wait_ge(*self.bank_read(t + 3))
        pe.wait_ge(*self.turned_read(t + 1))
        for k in range(TT):
            mm = pe.transpose(c.psum[:, 4 + u % 2, k * P:(k + 1) * P], c.tmp[:, u % 2, k * P:(k + 1) * P], c.ident[:])
        mm.then_inc(self.turned.sem, 1)

    def tensor(self, pe):
        for count in (self.bank_read, self.turned, self.turned_read):
            pe.sem_inc(count.sem, 2)
        for i, u in repeat(pe, self.tiles, self.unroll):
            self.products(pe, i, u)
            if u > 0:
                self.turn(pe, i, u - 1)
            if u == self.unroll - 1 or self.is_last(i, u):
                self.turn(pe, i, u)

    def is_last(self, i, u):
        whole = self.tiles // self.unroll
        return u == self.tiles - whole * self.unroll - 1 and isinstance(i, int) and i == whole

    def scalar_tile(self, act, chain, i, u):
        act.wait_ge(*self.done(i, u))
        act.wait_ge(*self.turned(i * self.unroll + u + 1))
        act.copy(self.c.tmp[:, u % 2], self.out(u)).then_inc(self.bank_read.sem, 1)

    def vector_tile(self, dve, chain, i, u):
        t = i * self.unroll + u
        dve.wait_ge(*self.turned(t + 3))
        turned = self.c.psum[:, 4 + u % 2].rearrange("p (t n) -> p t n", t=TT)[:, :, :self.cols]
        self.c.nc.vector.tensor_copy(self.dst[:, :, bass.ds(t * P, self.cols)], turned).then_inc(self.turned_read.sem, 1)


class Residual(Linear):

    def __init__(self, c, tiles=KT, gather=True, **kw):
        self.gather = gather
        super().__init__(c, tiles, **kw)

    def begin(self):
        c = self.c
        self.sq_done, self.sq_used = c.count("sq_done", self.tiles), c.count("sq_used", self.tiles + 2)

    def tensor(self, pe):
        pe.sem_inc(self.sq_used.sem, 2)
        super().tensor(pe)

    def vector_begin(self, dve, chain):
        chain.step(self.c.nc.vector.memset(self.c.ssq[:], 0.0))

    def vector_tile(self, dve, chain, i, u):
        c, t = self.c, i * self.unroll + u
        dve.wait_ge(*self.done(i, u))
        c.nc.vector.tensor_tensor(at(c.x, t), at(c.x, t), self.out(u), ALU.add).then_inc(self.bank_read.sem, 1)
        dve.wait_ge(*self.sq_done(t + 1))
        dve.wait_ge(*self.sq_used(t + 2))
        c.nc.vector.tensor_tensor(c.ssq[:], c.ssq[:], c.sq[:, u % 2], ALU.add).then_inc(self.sq_used.sem, 1)

    def scalar_tile(self, act, chain, i, u):
        c, t = self.c, i * self.unroll + u
        act.wait_ge(*self.bank_read(t + 3))
        act.wait_ge(*self.sq_used(t + 1))
        act.activation(c.sq[:, u % 2], at(c.x, t), ACT.Square).then_inc(self.sq_done.sem, 1)


class ReluSquare(Linear):

    def __init__(self, c, tiles, dst, **kw):
        self.dst = dst
        super().__init__(c, tiles, **kw)

    def begin(self):
        c = self.c
        self.val_ready, self.hi_done = c.count("val_ready", self.tiles), c.count("hi_done", self.tiles)
        self.lo_done = c.count("lo_done", self.tiles + 2)

    def tensor(self, pe):
        pe.sem_inc(self.lo_done.sem, 2)
        super().tensor(pe)

    def scalar_tile(self, act, chain, i, u):
        c, t = self.c, i * self.unroll + u
        act.wait_ge(*self.done(i, u))
        act.wait_ge(*self.lo_done(t + 1))
        act.activation(c.tmp[:, u % 2], self.out(u), ACT.Relu).then_inc(self.bank_read.sem, 1)
        act.wait_ge(*self.bank_read(t + 3))
        act.activation(at(self.dst[0], t), c.tmp[:, u % 2], ACT.Square).then_inc(self.hi_done.sem, 1)

    def vector_tile(self, dve, chain, i, u):
        c, t = self.c, i * self.unroll + u
        dve.wait_ge(*self.bank_read(t + 3))
        c.nc.vector.tensor_tensor(c.sq[:, u % 2], c.tmp[:, u % 2], c.tmp[:, u % 2],
                                  ALU.mult).then_inc(self.val_ready.sem, 1)
        dve.wait_ge(*self.val_ready(t + 1))
        dve.wait_ge(*self.hi_done(t + 1))
        c.nc.vector.tensor_tensor(at(self.dst[1], t), c.sq[:, u % 2], at(self.dst[0], t),
                                  ALU.subtract).then_inc(self.lo_done.sem, 1)


class Steps:

    def __init__(self, c, name, steps, turns, before=0):
        assert len(set(steps)) == len(steps)
        self.steps, self.before = steps, before
        self.count, self.next = c.count(name, len(steps) * (turns + before)), 0

    def begin(self, eng):
        eng.sem_inc(self.count.sem, self.before * len(self.steps))

    def mark(self, instruction, step):
        assert self.steps[self.next % len(self.steps)] == step, (self.steps[self.next % len(self.steps)], step)
        self.next += 1
        instruction.then_inc(self.count.sem, 1)

    def __call__(self, turn, step):
        return self.count(turn * len(self.steps) + self.before * len(self.steps) + self.steps.index(step) + 1)


class ConvProject(Linear):
    TAPS = 4

    def __init__(self, c, tiles, dst):
        self.dst = dst
        self.raw, self.acc = c.take(2, SEQ + 16), c.take(2, SEQ)
        super().__init__(c, tiles)

    def begin(self):
        c = self.c
        self.conv_done = c.count("val_ready", self.tiles)
        self.silu_done = c.count("hi_done", self.tiles + 2)
        self.pads = self.TAPS - 1

    vector_marks = 3

    def tensor(self, pe):
        pe.sem_inc(self.silu_done.sem, 2)
        super().tensor(pe)

    def vector_begin(self, dve, chain):
        chain.step(self.c.nc.vector.memset(self.raw[:, :, :self.pads], 0.0))

    def scalar_tile(self, act, chain, i, u):
        t = i * self.unroll + u
        act.wait_ge(*self.done(i, u))
        act.wait_ge(*self.silu_done(t + 1))
        act.copy(self.raw[:, u % 2, self.pads:self.pads + SEQ], self.out(u)).then_inc(self.bank_read.sem, 1)
        act.wait_ge(*self.conv_done(t + 1))
        act.activation(at(self.dst, t), self.acc[:, u % 2], ACT.Silu).then_inc(self.silu_done.sem, 1)

    def vector_tile(self, dve, chain, i, u):
        c, t = self.c, i * self.unroll + u
        v, raw, acc = c.nc.vector, self.raw[:, u % 2], self.acc[:, u % 2]
        dve.wait_ge(*self.bank_read(t + 3))
        dve.wait_ge(*self.silu_done(t + 1))

        def tap(j):
            return c.conv_w[:, bass.ds(t, 1), j:j + 1].rearrange("p a b -> p (a b)")

        chain.step(v.tensor_scalar(acc, raw[:, :SEQ], tap(0), None, ALU.mult))
        for j in range(1, self.TAPS):
            ins = v.scalar_tensor_tensor(acc, raw[:, j:j + SEQ], tap(j), acc, ALU.mult, ALU.add)
            if j < self.TAPS - 1:
                chain.step(ins)
            else:
                ins.then_inc(self.conv_done.sem, 1)


class HeadNorm(Stage):

    def __init__(self, c, tiles, per=1, n=1.0, scale=1.0, gains=None):
        self.c, self.tiles, self.per, self.n, self.scale = c, tiles, per, n, scale
        self.gains = gains or [None] * len(tiles)
        self.cols = len(tiles) * per
        self.var = c.take(3, TT, self.cols)
        self.rows = c.take(SEQ)
        self.sq_done, self.sums_ready = c.count("sq_done", len(tiles)), c.count("sum_ready", len(tiles) + 2)
        self.inverse, self.root = c.count("var_ready", 1), c.count("rstd_ready", 1)
        self.turned, self.rows_ready = c.count("turned", 1), c.count("hi_done", 1)
        self.spread, self.scaled = c.count("aux_a", len(tiles)), c.count("aux_b", len(tiles))

    def tensor(self, pe):
        c = self.c
        sums = c.psum[:, 0, :TT * self.cols].rearrange("p (t n) -> p t n", t=TT)
        ones = c.ones[:, :1] if self.per == 1 else c.halves[:]
        pe.sem_inc(self.sums_ready.sem, 2)
        for j in range(len(self.tiles)):
            pe.wait_ge(*self.sq_done(j + 1))
            for t in range(TT):
                mm = pe.matmul(sums[:, t, j * self.per:(j + 1) * self.per], c.sq[:, j % 2, t * P:(t + 1) * P], ones,
                               start=True, stop=True)
            mm.then_inc(self.sums_ready.sem, 1)
        pe.wait_ge(*self.root(1))
        for t in range(TT):
            mm = pe.transpose(c.psum[:self.cols, 1, t * P:(t + 1) * P], self.var[:, 2, t], c.ident[:])
        mm.then_inc(self.turned.sem, 1)
        pe.wait_ge(*self.rows_ready(1))
        for j in range(len(self.tiles)):
            if j >= 2:
                pe.wait_ge(*self.scaled(j - 1))
            for k in range(self.per):
                to, wide = slice(k * P // self.per, (k + 1) * P // self.per), P // self.per
                row = j * self.per + k
                mm = pe.matmul(c.psum[to, 2 + j % 2], c.ident[:self.cols, row:row + 1].broadcast_to([self.cols, wide]),
                               self.rows[:self.cols], start=True, stop=True)
            mm.then_inc(self.spread.sem, 1)

    def scalar(self, act, chain):
        c = self.c
        for j, tile in enumerate(self.tiles):
            act.wait_ge(*self.sums_ready(j + 1))
            act.activation(c.sq[:, j % 2], tile, ACT.Square).then_inc(self.sq_done.sem, 1)
        act.wait_ge(*self.inverse(1))
        act.activation(self.var[:, 2], self.var[:, 1], ACT.Sqrt, scale=self.scale ** 2).then_inc(self.root.sem, 1)
        act.wait_ge(*self.turned(1))
        act.copy(self.rows[:self.cols], c.psum[:self.cols, 1]).then_inc(self.rows_ready.sem, 1)

    def vector(self, dve, chain):
        c, v = self.c, self.c.nc.vector
        dve.wait_ge(*self.sums_ready(len(self.tiles) + 2))
        sums = c.psum[:, 0, :TT * self.cols].rearrange("p (t n) -> p t n", t=TT)
        chain.step(v.tensor_scalar(self.var[:, 0], sums, 1.0 / self.n, EPS, ALU.mult, ALU.add))
        v.reciprocal(self.var[:, 1], self.var[:, 0]).then_inc(self.inverse.sem, 1)
        for j, tile in enumerate(self.tiles):
            dve.wait_ge(*self.spread(j + 1))
            gain = 1.0 if self.gains[j] is None else self.gains[j]
            v.scalar_tensor_tensor(tile, tile, gain, c.psum[:, 2 + j % 2], ALU.mult,
                                   ALU.mult).then_inc(self.scaled.sem, 1)


class DnGates(Stage):

    def __init__(self, c, ab):
        self.c, self.ab = c, ab
        n = TT * DN_HEADS
        self.w = c.take(12, TT, DN_HEADS)
        names = ("z", "abs", "soft", "softplus", "g", "beta", "gc", "rest", "beg", "dk", "eg", "minus")
        self.at = {name: self.w[:, k] for k, name in enumerate(names)}
        self.rate = c.take(DN_HEADS)
        self.last = c.take(2, TT, DN_HEADS)
        self.rows = c.take(2, SEQ)
        self.rows_dram = c.nc.dram_tensor("dn_rows", (2, DN_HEADS, SEQ), F32, kind="Internal").ap()
        self.did_dve = Steps(c, "aux_a", ("z", "minus", "abs", "sp", "g", "gc", "rest", "beg"), 1)
        self.did_act = Steps(c, "aux_b", ("exp", "ln", "rate", "beta", "eg", "dk", "last", "rows"), 1)
        self.did_pe = Steps(c, "aux_c", ("sums", "rows"), 1)
        self.stored = c.count("aux_d", 32)

    def vector(self, dve, chain):
        c, v, a, did = self.c, self.c.nc.vector, self.at, self.did_dve
        bias = c.dn_small[:, 1:2].broadcast_to([P, TT, DN_HEADS])
        did.mark(v.tensor_tensor(a["z"], self.ab[:, :, :DN_HEADS], bias, ALU.add), "z")
        dve.wait_ge(*did(0, "z"))
        did.mark(v.tensor_scalar(a["minus"], a["z"], -1.0, None, ALU.mult), "minus")
        dve.wait_ge(*did(0, "minus"))
        did.mark(v.tensor_tensor(a["abs"], a["z"], a["minus"], ALU.max), "abs")
        dve.wait_ge(*self.did_act(0, "ln"))
        did.mark(v.scalar_tensor_tensor(a["softplus"], a["z"], 0.0, a["soft"], ALU.max, ALU.add), "sp")
        dve.wait_ge(*did(0, "sp"))
        dve.wait_ge(*self.did_act(0, "rate"))
        rate = self.rate[:].unsqueeze(1).broadcast_to([P, TT, DN_HEADS])
        did.mark(v.scalar_tensor_tensor(a["g"], a["softplus"], -1.0, rate, ALU.mult, ALU.mult), "g")
        dve.wait_ge(*self.did_pe(0, "sums"))
        n = TT * DN_HEADS
        did.mark(v.tensor_copy(a["gc"], c.psum[:, 0, :n].rearrange("p (t h) -> p t h", t=TT)), "gc")
        dve.wait_ge(*did(0, "gc"))
        did.mark(v.tensor_tensor(a["rest"], c.psum[:, 0, n:2 * n].rearrange("p (t h) -> p t h", t=TT), a["gc"],
                                 ALU.subtract), "rest")
        dve.wait_ge(*self.did_act(0, "eg"))
        did.mark(v.tensor_tensor(a["beg"], a["beta"], a["eg"], ALU.mult), "beg")

    def scalar(self, act, chain):
        c, a, did = self.c, self.at, self.did_act
        act.wait_ge(*self.did_dve(0, "abs"))
        did.mark(act.activation(a["soft"], a["abs"], ACT.Exp, scale=-1.0), "exp")
        act.wait_ge(*did(0, "exp"))
        did.mark(act.activation(a["soft"], a["soft"], ACT.Ln, bias=1.0), "ln")
        did.mark(act.activation(self.rate[:], c.dn_small[:, 0], ACT.Exp), "rate")
        did.mark(act.activation(a["beta"], self.ab[:, :, DN_HEADS:], ACT.Sigmoid), "beta")
        act.wait_ge(*self.did_dve(0, "gc"))
        did.mark(act.activation(a["eg"], a["gc"], ACT.Exp), "eg")
        act.wait_ge(*self.did_dve(0, "rest"))
        did.mark(act.activation(a["dk"], a["rest"], ACT.Exp), "dk")
        n = TT * DN_HEADS
        did.mark(act.activation(self.last[:], c.psum[:, 0, 2 * n:4 * n].rearrange("p (b t h) -> p b t h", b=2, t=TT),
                                ACT.Exp), "last")
        act.wait_ge(*self.did_pe(0, "rows"))
        did.mark(act.copy(self.rows[:DN_HEADS], c.psum[:DN_HEADS, 1:3]), "rows")

    def tensor(self, pe):
        c, a = self.c, self.at
        n = TT * DN_HEADS
        pe.wait_ge(*self.did_dve(0, "g"))
        g = a["g"].rearrange("p t h -> p (t h)")
        for k, w in enumerate((c.prefix[:], c.chunks[:], c.first[:, 0], c.first[:, 1])):
            mm = pe.matmul(c.psum[:, 0, k * n:(k + 1) * n], w, g, start=True, stop=True)
        self.did_pe.mark(mm, "sums")
        pe.wait_ge(*self.did_dve(0, "gc"))
        pe.wait_ge(*self.did_act(0, "beta"))
        for k, name in enumerate(("gc", "beta")):
            for t in range(TT):
                mm = pe.transpose(c.psum[:DN_HEADS, 1 + k, t * P:(t + 1) * P], a[name][:, t], c.ident[:])
        self.did_pe.mark(mm, "rows")

    def sync(self, sp):
        sp.wait_ge(*self.did_act(0, "rows"))
        for k in range(2):
            sp.dma_start(self.rows_dram[k], self.rows[:DN_HEADS, k]).then_inc(self.stored.sem, 16)
        sp.wait_ge(*self.stored(32))


class DeltaChunks(Stage):

    LANES, LEVELS = 2, 6
    COUPLED, SQUARED = 1, 2

    def __init__(self, c, qkv, gates):
        self.c, self.qkv, self.g = c, qkv, gates
        self.qkd, self.kd = c.h_words[:, :DN_HEADS], c.h_words[:, DN_HEADS:]
        self.k, self.v, self.x, self.xt, self.y = (c.take(self.LANES, SEQ) for _ in range(5))
        self.grow, self.beta, self.decay = gates.rows, c.sq, c.tmp
        turns = DN_HEADS // self.LANES
        self.fetched = [c.count(f"fetched_{b}", 16 * 4 * turns) for b in range(self.LANES)]
        levels = range(1, self.LEVELS)
        pe = ["kk", "kq", "k_turned", "v_turned", "x0"] + [f"{s}{b}" for b in levels for s in ("y", "zt")]
        pe += ["u", "wt"]
        dve = [f"d{t}" for t in range(TT)] + ["decay", "qkd", "kkd", "at", "ct0", "xt0", "qd"]
        dve += [f"{s}{b}" for b in levels for s in ("ct", "x", "xt") if (s, b) != ("x", self.LEVELS - 1)]
        dve += ["wt"]
        act = ["decay", "grow"] + [f"{s}{t}" for t in range(TT) for s in ("kbg", "kd", "vb")]
        act += ["x0"] + [f"y{b}" for b in levels] + ["u"]
        self.pe_did, self.dve_did, self.act_did = (
            [Steps(c, f"{eng}_lane_{lane}", steps, turns, before=1) for lane in range(self.LANES)]
            for eng, steps in (("tensor", pe), ("vector", dve), ("scalar", act)))

    def heads(self, eng):
        for i, _ in repeat(eng, DN_HEADS // self.LANES, 1):
            yield i, [(lane, i * self.LANES + lane) for lane in range(self.LANES)]

    def sync(self, sp):
        for i, lanes in self.heads(sp):
            for lane, head in lanes:
                sp.wait_ge(*self.pe_did[lane](i - 1, "wt"))
                rows = self.g.rows_dram
                moves = [(self.k[:, lane], at(self.qkv, DN_HEADS + head)),
                         (self.v[:, lane], at(self.qkv, 2 * DN_HEADS + head)),
                         (self.grow[:, lane], rows[0, bass.ds(head, 1)].broadcast_to([P, SEQ])),
                         (self.beta[:, lane], rows[1, bass.ds(head, 1)].broadcast_to([P, SEQ]))]
                for to, of in moves:
                    sp.dma_start(to, of).then_inc(self.fetched[lane].sem, 16)

    def tensor(self, pe):
        c = self.c
        tiles = [slice(t * P, (t + 1) * P) for t in range(TT)]
        for did in self.pe_did + self.dve_did + self.act_did:
            did.begin(pe)

        def product(bank, left, right):
            for t in tiles:
                mm = pe.matmul(c.psum[:, bank, t], left[:, t], right[:, t], start=True, stop=True)
            return mm

        def turn(bank, of):
            for t in tiles:
                mm = pe.transpose(c.psum[:, bank, t], of[:, t], c.ident[:])
            return mm

        for i, lanes in self.heads(pe):
            for lane, head in lanes:
                did, b, k = self.pe_did[lane], 4 * lane, self.k[:, lane]
                pe.wait_ge(*self.fetched[lane](i * 64 + 64))
                pe.wait_ge(*self.act_did[lane](i - 1, "u"))
                pe.wait_ge(*self.dve_did[lane](i - 1, "wt"))
                did.mark(product(b, k, k), "kk")
                did.mark(product(b + 1, k, at(self.qkv, head)), "kq")
                did.mark(turn(b + 2, k), "k_turned")
                did.mark(turn(b + 3, self.v[:, lane]), "v_turned")
            for lane, _ in lanes:
                pe.wait_ge(*self.dve_did[lane](i, "xt0"))
                self.pe_did[lane].mark(turn(4 * lane, self.xt[:, lane]), "x0")
            for n in range(1, self.LEVELS):
                for lane, _ in lanes:
                    dve, act, b = self.dve_did[lane], self.act_did[lane], 4 * lane
                    pe.wait_ge(*(act(i, "x0") if n == 1 else dve(i, f"xt{n - 1}")))
                    pe.wait_ge(*dve(i, f"ct{n}"))
                    self.pe_did[lane].mark(product(b + self.COUPLED, self.beta[:, lane], self.x[:, lane]), f"y{n}")
                for lane, _ in lanes:
                    b, x, xt, y = 4 * lane, self.x[:, lane], self.xt[:, lane], self.y[:, lane]
                    pe.wait_ge(*self.act_did[lane](i, f"y{n}"))
                    if n < self.LEVELS - 1:
                        product(b + self.SQUARED, xt, y)
                    self.pe_did[lane].mark(product(b + self.SQUARED + 1, y, xt), f"zt{n}")
            for lane, _ in lanes:
                did, b, xt = self.pe_did[lane], 4 * lane, self.xt[:, lane]
                pe.wait_ge(*self.dve_did[lane](i, f"xt{self.LEVELS - 1}"))
                pe.wait_ge(*self.act_did[lane](i, f"vb{TT - 1}"))
                did.mark(product(b, xt, self.v[:, lane]), "u")
                did.mark(product(b + 1, self.k[:, lane], xt), "wt")

    def vector(self, dve, chain):
        c, v, g = self.c, self.c.nc.vector, self.g
        tiles = [slice(t * P, (t + 1) * P) for t in range(TT)]

        def tiled(buf):
            return buf.rearrange("p (t n) -> p t n", t=TT)

        def mask(m):
            return m.unsqueeze(1).broadcast_to([P, TT, P])

        for i, lanes in self.heads(dve):
            for lane, head in lanes:
                decay, grow, did = self.decay[:, lane], self.grow[:, lane], self.dve_did[lane]
                dve.wait_ge(*self.fetched[lane](i * 64 + 64))
                for t in range(TT):
                    did.mark(v.tensor_scalar(decay[:, tiles[t]], grow[:, tiles[t]],
                                             g.at["gc"][:, t, bass.ds(head, 1)], 0.0, ALU.subtract, ALU.min), f"d{t}")
            for lane, head in lanes:
                decay, beta, did = self.decay[:, lane], self.beta[:, lane], self.dve_did[lane]
                act, pe, b = self.act_did[lane], self.pe_did[lane], 4 * lane
                dve.wait_ge(*act(i, "decay"))
                did.mark(v.tensor_tensor(tiled(decay), tiled(decay), mask(c.prefix[:]), ALU.mult), "decay")
                dve.wait_ge(*did(i, "decay"))
                dve.wait_ge(*pe(i, "kq"))
                did.mark(v.tensor_tensor(at(self.qkd, head), c.psum[:, b + 1], decay, ALU.mult), "qkd")
                dve.wait_ge(*did(i, "qkd"))
                did.mark(v.tensor_tensor(decay, c.psum[:, b], decay, ALU.mult), "kkd")
            for lane, head in lanes:
                decay, beta, did = self.decay[:, lane], self.beta[:, lane], self.dve_did[lane]
                dve.wait_ge(*did(i, "kkd"))
                did.mark(v.tensor_tensor(decay, decay, beta, ALU.mult), "at")
            for lane, head in lanes:
                decay, beta, did = self.decay[:, lane], self.beta[:, lane], self.dve_did[lane]
                dve.wait_ge(*did(i, "at"))
                did.mark(v.tensor_tensor(tiled(beta), tiled(decay), mask(c.levels[:, 0]), ALU.mult), "ct0")
            for lane, head in lanes:
                beta, did, act = self.beta[:, lane], self.dve_did[lane], self.act_did[lane]
                dve.wait_ge(*did(i, "ct0"))
                did.mark(v.scalar_tensor_tensor(tiled(self.xt[:, lane]), tiled(beta), -1.0, mask(c.ident[:]),
                                                ALU.mult, ALU.add), "xt0")
                dve.wait_ge(*act(i, "grow"))
                q = at(self.qkv, head)
                did.mark(v.tensor_tensor(q, q, self.grow[:, lane], ALU.mult), "qd")
            for n in range(1, self.LEVELS):
                for lane, _ in lanes:
                    did, pe = self.dve_did[lane], self.pe_did[lane]
                    dve.wait_ge(*(did(i, "xt0") if n == 1 else pe(i, f"y{n - 1}")))
                    did.mark(v.tensor_tensor(tiled(self.beta[:, lane]), tiled(self.decay[:, lane]),
                                             mask(c.levels[:, n]), ALU.mult), f"ct{n}")
                for lane, _ in lanes:
                    did, b, x, xt = self.dve_did[lane], 4 * lane, self.x[:, lane], self.xt[:, lane]
                    dve.wait_ge(*self.pe_did[lane](i, f"zt{n}"))
                    if n < self.LEVELS - 1:
                        did.mark(v.tensor_tensor(x, x, c.psum[:, b + self.SQUARED], ALU.subtract), f"x{n}")
                    did.mark(v.tensor_tensor(xt, xt, c.psum[:, b + self.SQUARED + 1], ALU.subtract), f"xt{n}")
            for lane, head in lanes:
                dve.wait_ge(*self.pe_did[lane](i, "wt"))
                self.dve_did[lane].mark(v.tensor_copy(at(self.qkv, DN_HEADS + head), c.psum[:, 4 * lane + 1]), "wt")

    def scalar(self, act, chain):
        c, g = self.c, self.g
        tiles = [slice(t * P, (t + 1) * P) for t in range(TT)]
        for i, lanes in self.heads(act):
            for lane, _ in lanes:
                did, decay, grow = self.act_did[lane], self.decay[:, lane], self.grow[:, lane]
                act.wait_ge(*self.dve_did[lane](i, f"d{TT - 1}"))
                did.mark(act.activation(decay, decay, ACT.Exp), "decay")
                did.mark(act.activation(grow, grow, ACT.Exp), "grow")
            for lane, head in lanes:
                act.wait_ge(*self.pe_did[lane](i, "v_turned"))
                kd = at(self.kd, head)
                for t in range(TT):
                    for name, to, bank, by in (("kbg", self.k[:, lane], 2, "beg"), ("kd", kd, 2, "dk"),
                                               ("vb", self.v[:, lane], 3, "beta")):
                        self.act_did[lane].mark(
                            act.activation(to[:, tiles[t]], c.psum[:, 4 * lane + bank, tiles[t]], ACT.Copy,
                                           scale=g.at[by][:, t, bass.ds(head, 1)]), f"{name}{t}")
            for lane, _ in lanes:
                act.wait_ge(*self.pe_did[lane](i, "x0"))
                self.act_did[lane].mark(act.copy(self.x[:, lane], c.psum[:, 4 * lane]), "x0")
            for n in range(1, self.LEVELS):
                for lane, _ in lanes:
                    act.wait_ge(*self.pe_did[lane](i, f"y{n}"))
                    self.act_did[lane].mark(act.copy(self.y[:, lane], c.psum[:, 4 * lane + self.COUPLED]), f"y{n}")
            for lane, head in lanes:
                act.wait_ge(*self.pe_did[lane](i, "u"))
                self.act_did[lane].mark(act.copy(at(self.qkv, 2 * DN_HEADS + head), c.psum[:, 4 * lane]), "u")


class DeltaScan(Stage):

    GROUPS = 2

    def __init__(self, c, qkv, chunks):
        self.c, self.g, self.chunks = c, chunks.g, chunks
        self.per = DN_HEADS // self.GROUPS
        self.q, self.wt, self.u = (qkv[:, n * DN_HEADS:(n + 1) * DN_HEADS] for n in range(3))
        self.state = [c.tmp, c.sq]
        self.last = SEQ // CHUNK - 1
        scan = range(self.last + 1)
        name = lambda n, steps: [f"{s}{n}_{g}" for s in steps for g in range(self.GROUPS)]
        pe, dve, act = [], [f"s{-1}_{g}" for g in range(self.GROUPS)], []
        for n in scan:
            pe += name(n, ("ws",)) + [f"{s}{n}_{g}" for g in range(self.GROUPS) for s in ("ds", "o")[n == self.last:]]
            dve += name(n, ("vn",)) + (name(n, ("faded", "s")) if n < self.last else [])
        act = [f"o{t}_{g}" for t in range(TT) for g in range(self.GROUPS)]
        self.pe_did, self.dve_did, self.act_did = (Steps(c, f"{eng}_scan", steps, 1)
                                                   for eng, steps in (("tensor", pe), ("vector", dve), ("scalar", act)))

    def heads(self, g):
        return range(g * self.per, (g + 1) * self.per)

    def tensor(self, pe):
        c, did, dve, act = self.c, self.pe_did, self.dve_did, self.act_did
        qkd, kd = self.chunks.qkd, self.chunks.kd
        for n in range(self.last + 1):
            t, half = n // 2, n % 2
            tile, tokens = slice(t * P, (t + 1) * P), slice(n * CHUNK, (n + 1) * CHUNK)
            rows = slice(half * CHUNK, (half + 1) * CHUNK)
            state = self.state[n % 2]
            col = lambda h: slice(h % self.per * P, (h % self.per + 1) * P)
            for g in range(self.GROUPS):
                pe.wait_ge(*dve(0, f"s{n - 1}_{g}"))
                for h in self.heads(g):
                    mm = pe.matmul(c.psum[:, g, col(h)], self.wt[:, h, tile], state[:, g, col(h)], start=True, stop=True)
                did.mark(mm, f"ws{n}_{g}")
            for g in range(self.GROUPS):
                pe.wait_ge(*dve(0, f"vn{n}_{g}"))
                if n < self.last:
                    for h in self.heads(g):
                        mm = pe.matmul(c.psum[:, 2 + g, col(h)], kd[rows, h, tile], self.u[rows, h, tile],
                                       start=True, stop=True)
                    did.mark(mm, f"ds{n}_{g}")
                if t >= 2 and half == 0:
                    pe.wait_ge(*act(0, f"o{t - 2}_{g}"))
                for h in self.heads(g):
                    out = c.psum[:, 4 + t % 2 * 2 + g, col(h)][:, rows]
                    pe.matmul(out, state[:, g, col(h)], self.q[:, h, tokens], start=True, stop=False)
                    mm = pe.matmul(out, self.u[rows, h, tile], qkd[rows, h, tokens], start=False, stop=True)
                did.mark(mm, f"o{n}_{g}")

    def vector(self, dve, chain):
        c, v, did, pe = self.c, self.c.nc.vector, self.dve_did, self.pe_did

        def split(buf):
            return buf.rearrange("p (h n) -> p h n", n=P)

        for g in range(self.GROUPS):
            did.mark(v.memset(self.state[0][:, g], 0.0), f"s{-1}_{g}")
        for n in range(self.last + 1):
            t, half = n // 2, n % 2
            rows = slice(half * CHUNK, (half + 1) * CHUNK)
            for g in range(self.GROUPS):
                u = self.u[rows, g * self.per:(g + 1) * self.per, t * P:(t + 1) * P]
                dve.wait_ge(*pe(0, f"ws{n}_{g}"))
                did.mark(v.tensor_tensor(u, u, split(c.psum[rows, g]), ALU.subtract), f"vn{n}_{g}")
            if n == self.last:
                break
            for g in range(self.GROUPS):
                last = self.g.last[:, half, t, g * self.per:(g + 1) * self.per].unsqueeze(2).broadcast_to([P, self.per, P])
                did.mark(v.tensor_tensor(split(self.state[(n + 1) % 2][:, g]), split(self.state[n % 2][:, g]), last,
                                         ALU.mult), f"faded{n}_{g}")
            for g in range(self.GROUPS):
                state = self.state[(n + 1) % 2][:, g]
                dve.wait_ge(*did(0, f"faded{n}_{g}"))
                dve.wait_ge(*pe(0, f"ds{n}_{g}"))
                did.mark(v.tensor_tensor(state, state, c.psum[:, 2 + g], ALU.add), f"s{n}_{g}")

    def scalar(self, act, chain):
        c = self.c
        for t in range(TT):
            for g in range(self.GROUPS):
                act.wait_ge(*self.pe_did(0, f"o{2 * t + 1}_{g}"))
                self.act_did.mark(act.copy(self.q[:, g * self.per:(g + 1) * self.per, t * P:(t + 1) * P],
                                           c.psum[:, 4 + t % 2 * 2 + g].rearrange("p (h n) -> p h n", n=P)), f"o{t}_{g}")


class Gate(Stage):

    def __init__(self, c, out, gate):
        self.c, self.out, self.gate = c, out, gate
        self.val_ready, self.hi_done, self.lo_done = (c.count(n, KT) for n in ("val_ready", "hi_done", "lo_done"))

    def scalar(self, act, chain):
        for k in range(KT):
            act.wait_ge(*self.val_ready(k + 1))
            act.copy(self.c.h_hi[:, k], self.out[:, k]).then_inc(self.hi_done.sem, 1)

    def vector(self, dve, chain):
        c, v = self.c, self.c.nc.vector
        for k in range(KT + 1):
            if k < KT:
                v.tensor_tensor(self.out[:, k], self.out[:, k], self.gate[:, k], ALU.mult).then_inc(self.val_ready.sem, 1)
            if k > 0:
                dve.wait_ge(*self.hi_done(k))
                v.tensor_tensor(c.h_lo[:, k - 1], self.out[:, k - 1], c.h_hi[:, k - 1],
                                ALU.subtract).then_inc(self.lo_done.sem, 1)


class Attention(Stage):
    BODY_HEADS = 4
    TURN, VALUES, PAIR = 2, 3, 5

    def __init__(self, c, heads, fetch, dmas, dst, groups=1, small=(None,), masks=None, select=None, gates=None,
                 block_mask=False, direct=None):
        self.direct = direct
        self.c, self.heads, self.fetch, self.dst, self.groups = c, heads, fetch, dst, groups
        self.small = small
        self.passes = len(small)
        self.masks, self.select, self.gates, self.block_mask = masks, select, gates, block_mask
        self.dmas = dmas
        self.body = self.BODY_HEADS * self.passes
        self.bodies = heads // self.BODY_HEADS
        self.rows = self.body * TT
        self.banks = 2 if groups == 1 else 3
        self.deep = 4 if self.bodies > 1 else 3
        self.bias = c.take(2 * groups, SEQ)
        if direct is None:
            self.q, self.k = c.take(2 * groups, SEQ), c.take(2 * groups, SEQ)
            self.v = c.take(2 * groups, TT * HEAD_DIM)
            self.s = c.take(self.deep * groups, SEQ)
            self.pt = c.take(2 * groups, SEQ)
            self.pair = c.take(2, TT, P)
        else:
            n = self.deep * groups
            self.s, self.pt = c.h_words[:, :n], c.h_words[:, n:n + 2 * groups]
            self.pair = c.tmp.rearrange("p a (t n) -> p a t n", t=TT)
        self.peak, self.shift = c.take(4, 4), c.take(4, 4)
        self.sums, self.scale = c.take(TT, 4), c.take(3, 4)
        self.both = c.take(2, SEQ) if select is not None else None
        n, r = self.bodies * self.rows, c.count
        rounds = self.bodies * self.body
        self.fetched = [r(f"fetched_{b}", 16 * self.transfers(b, rounds, 0)) for b in range(2)]
        self.fetched_v = [r(f"fetched_v_{b}", 16 * self.transfers(b, rounds, 1)) for b in range(2)]
        self.scores_ready, self.scores_read = r("scores_ready", n * groups), r("scores_read", n * groups + 2 * TT * groups)
        self.max_ready, self.probs_ready = r("max_ready", n), r("probs_ready", n * groups)
        self.turned, self.turned_read = r("turned", (n + self.deep) * groups), r("turned_read", n * groups + 2)
        self.attended, self.row_done = r("attended", n + 2), r("row_done", n + 2 * TT)
        self.pair_turned, self.pair_hi = r("pair_turned", heads // 2 + 2), r("pair_hi", heads // 2)
        self.pair_lo = r("pair_lo", heads // 2 + 1)

    def transfers(self, parity, rounds, which):
        return sum(self.dmas[r % self.passes][which] * self.groups for r in range(rounds) if r % 2 == parity)

    def fetched_value(self, i, r, which=0):
        count = (self.fetched, self.fetched_v)[which][r % 2]
        return count(i * (16 * self.transfers(r % 2, self.body, which)) + 16 * self.transfers(r % 2, r + 1, which))

    def width(self, row):
        return self.small[row // TT % self.passes] or P * (row % TT + 1)

    def blocks(self, row):
        w = self.width(row)
        return [(a, min(P, w - a)) for a in range(0, w, P)]

    def ends_pair(self, row):
        return 0 <= row < self.rows and (row + 1) % (2 * self.passes * TT) == 0

    def buffer(self, row, g):
        return row // TT % 2 * self.groups + g

    def operands(self, row, g):
        if self.direct is not None:
            return self.direct(row // TT, g)
        b = self.buffer(row, g)
        return (self.q[:HEAD_DIM, b], self.k[:HEAD_DIM, b],
                lambda j: self.v[:, b, j * HEAD_DIM:(j + 1) * HEAD_DIM])

    def sync(self, sp):
        for i, _ in repeat(sp, self.bodies, 1):
            for r in range(self.body):
                moves = [self.fetch(self, r % 2 * self.groups + g, i, r // self.passes, r % self.passes, g)
                         for g in range(self.groups)]
                sp.wait_ge(*self.scores_read((i * self.rows + (r + 1) * TT) * self.groups))
                for first, _ in moves:
                    assert len(first) == self.dmas[r % self.passes][0]
                    for to, of in first:
                        sp.dma_start(to, of).then_inc(self.fetched[r % 2].sem, 16)
                if not moves[0][1]:
                    continue
                sp.wait_ge(*self.row_done(i * self.rows + (r + 1) * TT))
                for _, then in moves:
                    assert len(then) == self.dmas[r % self.passes][1]
                    for to, of in then:
                        sp.dma_start(to, of).then_inc(self.fetched_v[r % 2].sem, 16)

    def tensor(self, pe):
        c, G = self.c, self.groups
        for count, n in ((self.scores_read, 2 * TT * G), (self.turned, self.deep * G), (self.turned_read, 2),
                         (self.attended, 2), (self.row_done, 2 * TT), (self.pair_turned, 2), (self.pair_lo, 1)):
            pe.sem_inc(count.sem, n)
        for i, _ in repeat(pe, self.bodies, 1):
            for s in range(self.rows + self.PAIR + 1):
                if s < self.rows:
                    row, w = s, self.width(s)
                    if row % TT == 0:
                        pe.wait_ge(*self.fetched_value(i, row // TT))
                    for g in range(G):
                        cell = i * (self.rows * G) + row * G + g
                        q, k, _ = self.operands(row, g)
                        pe.wait_ge(*self.scores_read(cell + 1 - self.banks + 2 * TT * G))
                        queries = slice(row % TT * P, (row % TT + 1) * P)
                        pe.matmul(c.psum[:, (row * G + g) % self.banks, :w], q[:, queries], k[:, :w],
                                  start=True, stop=True).then_inc(self.scores_ready.sem, 1)
                if 0 <= s - self.TURN < self.rows:
                    row = s - self.TURN
                    for g in range(G):
                        cell = i * (self.rows * G) + row * G + g
                        pe.wait_ge(*self.probs_ready(cell + 1))
                        pe.wait_ge(*self.turned_read(cell + 1))
                        for a, n in self.blocks(row):
                            mm = pe.transpose(c.psum[:n, self.banks + (row * G + g) % 2, a:a + P],
                                              self.s[:, row % self.deep * G + g, a:a + n], c.ident[:])
                        mm.then_inc(self.turned.sem, 1)
                if 0 <= s - self.VALUES < self.rows:
                    row = s - self.VALUES
                    out = c.psum[:, self.banks + 2 + row % 2, :HEAD_DIM]
                    pe.wait_ge(*self.row_done(i * self.rows + row + 2 * TT - 1))
                    if self.direct is None and row % TT == 0:
                        pe.wait_ge(*self.fetched_value(i, row // TT, 1))
                    for g in range(G):
                        cell = i * (self.rows * G) + row * G + g
                        _, _, v = self.operands(row, g)
                        pe.wait_ge(*self.turned_read(cell + 3))
                        for j, (a, n) in enumerate(self.blocks(row)):
                            mm = pe.matmul(out, self.pt[:n, row % 2 * G + g, a:a + P],
                                           v(j)[:n],
                                           start=(g == 0 and j == 0), stop=(g == G - 1 and a + n == self.width(row)))
                    mm.then_inc(self.attended.sem, 1)
                if self.ends_pair(s - self.PAIR):
                    row = s - self.PAIR
                    pair = row // (2 * self.passes * TT)
                    pe.wait_ge(*self.row_done(i * self.rows + row + 1 + 2 * TT))
                    pe.wait_ge(*self.pair_lo(i * (self.BODY_HEADS // 2) + pair + 1))
                    for t in range(TT):
                        mm = pe.transpose(c.psum[:, 7, t * P:(t + 1) * P], self.pair[:, pair % 2, t], c.ident[:])
                    mm.then_inc(self.pair_turned.sem, 1)

    def vector(self, dve, chain):
        c, v, G = self.c, self.c.nc.vector, self.groups
        extra = (G > 1) + (self.select is not None) * (TT - 1) / TT + (G > 1) + 1 + (self.gates is not None)
        extra = int(self.rows * extra) + self.block_mask * self.body
        for i, _ in repeat(dve, self.bodies, 1, chain, extra):
            for s in range(self.rows + self.PAIR + 1):
                if s < self.rows:
                    row, w, t = s, self.width(s), s % TT
                    ps = row // TT % self.passes
                    if t == 0:
                        dve.wait_ge(*self.fetched_value(i, row // TT))
                        if self.block_mask:
                            chain.step(v.memset(self.bias[:CHUNK, self.buffer(row, 0), SEQ - CHUNK:], MASKED))
                    for g in range(G):
                        cell, b = i * (self.rows * G) + row * G + g, self.buffer(row, g)
                        bias = self.masks[:, t, :w] if self.small[ps] else self.bias[:, b, SEQ - w:]
                        if self.select is not None and t > 0:
                            if g == 0:
                                dve.wait_ge(*self.turned(i * (self.rows * G) + (row + 1) * G))
                            chain.step(v.tensor_tensor(self.both[:, row % 2, :w], bias, self.select[t - 1], ALU.add))
                            bias = self.both[:, row % 2, :w]
                        dve.wait_ge(*self.scores_ready(cell + 1))
                        if g == 0:
                            dve.wait_ge(*self.turned(i * (self.rows * G) + (row + 1) * G))
                        dve.sem_inc(c.passed, 1)
                        v.tensor_tensor_reduce(
                            out=self.s[:, row % self.deep * G + g, :w], in0=c.psum[:, (row * G + g) % self.banks, :w], in1=bias,
                            scale=1.0, scalar=-3e38, op0=ALU.add, op1=ALU.max,
                            accum_out=self.peak[:, t, g:g + 1]).then_inc(self.scores_read.sem, 1)
                    dve.wait_ge(*self.scores_read(i * (self.rows * G) + (row + 1) * G + 2 * TT * G))
                    peak = self.peak[:, t, 0:1]
                    if G > 1:
                        chain.step(v.tensor_reduce(self.peak[:, t, 3:4], self.peak[:, t, :G], AX.X, ALU.max))
                        peak = self.peak[:, t, 3:4]
                    v.tensor_scalar(self.shift[:, t, 0:1], peak, -1.0, None,
                                    ALU.mult).then_inc(self.max_ready.sem, 1)
                if 0 <= s - self.VALUES < self.rows:
                    row, t = s - self.VALUES, (s - self.VALUES) % TT
                    head, ps = row // TT // self.passes, row // TT % self.passes
                    dve.wait_ge(*self.attended(i * self.rows + row + 3))
                    sums = self.sums[:, t, 0:1]
                    if G > 1:
                        chain.step(v.tensor_reduce(self.sums[:, t, 3:4], self.sums[:, t, :G], AX.X, ALU.add))
                        sums = self.sums[:, t, 3:4]
                    chain.step(v.reciprocal(self.scale[:, 0, row % 2:row % 2 + 1], sums))
                    scale = self.scale[:, 0, row % 2:row % 2 + 1]
                    if self.gates is not None:
                        gate = self.gates[:, t, bass.ds(i * self.body + head * self.passes + ps, 1)]
                        chain.step(v.tensor_tensor(self.scale[:, 1, row % 2:row % 2 + 1], scale, gate, ALU.mult))
                        scale = self.scale[:, 1, row % 2:row % 2 + 1]
                    if head % 2 == 0 and ps == 0 and t == 0:
                        dve.wait_ge(*self.pair_turned(i * (self.BODY_HEADS // 2) + head // 2 + 1))
                    to = self.pair[:, head // 2 % 2, t, head % 2 * HEAD_DIM:(head % 2 + 1) * HEAD_DIM]
                    out = c.psum[:, self.banks + 2 + row % 2, :HEAD_DIM]
                    if ps == 0:
                        ins = v.tensor_scalar(to, out, scale, None, ALU.mult)
                    else:
                        dve.wait_ge(*self.row_done(i * self.rows + row - TT + 1 + 2 * TT))
                        ins = v.scalar_tensor_tensor(to, out, scale, to, ALU.mult, ALU.add)
                    ins.then_inc(self.row_done.sem, 1)
                if self.ends_pair(s - self.PAIR):
                    pair = i * (self.BODY_HEADS // 2) + (s - self.PAIR) // (2 * self.passes * TT)
                    dve.wait_ge(*self.pair_hi(pair + 1))
                    v.tensor_tensor(at(self.dst[1], pair), c.psum[:, 7], at(self.dst[0], pair),
                                    ALU.subtract).then_inc(self.pair_lo.sem, 1)

    def scalar(self, act, chain):
        c, G = self.c, self.groups
        for i, _ in repeat(act, self.bodies, 1):
            for s in range(self.rows + self.PAIR + 1):
                if 0 <= s - self.TURN < self.rows:
                    row = s - self.TURN
                    last = self.blocks(row)[-1]
                    act.wait_ge(*self.attended(i * self.rows + row + 1))
                    for g in range(G):
                        cell = i * (self.rows * G) + row * G + g
                        act.wait_ge(*self.turned(cell + 1 + self.deep * G))
                        act.copy(self.pt[:last[1], row % 2 * G + g, :last[0] + P],
                                 c.psum[:last[1], self.banks + (row * G + g) % 2, :last[0] + P]
                                 ).then_inc(self.turned_read.sem, 1)
                if s < self.rows:
                    row, w, t = s, self.width(s), s % TT
                    act.wait_ge(*self.max_ready(i * self.rows + row + 1))
                    for g in range(G):
                        p = self.s[:, row % self.deep * G + g, :w]
                        act.activation(p, p, ACT.Exp, bias=self.shift[:, t, 0:1],
                                       accum_out=self.sums[:, t, g:g + 1]).then_inc(self.probs_ready.sem, 1)
                if self.ends_pair(s - self.PAIR):
                    pair = i * (self.BODY_HEADS // 2) + (s - self.PAIR) // (2 * self.passes * TT)
                    act.wait_ge(*self.pair_turned(pair + 3))
                    act.copy(at(self.dst[0], pair), c.psum[:, 7]).then_inc(self.pair_hi.sem, 1)


class SplitWindows(Stage):

    def __init__(self, c, tiles, hi, lo):
        self.c, self.tiles, self.hi, self.lo = c, tiles, hi, lo
        self.full = c.take(2, CMP_LEN, CMP_PAD + 2)
        self.cleared, self.copied, self.hi_done = c.count("aux_a", 1), c.count("aux_b", 6), c.count("hi_done", 1)

    def vector(self, dve, chain):
        v, c = self.c.nc.vector, self.c
        v.memset(self.full[:], 0.0).then_inc(self.cleared.sem, 1)
        dve.wait_ge(*self.cleared(1))
        for kind, tile in enumerate(self.tiles):
            by = tile.rearrange("p (n l) -> p l n", l=CMP_STRIDE)
            for j in range(2):
                v.tensor_copy(self.full[:, kind, j * CMP_STRIDE:(j + 1) * CMP_STRIDE, :CMP_N],
                              by[:, :, j:j + CMP_N]).then_inc(self.copied.sem, 1)
            pos = c.cmp_pos[:, kind].unsqueeze(2).broadcast_to([P, CMP_LEN, 2])
            v.tensor_copy(self.full[:, kind, :, CMP_PAD:], pos).then_inc(self.copied.sem, 1)
        dve.wait_ge(*self.hi_done(1))
        v.tensor_tensor(self.lo[:], self.full[:], self.hi[:], ALU.subtract)

    def scalar(self, act, chain):
        act.wait_ge(*self.copied(6))
        act.copy(self.hi[:], self.full[:]).then_inc(self.hi_done.sem, 1)


class Compress(Linear):

    def __init__(self, c, source, keys, values):
        self.keys, self.values = keys, values
        self.sum = c.take(2, CMP_PAD + 2)
        super().__init__(c, 2, source=source, slots=(SLOT_TILES,) * (CMP_LEN // SLOT_TILES), unroll=2)

    def begin(self):
        self.added, self.turned = self.c.count("aux_a", 4), self.c.count("aux_b", 1)

    def out(self, u):
        return self.c.psum[:, u % 2, :CMP_PAD + 2]

    def rhs(self, part, k):
        return part[:, self.kind, k]

    def tensor(self, pe):
        super().tensor(pe)
        pe.wait_ge(*self.added(4))
        pe.transpose(self.c.psum[:CMP_PAD, 2, :P], self.sum[:, 1, :CMP_PAD], self.c.ident[:]).then_inc(self.turned.sem, 1)

    def scalar_tile(self, act, chain, i, u):
        act.wait_ge(*self.done(i, u))
        act.copy(self.sum[:, u], self.out(u)).then_inc(self.bank_read.sem, 1)

    def scalar(self, act, chain):
        super().scalar(act, chain)
        act.wait_ge(*self.turned(1))
        act.copy(self.values[:CMP_PAD], self.c.psum[:CMP_PAD, 2, :P])

    def vector_begin(self, dve, chain):
        self.c.nc.vector.memset(self.keys, 0.0).then_inc(self.added.sem, 1)
        dve.wait_ge(*self.added(1))

    def vector_tile(self, dve, chain, i, u):
        v = self.c.nc.vector
        dve.wait_ge(*self.bank_read(u + 3))
        to = self.keys[:, :CMP_PAD] if u == 0 else self.sum[:, 1, :CMP_PAD]
        v.tensor_scalar(to, self.sum[:, u, :CMP_PAD], self.sum[:, u, CMP_PAD:CMP_PAD + 1], None,
                        ALU.add).then_inc(self.added.sem, 1)
        dve.wait_ge(*self.added(u + 2))
        if u == 1:
            v.memset(self.sum[:, 0], 0.0).then_inc(self.added.sem, 1)


class TopKeys(Stage):

    def __init__(self, c, iq, ik, iw, out):
        self.c, self.iq, self.ik, self.iw, self.out = c, iq, ik, iw, out
        self.rel, self.best = c.take(2, SEQ), c.take(3, 8)
        self.score = c.take(3, SEQ)
        n = (TT - 1) * IDX_HEADS
        self.scored, self.relu_done = c.count("aux_a", n), c.count("aux_b", n + 2)
        self.added = c.count("aux_c", n + 2)

    def tensor(self, pe):
        c = self.c
        pe.sem_inc(self.relu_done.sem, 2)
        pe.sem_inc(self.added.sem, 2)
        for t in range(1, TT):
            for h in range(IDX_HEADS):
                n = (t - 1) * IDX_HEADS + h
                half = slice(h % 2 * HEAD_DIM, (h % 2 + 1) * HEAD_DIM)
                pe.wait_ge(*self.relu_done(n + 1))
                pe.matmul(c.psum[:, n % 2, :(t + 1) * P], self.iq[half, h // 2, t * P:(t + 1) * P],
                          self.ik[half, :(t + 1) * P], start=True, stop=True).then_inc(self.scored.sem, 1)

    def scalar(self, act, chain):
        c = self.c
        for n in range((TT - 1) * IDX_HEADS):
            w = (n // IDX_HEADS + 2) * P
            act.wait_ge(*self.scored(n + 1))
            act.wait_ge(*self.added(n + 1))
            act.activation(self.rel[:, n % 2, :w], c.psum[:, n % 2, :w], ACT.Relu).then_inc(self.relu_done.sem, 1)

    def vector(self, dve, chain):
        c, v = self.c, self.c.nc.vector
        for n in range((TT - 1) * IDX_HEADS):
            t, h = n // IDX_HEADS + 1, n % IDX_HEADS
            w = (t + 1) * P
            dve.wait_ge(*self.relu_done(n + 3))
            score = self.score[:, t - 1, :w]
            before = c.causal[:, SEQ - w:] if h == 0 else score
            v.scalar_tensor_tensor(score, self.rel[:, n % 2, :w], self.iw[:, t, h:h + 1], before, ALU.mult,
                                   ALU.add).then_inc(self.added.sem, 1)
            dve.wait_ge(*self.added(n + 3))
        taken = -3e38
        for _ in range(TOPK // 8):
            for t in range(1, TT):
                chain.mark(v.max(self.best[:, t - 1], self.score[:, t - 1, :(t + 1) * P]))
            chain.wait()
            for t in range(1, TT):
                score = self.score[:, t - 1, :(t + 1) * P]
                chain.mark(v.match_replace(score, self.best[:, t - 1], score, taken))
            chain.wait()
        for t in range(1, TT):
            w = (t + 1) * P
            v.tensor_scalar(self.out[:, t - 1, :w], self.score[:, t - 1, :w], taken, MASKED, ALU.not_equal, ALU.mult)


class SigmoidGates(Stage):

    def __init__(self, c, source, out):
        self.c, self.source, self.out = c, source, out
        self.done = c.count("aux_a", 1)

    def scalar(self, act, chain):
        act.activation(self.out[:], self.source, ACT.Sigmoid).then_inc(self.done.sem, 1)

    def vector(self, dve, chain):
        v = self.c.nc.vector
        dve.wait_ge(*self.done(1))
        gates = self.out[:].rearrange("p t (h k) -> p t h k", k=3)[:, :, :, 0]
        valid = self.c.row_valid[:].unsqueeze(2).broadcast_to([P, TT, 8])
        v.tensor_tensor(gates, gates, valid, ALU.mult)


class Mix(Linear):
    two_banks = False

    def __init__(self, c, branches, dst):
        self.branches, self.dst = branches, dst
        self.gate, self.part = c.take(3, SEQ), c.take(3, SEQ)
        self.tiles_of = [((0, c.h_hi, c.h_lo, 0, KT),), ((1, c.h_hi, c.h_lo, 0, KT),), ((2, c.h_hi, c.h_lo, 0, KT),),
                         ((3, *branches[0], 0, 4), (4, *branches[1], 4, 4)), ((5, *branches[2], 0, 2),)]
        super().__init__(c, KT, slots=(8, 8, 8, 8, 2))

    def begin(self):
        c = self.c
        self.did_act = Steps(c, "aux_a", ("g0", "g1", "g2", "hi"), KT, before=1)
        self.did_dve = Steps(c, "aux_b", ("a", "b", "ab", "c", "abc", "lo"), KT, before=1)

    def tensor(self, pe):
        c = self.c
        self.did_act.begin(pe)
        self.did_dve.begin(pe)
        for i, u in repeat(pe, self.tiles, self.unroll):
            t = i * self.unroll + u
            for j, parts in enumerate(self.tiles_of):
                k0 = self.slot0 + u * self.per + j
                s = k0 % RING
                pe.wait_ge(*(self.did_act(t - 1, f"g{j}") if j < 3 else self.did_dve(t - 1, "b" if j == 3 else "c")))
                pe.wait_ge(c.lo_ready, i * (self.unroll * self.per) + k0 + 1)
                for bank, hi, lo, first, n in parts:
                    for k in range(n):
                        pairs = ((c.w_hi, hi), (c.w_hi, lo), (c.w_lo, hi))
                        for m, (w, x) in enumerate(pairs):
                            mm = pe.matmul(c.psum[:, bank], w[:, s, first + k], x[:, k],
                                           start=(k == 0 and m == 0), stop=(k == n - 1 and m == 2))
                mm.then_inc(c.slot_used, 1)

    def slot_done(self, i, u, j):
        return self.c.slot_used, (i * self.unroll + u) * self.per + j + 1 + self.slot0 + RING

    def scalar(self, act, chain):
        c, did = self.c, self.did_act
        for i, u in repeat(act, self.tiles, self.unroll):
            t = i * self.unroll + u
            for j in range(self.per):
                c.split_hi(act, i, self.unroll * self.per, self.slot0 + u * self.per + j + AHEAD)
                if j < 3:
                    act.wait_ge(*self.slot_done(i, u, j))
                    act.wait_ge(*self.did_dve(t - 1, ("a", "b", "c")[j]))
                    did.mark(act.activation(self.gate[:, j], c.psum[:, j], ACT.Sigmoid), f"g{j}")
            act.wait_ge(*self.did_dve(t, "abc"))
            did.mark(act.copy(at(self.dst[0], t), self.part[:, 0]), "hi")

    def vector(self, dve, chain):
        c, v, did = self.c, self.c.nc.vector, self.did_dve
        for i, u in repeat(dve, self.tiles, self.unroll):
            t = i * self.unroll + u
            gate, part = self.gate, self.part
            for j in range(self.per):
                c.split_lo(dve, i, self.unroll * self.per, self.slot0 + u * self.per + j + AHEAD)
                if j == 3:
                    dve.wait_ge(*self.slot_done(i, u, 3))
                    dve.wait_ge(*self.did_act(t, "g1"))
                    did_lo = did(t - 1, "lo")
                    dve.wait_ge(*did_lo)
                    did.mark(v.tensor_tensor(part[:, 0], gate[:, 0], c.psum[:, 3], ALU.mult), "a")
                    did.mark(v.tensor_tensor(part[:, 1], gate[:, 1], c.psum[:, 4], ALU.mult), "b")
                    dve.wait_ge(*did(t, "b"))
                    did.mark(v.tensor_tensor(part[:, 0], part[:, 0], part[:, 1], ALU.add), "ab")
            dve.wait_ge(*self.slot_done(i, u, 4))
            dve.wait_ge(*self.did_act(t, "g2"))
            did.mark(v.tensor_tensor(part[:, 2], gate[:, 2], c.psum[:, 5], ALU.mult), "c")
            dve.wait_ge(*did(t, "c"))
            did.mark(v.tensor_tensor(part[:, 0], part[:, 0], part[:, 2], ALU.add), "abc")
            dve.wait_ge(*self.did_act(t, "hi"))
            did.mark(v.tensor_tensor(at(self.dst[1], t), part[:, 0], at(self.dst[0], t), ALU.subtract), "lo")


class SwiGlu(Linear):
    two_banks = False

    def __init__(self, c, tiles, dst):
        self.dst = dst
        super().__init__(c, tiles, slots=(SLOT_TILES, SLOT_TILES), unroll=2)

    def begin(self):
        c = self.c
        self.did_act = Steps(c, "aux_a", ("silu", "hi"), self.tiles, before=2)
        self.did_dve = Steps(c, "aux_b", ("value", "lo"), self.tiles, before=2)

    def tensor(self, pe):
        c = self.c
        self.did_act.begin(pe)
        self.did_dve.begin(pe)
        for i, u in repeat(pe, self.tiles, self.unroll):
            t = i * self.unroll + u
            for j in range(2):
                k0 = self.slot0 + u * self.per + j
                s = k0 % RING
                pe.wait_ge(*(self.did_act(t - 2, "silu") if j == 0 else self.did_dve(t - 2, "value")))
                pe.wait_ge(c.lo_ready, i * (self.unroll * self.per) + k0 + 1)
                for k in range(KT):
                    pairs = ((c.w_hi, c.h_hi), (c.w_hi, c.h_lo), (c.w_lo, c.h_hi))
                    for n, (w, x) in enumerate(pairs):
                        mm = pe.matmul(c.psum[:, u % 2 * 2 + j], w[:, s, k], x[:, k], start=(k == 0 and n == 0),
                                       stop=(k == KT - 1 and n == 2))
                mm.then_inc(c.slot_used, 1)

    def scalar_tile(self, act, chain, i, u):
        c, t = self.c, i * self.unroll + u
        act.wait_ge(c.slot_used, t * self.per + 1 + self.slot0 + RING)
        act.wait_ge(*self.did_dve(t - 2, "value"))
        self.did_act.mark(act.activation(c.tmp[:, u % 2], c.psum[:, u % 2 * 2], ACT.Silu), "silu")
        act.wait_ge(*self.did_dve(t, "value"))
        self.did_act.mark(act.copy(at(self.dst[0], t), c.sq[:, u % 2]), "hi")

    def vector_tile(self, dve, chain, i, u):
        c, t, v = self.c, i * self.unroll + u, self.c.nc.vector
        dve.wait_ge(*self.done(i, u))
        dve.wait_ge(*self.did_act(t, "silu"))
        dve.wait_ge(*self.did_dve(t - 2, "lo"))
        self.did_dve.mark(v.tensor_tensor(c.sq[:, u % 2], c.tmp[:, u % 2], c.psum[:, u % 2 * 2 + 1], ALU.mult), "value")
        dve.wait_ge(*self.did_act(t, "hi"))
        self.did_dve.mark(v.tensor_tensor(at(self.dst[1], t), c.sq[:, u % 2], at(self.dst[0], t), ALU.subtract), "lo")


def build_stages(c, upto=None):
    io = c.io

    def fresh():
        c.used = 0

    def mlp(index):
        c.used = 0
        hidden = c.take_parts(FF_HALF, SEQ)
        st = [Norm(c, index)]
        for _ in range(2):
            st.append(ReluSquare(c, FF_HALF, hidden))
            st.append(Residual(c, source=hidden, slots=(SLOT_TILES,) * (FF_HALF // SLOT_TILES)))
        return st

    st = [Load(c), Norm(c, 0)]
    q, k, v = c.take(KT, SEQ), c.take(KT, SEQ), c.take(TT, D)
    st += [Project(c, KT, q, scale=HEAD_DIM ** -0.5), Project(c, KT, k), ProjectTokens(c, KT, v)]

    def fetch(a, b, i, head, ps, g):
        half, pair = head % 2 * HEAD_DIM, head // 2
        tile = bass.ds(i * 2 + pair, 1)
        return ([(a.q[:HEAD_DIM, b], q[half:half + HEAD_DIM, tile].rearrange("p o n -> p (o n)")),
                 (a.k[:HEAD_DIM, b], k[half:half + HEAD_DIM, tile].rearrange("p o n -> p (o n)")),
                 (a.bias[:, b], io["rel"][bass.ds(i * 4 + head, 1)].rearrange("o p n -> p (o n)"))],
                [(a.v[:, b].rearrange("p (t n) -> p t n", t=TT),
                  v[:, :, bass.ds(i * (4 * HEAD_DIM) + head * HEAD_DIM, HEAD_DIM)])])

    st += [Attention(c, ATTN_HEADS, fetch, ((3, 1),), (c.h_hi, c.h_lo), block_mask=True)]
    st += [Residual(c)] + mlp(1)
    c.used = 0
    qkv, z, ab = c.take(3 * KT, SEQ), c.take(KT, SEQ), c.take(TT, 2 * DN_HEADS)
    mark = c.used
    st += [Norm(c, 2), ConvProject(c, 3 * KT, qkv), Project(c, KT, z, func=ACT.Silu),
           ProjectTokens(c, 1, ab, cols=2 * DN_HEADS)]
    c.used = mark
    for part, scale in ((0, DN_HEAD_DIM ** -0.5), (1, 1.0)):
        st += [HeadNorm(c, [qkv[:, part * KT + k] for k in range(KT)], scale=scale)]
        c.used = mark
    gates = DnGates(c, ab)
    chunks = DeltaChunks(c, qkv, gates)
    st += [gates, chunks, DeltaScan(c, qkv, chunks)]
    c.used = mark
    st += [HeadNorm(c, [qkv[:, k] for k in range(KT)], n=DN_HEAD_DIM, gains=[c.dn_small[:, 2, :1]] * KT),
           Gate(c, qkv, z), Residual(c)] + mlp(3)
    st += [Norm(c, 4, keep=True)]

    c.used = 0
    out_a, out_b = c.take_parts(4, SEQ), c.take_parts(4, SEQ)
    mark = c.used
    scale = HEAD_DIM ** -0.5
    gain = [c.gains[:, k:k + 1] for k in range(6)]

    a_tiles, a_tokens, select = c.take(8, SEQ), c.take(TT, P), c.take(3, SEQ)
    inner = c.used
    st += [Norm(c, 5), Project(c, 8, a_tiles), ProjectTokens(c, 1, a_tokens)]
    st += [HeadNorm(c, [a_tiles[:, k] for k in range(4)], per=2, n=HEAD_DIM, scale=scale, gains=[gain[0]] * 4)]
    c.used = inner
    st += [HeadNorm(c, [a_tiles[:, 4]], per=2, n=HEAD_DIM, gains=[gain[1]])]
    c.used = inner
    st += [TopKeys(c, a_tiles[:, 5:7], a_tiles[:, 7], a_tokens[:, :, HEAD_DIM:HEAD_DIM + IDX_HEADS], select)]
    c.used = inner

    def fetch_a(a, b, i, head, ps, g):
        half = head % 2 * HEAD_DIM
        q = a_tiles[half:half + HEAD_DIM, bass.ds(i * 2 + head // 2, 1)].rearrange("p o n -> p (o n)")
        return ([(a.q[:HEAD_DIM, b], q), (a.k[:HEAD_DIM, b], a_tiles[:HEAD_DIM, 4]),
                 (a.bias[:, b], io["rel_2"][bass.ds(i * 4 + head, 1)].rearrange("o p n -> p (o n)"))],
                [(a.v[:, b].rearrange("p (t n) -> p t n", t=TT), a_tokens[:, :, :HEAD_DIM])])

    widths = [select[:, t - 1, :(t + 1) * P] for t in range(1, TT)]
    st += [Attention(c, 8, fetch_a, ((3, 1),), out_a, select=widths)]

    c.used = mark
    b_tiles, b_tokens, keys_cmp = c.take(8, SEQ), c.take(TT, 3 * P), c.take(SEQ)
    values_cmp, gates_b = c.take(P), c.take(TT, 24)
    inner = c.used
    cmp_hi, cmp_lo = c.take_parts(2, CMP_LEN, CMP_PAD + 2)
    st += [Project(c, 8, b_tiles), ProjectTokens(c, 3, b_tokens),
           SplitWindows(c, [b_tiles[:, 4], b_tiles[:, 5]], cmp_hi, cmp_lo),
           Compress(c, (cmp_hi, cmp_lo), keys_cmp[:], values_cmp)]
    c.used = inner
    st += [HeadNorm(c, [b_tiles[:, k] for k in range(4)], per=2, n=HEAD_DIM, scale=scale, gains=[gain[2]] * 4)]
    c.used = inner
    st += [HeadNorm(c, [b_tiles[:, 6], b_tiles[:, 7], keys_cmp[:]], per=2, n=HEAD_DIM, gains=[gain[3]] * 3)]
    c.used = inner
    st += [SigmoidGates(c, b_tokens[:, :, :24], gates_b)]

    def fetch_b(a, b, i, head, ps, g):
        group, pair = head % 2, i * 2 + head // 2
        half = slice(group * HEAD_DIM, (group + 1) * HEAD_DIM)
        q = (a.q[:HEAD_DIM, b], b_tiles[half, bass.ds(pair, 1)].rearrange("p o n -> p (o n)"))
        if ps == 0:
            return ([q, (a.k[:HEAD_DIM, b, :CMP_PAD], keys_cmp[half, :CMP_PAD])],
                    [(a.v[:CMP_PAD, b, :HEAD_DIM], values_cmp[:CMP_PAD, half])])
        cols = slice(ps * P + group * HEAD_DIM, ps * P + (group + 1) * HEAD_DIM)
        rel = io["rel_2"][bass.ds(pair + (8 + 4 * group), 1)].rearrange("o p n -> p (o n)")
        return ([q, (a.k[:HEAD_DIM, b], b_tiles[half, 5 + ps]), (a.bias[:, b], rel)],
                [(a.v[:, b].rearrange("p (t n) -> p t n", t=TT), b_tokens[:, :, cols])])

    st += [Attention(c, 8, fetch_b, ((2, 1), (3, 1), (3, 1)), out_b, small=(CMP_PAD, None, None), masks=c.cmp_mask, gates=gates_b)]

    c.used = mark
    out_c = c.take_parts(2, SEQ)
    inner = c.used
    c_q, c_k, c_v = c.take(6, SEQ), c.take(6, SEQ), c.take(TT, 6 * P)
    rest = c.used
    st += [Project(c, 6, c_q), Project(c, 6, c_k), ProjectTokens(c, 6, c_v)]
    st += [HeadNorm(c, [c_q[:, k] for k in range(6)], per=2, n=HEAD_DIM, scale=scale, gains=[gain[4]] * 6)]
    c.used = rest
    st += [HeadNorm(c, [c_k[:, k] for k in range(6)], per=2, n=HEAD_DIM, gains=[gain[5]] * 6)]
    c.used = rest

    def direct_c(head, g):
        half, tile = slice(head % 2 * HEAD_DIM, (head % 2 + 1) * HEAD_DIM), g * 2 + head // 2
        col = (g * 4 + head) * HEAD_DIM
        return c_q[half, tile], c_k[half, tile], lambda j: c_v[:, j, col:col + HEAD_DIM]

    def fetch_c(a, b, i, head, ps, g):
        return [(a.bias[:, b], io["rel_2"][16 + g * 4 + head])], []

    st += [Attention(c, 4, fetch_c, ((1, 0),), out_c, groups=3, direct=direct_c)]

    c.used = inner
    mixed = c.take_parts(KT, SEQ)
    st += [Norm(c, 5), Mix(c, (out_a, out_b, out_c), mixed), Residual(c, source=mixed), Norm(c, 6)]
    c.used = 0
    hidden = c.take_parts(FF2, SEQ)
    st += [SwiGlu(c, FF2, hidden), Residual(c, source=hidden, slots=(SLOT_TILES, SLOT_TILES, FF2 - 2 * SLOT_TILES))]
    return st[:upto]


def program(nc, io, upto=None, dump=()):
    ctx = ExitStack()
    with ctx:
        c = Core(nc, ctx, io)
        stages = build_stages(c, upto)
        consts = io["consts"]
        loads = [(c.x[:], io["x"]), (c.norm_w[:], io["norms"]), (c.conv_w[:], io["conv"]),
                 (c.dn_small[:], io["dn_small"]), (c.ones[:], consts[:, 0]), (c.ident[:], consts[:, 1]),
                 (c.prefix[:], consts[:, 2]), (c.chunks[:], consts[:, 3]), (c.first[:], consts[:, 4:6]),
                 (c.levels[:], consts[:, 6:12]), (c.halves[:], io["halves"])]
        loads += [(c.causal[:], io["causal"]), (c.gains[:], io["gains"]), (c.cmp_pos[:], io["cmp_pos"]),
                  (c.cmp_mask[:], io["cmp_mask"]), (c.row_valid[:], io["row_valid"])]
        c.n_loads = len(loads)
        block = ctx.enter_context(nc.Block())

        def stage_end(eng, n):
            eng.drain().then_inc(c.all_done, 1)
            eng.wait_ge(c.all_done, 4 * (n + 1))

        @block.sync
        def _(sp):
            for dst, src in loads:
                sp.dma_start(dst, src).then_inc(c.loaded, 16)
            for n in range(RING):
                src = io["stream"][n].rearrange("p (k n) -> p k n", n=P)
                sp.dma_start(c.w_raw[:, n], src).then_inc(c.raw_loaded[n], 16)
            for n, stage in enumerate(stages):
                stage.sync(sp)
                stage_end(sp, n)
            loaded = RING + c.slots + AHEAD - 1
            for n in range(RING):
                sp.wait_ge(c.raw_loaded[n], -(-(loaded - n) // RING) * 16)
            if upto is None:
                sp.dma_start(io["out"], c.x[:]).then_inc(c.stored, 16)
                sp.wait_ge(c.stored, 16)
            for n, what in enumerate(dump):
                sp.dma_start(io[f"dump{n}"], what(c, stages)).then_inc(c.stored, 16)
                sp.wait_ge(c.stored, 16 * (n + 1))

        @block.tensor
        def _(pe):
            pe.wait_ge(c.loaded, 16 * c.n_loads)
            for n, stage in enumerate(stages):
                stage.tensor(pe)
                stage_end(pe, n)

        @block.vector
        def _(dve):
            chain = Chain(dve, c.chains[1])
            dve.wait_ge(c.loaded, 16 * c.n_loads)
            for n, stage in enumerate(stages):
                stage.vector(dve, chain)
                stage_end(dve, n)

        @block.scalar
        def _(act):
            chain = Chain(act, c.chains[0])
            for n, stage in enumerate(stages):
                stage.scalar(act, chain)
                stage_end(act, n)


def tiles(w, per=None):
    rows, cols = w.shape
    k, n = rows // P, -(-cols // P)
    w = np.pad(w, ((0, 0), (0, n * P - cols)))
    per = per or -(-k // SLOT_TILES)
    w = w.reshape(k, P, n, P).transpose(2, 1, 0, 3)
    w = np.pad(w, ((0, 0), (0, 0), (0, per * SLOT_TILES - k), (0, 0)))
    return w.reshape(n, P, per, SLOT_TILES * P).transpose(0, 2, 1, 3).reshape(n * per, P, SLOT_TILES * P)


def channels(v):
    return np.moveaxis(v.reshape(*v.shape[:-1], -1, P), -1, 0)


def toeplitz(rows):
    return rows[:, np.arange(SEQ)[None] + (P - 1 - np.arange(P))[:, None]]


def bucket(dist):
    n, exact = np.maximum(dist, 0), REL_BUCKETS // 2
    large = exact + (np.log(np.maximum(n, 1).astype(np.float32) / np.float32(exact))
                     / np.float32(math.log(REL_MAX_DIST / exact)) * np.float32(REL_BUCKETS - exact)).astype(np.int32)
    return np.where(n < exact, n, np.minimum(large, REL_BUCKETS - 1))


def second_stream(a):
    w = a["w_in_2"][0]
    sizes = (512, 64, 64, 256, 64, 4, 512, 768, 24, 2304, 3072)
    a_q, a_k, a_v, i_q, i_k, i_w, b_q, b_kv, b_g, c_qkv, mix = np.split(w, np.cumsum(sizes)[:-1], axis=1)
    order = [p + 4 * g for p in range(4) for g in range(2)]
    heads = lambda m, n: m.reshape(D, 8, n)[:, order].reshape(D, 8 * n)
    kc, vc, ks, vs, kw, vw = np.split(b_kv, 6, axis=1)
    pad = lambda m: np.pad(m, ((0, 0), (0, P - m.shape[1])))
    c_q, c_k, c_v = np.split(c_qkv, 3, axis=1)
    stream = []
    stream.append(tiles(np.concatenate([a_q, a_k, a_k, i_q, i_k, i_k], axis=1)))
    stream.append(tiles(pad(np.concatenate([a_v, i_w], axis=1))))
    stream.append(tiles(np.concatenate([heads(b_q, HEAD_DIM), kc, vc, ks, kw, pad(heads(b_g, 3)), vs, vw], axis=1)))
    cmp = a["nsa_cmp_w_2"][0]
    both = np.zeros((2, CMP_LEN, 2, HEAD_DIM, 2, HEAD_DIM), np.float32)
    both[:, :, 0, :, 0], both[:, :, 1, :, 1] = cmp, cmp
    for kind in both.reshape(2, CMP_LEN * P, P):
        stream.append(tiles(kind))
    stream.append(tiles(np.concatenate([c_q, c_k, c_v], axis=1)))
    rows = np.concatenate([np.r_[h * HEAD_DIM:(h + 1) * HEAD_DIM] for h in order])
    branch_ab = tiles(np.concatenate([a["w_branch_a_2"][0], a["w_branch_b_2"][0][rows]], axis=0))
    branch_c = tiles(a["w_branch_c_2"][0])
    gate = tiles(mix).reshape(3, KT, P, SLOT_TILES * P)
    mixed = np.stack([*gate, branch_ab, branch_c], axis=1)
    gate, up = (tiles(m) for m in np.split(a["w_ffn_in_2"][0], 2, axis=1))
    stream += [mixed.reshape(-1, P, SLOT_TILES * P), tiles(a["w_out_2"][0])]
    stream += [np.stack([gate, up], axis=1).reshape(-1, P, SLOT_TILES * P), tiles(a["w_ffn_out_2"][0])]
    return stream


def lay_out(a):
    rel = a["attn_rel_bias"][0][:, ::-1]
    rel = np.concatenate([np.repeat(rel[:, :1], SEQ - 1 - MAX_REL, axis=1), rel[:, :MAX_REL + P]], axis=1)
    half = D_FF // 2

    def mlp(i):
        up, down = a["mlp_w_up"][i], a["mlp_w_down"][i]
        return [tiles(up[:, :half]), tiles(down[:half]), tiles(up[:, half:]), tiles(down[half:])]

    stream = [tiles(a["attn_w_qkv"][0]), tiles(a["attn_w_o"][0]), *mlp(0),
              tiles(a["dn_w_in"][0]), tiles(a["dn_w_o"][0]), *mlp(1)]
    stream += second_stream(a)
    stream.append(np.zeros((AHEAD + RING - 1, P, SLOT_TILES * P), np.float32))
    norms = np.stack([a["attn_norm"][0], a["mlp_norm"][0], a["dn_norm"][0], a["mlp_norm"][1], a["final_norm"],
                      a["norm1_g_2"][0], a["norm2_g_2"][0], a["norm2_g_2"][0]])
    m, i = np.arange(P)[:, None], np.arange(P)[None]
    level = [(m >> n + 1 == i >> n + 1) & (m >> n & 1 == 0) & (i >> n & 1 == 1) for n in range(6)]
    consts = [m >= 0 * i, m == i, (m <= i) & (m // CHUNK == i // CHUNK), m // CHUNK == i // CHUNK,
              m + 0 * i < CHUNK, m + 0 * i >= CHUNK, *level]
    conv = a["dn_conv_w"][0]
    spread = lambda row: np.broadcast_to(row, (P, DN_HEADS))
    head_norm = np.broadcast_to(a["dn_head_norm"][0][:, None], (P, DN_HEADS))
    dist = np.arange(SEQ - 1, -P, -1)
    table = a["rel_bias_2"][bucket(dist)].T
    win = ((P, 1), (4 * P, 4), (16 * P, 16))
    seen = np.stack([dist >= 0] * 16 + [(dist >= 0) & (dist <= w) & (dist % d == 0) for w, d in win for _ in range(4)])
    rel_2 = np.where(seen, table, np.float32(MASKED))
    token = np.arange(TT)[None, :, None] * P + np.arange(P)[:, None, None]
    window = np.arange(CMP_PAD)[None, None]
    cmp_seen = (window * CMP_STRIDE + CMP_LEN - 1 <= token) & (window < CMP_N)
    twice = lambda v: np.concatenate([v, v], axis=-1)
    return {
        "rel_2": toeplitz(rel_2), "causal": toeplitz(np.where(dist >= 0, 0, MASKED).astype(np.float32)[None])[0],
        "gains": twice(a["qk_norm_g_2"][0]).T, "cmp_pos": twice(a["nsa_cmp_pos_2"][0]).transpose(2, 0, 1),
        "cmp_mask": np.where(cmp_seen, 0, MASKED).astype(np.float32),
        "row_valid": cmp_seen.any(axis=2).astype(np.float32),
        "rel": toeplitz(rel), "x": channels(a["x"][0]).transpose(0, 2, 1), "norms": channels(norms), 
        "consts": np.stack(consts, axis=1).astype(np.float32), "conv": channels(conv).transpose(0, 2, 1),
        "halves": (m // CHUNK == np.arange(2)[None]).astype(np.float32),
        "dn_small": np.stack([spread(a["dn_a_log"][0]), spread(a["dn_dt_bias"][0]), head_norm], axis=1),
        "stream": np.concatenate(stream),
    }


def kernel(**inputs):
    import concourse.bacc as bacc
    from concourse.bass_utils import run_bass_kernel_spmd

    nc = bacc.Bacc("TRN2", target_bir_lowering=False, num_devices=1)
    arrays = {f"in_{k}": np.ascontiguousarray(v) for k, v in lay_out({k: np.asarray(v) for k, v in inputs.items()}).items()}
    io = {k[3:]: nc.dram_tensor(k, v.shape, F32, kind="ExternalInput").ap() for k, v in arrays.items()}
    io["out"] = nc.dram_tensor("out", (P, KT, SEQ), F32, kind="ExternalOutput").ap()
    program(nc, io)
    out = run_bass_kernel_spmd(nc, [arrays], core_ids=[0]).results[0]["out"]
    return out.transpose(2, 1, 0).reshape(1, SEQ, D)
```
